# Optimizing a Trainium2 kernel written in Bass

```python
import jax
import jax.numpy as jnp
from jax import lax
import numpy as np

D_MODEL = 1024
BATCH = 1
SEQ = 256
DEPTH = 2

HEAD_DIM = 64
D_MIX = D_MODEL
A_WIDTH = D_MIX // 4
A_GROUPS = A_WIDTH // HEAD_DIM
CHUNK = 128
B_WIDTH = D_MIX // 2
B_HEADS = B_WIDTH // HEAD_DIM
DILATED_PATTERNS = ((128, 1), (512, 4), (2048, 16))
C_WIDTH = D_MIX - A_WIDTH - B_WIDTH
C_HEADS = C_WIDTH // HEAD_DIM
RET_CHUNK = 128
ROPE_BASE = 10000.0
IN_COLS = 2 * A_WIDTH + 3 * B_WIDTH + 4 * C_WIDTH
N_GROUPS = 4
EXPERTS_PER_GROUP = 4
N_EXPERTS = N_GROUPS * EXPERTS_PER_GROUP
TOP_K_INNER = 2
EXPERT_HIDDEN = D_MODEL // 2
EPS = 1e-6

kernel_name = 'hybrid_gmlp_dilated_retention_hmoe'

def rms_norm(x, g):
    xf = x.astype(jnp.float32)
    y = xf * lax.rsqrt(jnp.mean(xf * xf, axis=-1, keepdims=True) + EPS)
    return (y * g.astype(jnp.float32)).astype(x.dtype)

def causal_spatial_gating(z, ln_g, ln_b, w_s, b_s):
    bsz, seq, _ = z.shape
    u, v = jnp.split(z, 2, axis=-1)
    vf = v.astype(jnp.float32)
    mu = jnp.mean(vf, -1, keepdims=True)
    var = jnp.mean(jnp.square(vf - mu), -1, keepdims=True)
    vn = (vf - mu) * lax.rsqrt(var + EPS) * ln_g.astype(jnp.float32) + ln_b.astype(jnp.float32)
    vn = vn.reshape(bsz, seq // CHUNK, CHUNK, A_GROUPS, HEAD_DIM)
    causal = jnp.tril(jnp.ones((CHUNK, CHUNK), dtype=bool))
    w = jnp.where(causal, w_s.astype(jnp.float32), 0.0)
    s = jnp.einsum('gts,bcsgd->bctgd', w, vn) + b_s.astype(jnp.float32).T[:, :, None]
    return (u.astype(jnp.float32) * s.reshape(bsz, seq, A_WIDTH)).astype(z.dtype)

def dilated_branch(q, k, v, window, dilation):
    bsz, seq, nh, dh = q.shape
    back = window // dilation
    blk = back
    n_str = -(-seq // dilation)
    n_pad = -(-n_str // blk) * blk
    nb = n_pad // blk

    def to_streams(t):
        t = jnp.pad(t, ((0, 0), (0, n_str * dilation - seq), (0, 0), (0, 0)))
        t = t.reshape(bsz, n_str, dilation, nh, dh).transpose(0, 2, 1, 3, 4)
        t = jnp.pad(t, ((0, 0), (0, 0), (0, n_pad - n_str), (0, 0), (0, 0)))
        return t.reshape(bsz, dilation, nb, blk, nh, dh)

    def with_prev(t):
        prev = jnp.pad(t, ((0, 0), (0, 0), (1, 0), (0, 0), (0, 0), (0, 0)))[:, :, :-1]
        return jnp.concatenate([prev, t], axis=3)

    qs = to_streams(q)
    kb = with_prev(to_streams(k))
    vb = with_prev(to_streams(v))
    s = jnp.einsum('brnqhd,brnkhd->brnhqk', qs, kb,
                   preferred_element_type=jnp.float32) * (dh ** -0.5)
    qi = jnp.arange(blk)[:, None]
    ki = jnp.arange(2 * blk)[None, :]
    dist = blk + qi - ki
    band = (dist >= 0) & (dist <= back)
    first = (jnp.arange(nb) == 0)[:, None, None] & (ki < blk)[None]
    valid = band[None] & ~first
    s = jnp.where(valid[None, None, :, None], s, -jnp.inf)
    m = jnp.max(s, -1, keepdims=True)
    p = jnp.exp(s - m)
    l = jnp.sum(p, -1, keepdims=True)
    o = jnp.einsum('brnhqk,brnkhd->brnqhd', p / l, vb.astype(jnp.float32))
    lse = jnp.swapaxes((m + jnp.log(l))[..., 0], -1, -2)

    def from_streams(t):
        t = t.reshape((bsz, dilation, n_pad) + t.shape[4:])[:, :, :n_str]
        t = jnp.swapaxes(t, 1, 2)
        return t.reshape((bsz, n_str * dilation) + t.shape[3:])[:, :seq]

    return from_streams(o), from_streams(lse)

def dilated_attention(q, k, v):
    outs, lses = [], []
    for window, dilation in DILATED_PATTERNS:
        o, lse = dilated_branch(q, k, v, window, dilation)
        outs.append(o)
        lses.append(lse)
    wts = jax.nn.softmax(jnp.stack(lses, 0), axis=0)
    return jnp.einsum('pbsh,pbshd->bshd', wts, jnp.stack(outs, 0))

def rotary(x, pos):
    half = x.shape[-1] // 2
    inv = ROPE_BASE ** (-jnp.arange(half, dtype=jnp.float32) / half)
    ang = pos.astype(jnp.float32)[:, None] * inv[None]
    cos = jnp.cos(ang)[None, :, None, :]
    sin = jnp.sin(ang)[None, :, None, :]
    x1 = x[..., :half].astype(jnp.float32)
    x2 = x[..., half:].astype(jnp.float32)
    return jnp.concatenate([x1 * cos - x2 * sin, x1 * sin + x2 * cos], -1).astype(x.dtype)

def retention(q, k, v):
    bsz, seq, nh, dh = q.shape
    log_g = jnp.log(1.0 - 2.0 ** (-5.0 - jnp.arange(nh, dtype=jnp.float32)))
    c = RET_CHUNK
    nc = seq // c

    def chunks(t):
        return t.astype(jnp.float32).reshape(bsz, nc, c, nh, dh).transpose(1, 0, 3, 2, 4)

    qc, kc, vc = chunks(q), chunks(k * (dh ** -0.5)), chunks(v)
    idx = jnp.arange(c)
    diff = idx[:, None] - idx[None, :]
    decay_in = jnp.where(diff >= 0,
                         jnp.exp(log_g[:, None, None] * jnp.maximum(diff, 0)[None]), 0.0)
    k_decay = jnp.exp(log_g[:, None] * (c - 1 - idx)[None])[..., None]
    q_decay = jnp.exp(log_g[:, None] * (idx + 1)[None])[..., None]
    chunk_decay = jnp.exp(log_g * c)[:, None, None]

    def step(state, xs):
        qi, ki, vi = xs
        inner = jnp.einsum('bhqd,bhkd->bhqk', qi, ki) * decay_in
        o = (jnp.einsum('bhqk,bhkd->bhqd', inner, vi)
             + jnp.einsum('bhqd,bhde->bhqe', qi * q_decay, state))
        state = state * chunk_decay + jnp.einsum('bhkd,bhke->bhde', ki * k_decay, vi)
        return state, o

    state0 = jnp.zeros((bsz, nh, dh, dh), jnp.float32)
    _, o = lax.scan(step, state0, (qc, kc, vc))
    return o.transpose(1, 0, 3, 2, 4).reshape(bsz, seq, nh, dh)

def hier_moe(h, router_g, router_gb, router_e, router_eb, w_gate, w_up, w_down):
    bsz, seq, d = h.shape
    t = h.reshape(-1, d)
    n_tok = t.shape[0]
    g_logits = (t @ router_g).astype(jnp.float32) + router_gb.astype(jnp.float32)
    g_prob = jax.nn.softmax(g_logits, axis=-1)
    g_idx = jnp.argmax(g_logits, axis=-1)
    g_w = jnp.take_along_axis(g_prob, g_idx[:, None], axis=1)
    e_logits = ((t @ router_e).astype(jnp.float32) + router_eb.astype(jnp.float32)
                ).reshape(n_tok, N_GROUPS, EXPERTS_PER_GROUP)
    e_logits = jnp.take_along_axis(e_logits, g_idx[:, None, None], axis=1)[:, 0]
    top_v, top_i = lax.top_k(e_logits, TOP_K_INNER)
    top_w = jax.nn.softmax(top_v, axis=-1) * g_w
    expert_id = g_idx[:, None] * EXPERTS_PER_GROUP + top_i
    combine = jnp.sum(jax.nn.one_hot(expert_id, N_EXPERTS, dtype=jnp.float32)
                      * top_w[..., None], axis=1)
    y = jnp.zeros((n_tok, d), jnp.float32)
    for e in range(N_EXPERTS):
        he = jax.nn.silu(t @ w_gate[e]) * (t @ w_up[e])
        y = y + combine[:, e:e + 1] * (he @ w_down[e]).astype(jnp.float32)
    return y.astype(h.dtype).reshape(bsz, seq, d)

def hybrid_layer(x, norm1, w_in, a_ln_g, a_ln_b, a_ws, a_bs, ret_gn, w_out, norm2,
                 router_g, router_gb, router_e, router_eb, w_gate, w_up, w_down):
    bsz, seq, _ = x.shape
    h = rms_norm(x, norm1)
    z = h @ w_in
    sizes = [2 * A_WIDTH, B_WIDTH, B_WIDTH, B_WIDTH, C_WIDTH, C_WIDTH, C_WIDTH, C_WIDTH]
    za, bq, bk, bv, cq, ck, cv, cg = jnp.split(z, np.cumsum(sizes)[:-1].tolist(), axis=-1)

    def heads(t, n):
        return t.reshape(bsz, seq, n, HEAD_DIM)

    a_out = causal_spatial_gating(jax.nn.gelu(za), a_ln_g, a_ln_b, a_ws, a_bs)
    b_out = dilated_attention(heads(bq, B_HEADS), heads(bk, B_HEADS), heads(bv, B_HEADS))
    b_out = b_out.reshape(bsz, seq, B_WIDTH).astype(x.dtype)
    pos = jnp.arange(seq)
    ro = retention(rotary(heads(cq, C_HEADS), pos), rotary(heads(ck, C_HEADS), pos),
                   heads(cv, C_HEADS))
    mu = jnp.mean(ro, -1, keepdims=True)
    var = jnp.mean(jnp.square(ro - mu), -1, keepdims=True)
    on = ((ro - mu) * lax.rsqrt(var + EPS)).reshape(bsz, seq, C_WIDTH) * ret_gn.astype(jnp.float32)
    c_out = (jax.nn.silu(cg.astype(jnp.float32)) * on).astype(x.dtype)

    x = x + jnp.concatenate([a_out, b_out, c_out], axis=-1) @ w_out
    x = x + hier_moe(rms_norm(x, norm2), router_g, router_gb, router_e, router_eb,
                     w_gate, w_up, w_down)
    return x

def setup_inputs(seed: int = 0) -> dict:
    key = jax.random.key(seed)
    ks = jax.random.split(key, 20)
    L, D = DEPTH, D_MODEL

    def nrm(k, shape, scale):
        return scale * jax.random.normal(k, shape, jnp.float32)

    return {
        'x': nrm(ks[0], (BATCH, SEQ, D), 1.0),
        'norm1': 1.0 + nrm(ks[1], (L, D), 0.05),
        'w_in': nrm(ks[2], (L, D, IN_COLS), D ** -0.5),
        'a_ln_g': 1.0 + nrm(ks[3], (L, A_WIDTH), 0.05),
        'a_ln_b': nrm(ks[4], (L, A_WIDTH), 0.02),
        'a_ws': nrm(ks[5], (L, A_GROUPS, CHUNK, CHUNK), CHUNK ** -0.5),
        'a_bs': 1.0 + nrm(ks[6], (L, A_GROUPS, CHUNK), 0.1),
        'ret_gn': 1.0 + nrm(ks[7], (L, C_WIDTH), 0.05),
        'w_out': nrm(ks[8], (L, D_MIX, D), D_MIX ** -0.5),
        'norm2': 1.0 + nrm(ks[9], (L, D), 0.05),
        'router_g': nrm(ks[10], (L, D, N_GROUPS), D ** -0.5),
        'router_gb': nrm(ks[11], (L, N_GROUPS), 0.01),
        'router_e': nrm(ks[12], (L, D, N_EXPERTS), D ** -0.5),
        'router_eb': nrm(ks[13], (L, N_EXPERTS), 0.01),
        'w_gate': nrm(ks[14], (L, N_EXPERTS, D, EXPERT_HIDDEN), D ** -0.5),
        'w_up': nrm(ks[15], (L, N_EXPERTS, D, EXPERT_HIDDEN), D ** -0.5),
        'w_down': nrm(ks[16], (L, N_EXPERTS, EXPERT_HIDDEN, D), EXPERT_HIDDEN ** -0.5),
        'final_norm': 1.0 + nrm(ks[17], (D,), 0.05),
    }

def reference(x, norm1, w_in, a_ln_g, a_ln_b, a_ws, a_bs, ret_gn, w_out, norm2,
              router_g, router_gb, router_e, router_eb, w_gate, w_up, w_down, final_norm):
    for l in range(DEPTH):
        x = hybrid_layer(x, norm1[l], w_in[l], a_ln_g[l], a_ln_b[l], a_ws[l], a_bs[l],
                         ret_gn[l], w_out[l], norm2[l], router_g[l], router_gb[l],
                         router_e[l], router_eb[l], w_gate[l], w_up[l], w_down[l])
    return rms_norm(x, final_norm)


_drawn_inputs = setup_inputs


def setup_inputs(seed=0):
    import zlib

    import numpy as np

    out = dict(_drawn_inputs(seed))
    spreads = {}
    factors = {'a_ln_b': 4.402, 'router_gb': 2.902}
    for name, (base, spread) in spreads.items():
        noise = np.random.default_rng([zlib.crc32(name.encode()), seed]).standard_normal(out[name].shape)
        drawn = base * np.exp(spread * noise) if base else spread * noise
        out[name] = jnp.asarray(drawn.astype(out[name].dtype))
    for name, factor in factors.items():
        out[name] = (out[name] * factor).astype(out[name].dtype)
    return out
```

```python
import numpy as np
import concourse.bass as bass
from concourse import mybir
from contextlib import ExitStack

F32 = mybir.dt.float32
I32 = mybir.dt.int32
ALU = mybir.AluOpType
ACT = mybir.ActivationFunctionType
AX = mybir.AxisListType

P = 128
D = 1024
SEQ = 256
DEPTH = 2
T = SEQ // P
DC = D // P
HD = 64
COLS = 512
HID = D // 2
HC = HID // P
A_W, B_W, C_W = D // 4, D // 2, D // 4
GROUPS, PER_GROUP = 4, 4
EXPERTS = GROUPS * PER_GROUP
PAIRS = EXPERTS // 2
SLOTS = P // 2
ROUTE = GROUPS + EXPERTS
EPS = 1e-6
NEG = -1e30

CONST_PARTS = [("ident", P), ("logc", 3 * P), ("decay", 4 * 2 * P), ("cos", SEQ), ("sin", SEQ), ("swap", P),
               ("before", P), ("ones", P), ("slot", SLOTS), ("prio", EXPERTS), ("causal", P)]
CONST_AT, _n = {}, 0
for _name, _w in CONST_PARTS:
    CONST_AT[_name] = (_n, _n + _w)
    _n += _w
CONST_COLS = _n


def constant_table():
    c = np.zeros((P, CONST_COLS), np.float32)

    def put(name, v):
        a, b = CONST_AT[name]
        c[:, a:b] = v.reshape(P, b - a)

    i = np.arange(P)
    put("ident", np.eye(P))
    def logc(t, s):
        d = t[:, None] - s[None, :]
        n = ((d >= 0) & (d <= 128)) * 1.0 + ((d >= 0) & (d % 4 == 0)) + ((d >= 0) & (d % 16 == 0))
        return np.where(n > 0, np.log(np.maximum(n, 1)), NEG)
    put("logc", np.concatenate([logc(i, i), logc(i + P, np.arange(SEQ))], 1))
    g = 1.0 - 2.0 ** (-5.0 - np.arange(4))
    dist = np.concatenate([i[None, :] - i[:, None], P + i[None, :] - i[:, None]], 1)
    put("decay", np.where(dist[:, None, :] >= 0, g[None, :, None] ** np.maximum(dist, 0)[:, None, :], 0) * HD ** -0.5)
    half = HD // 2
    inv = np.float32(10000.0) ** (-np.arange(half, dtype=np.float32) / np.float32(half))
    ang = (np.arange(SEQ, dtype=np.float32)[None, :] * inv.astype(np.float32)[i % half, None]).astype(np.float32)
    put("cos", np.cos(ang.astype(np.float64)))
    put("sin", np.sin(ang.astype(np.float64)))
    sw = np.zeros((P, P))
    for m in range(P):
        if m % HD < half:
            sw[m + half, m] = -1.0
        else:
            sw[m - half, m] = 1.0
    put("swap", sw)
    put("before", (i[:, None] < i[None, :]) * 1.0)
    put("ones", np.ones((P, P)))
    put("slot", np.tile(np.arange(SLOTS), (P, 1)))
    put("prio", np.tile(EXPERTS - np.arange(EXPERTS), (P, 1)))
    put("causal", (i[:, None] <= i[None, :]) * 1.0)
    return c


class Signal:

    def __init__(self, sem, turn, start=0):
        self.sem, self.turn, self.start = sem, turn, start

    def at(self, i, k):
        return i * self.turn + (k + self.start)


def hybrid_trunk(nc, x_in, norm1, w_in, a_ln_g, a_ln_b, a_ws, a_bs, ret_gn, w_out, norm2, router_g, router_gb,
                 router_e, router_eb, w_gate, w_up, w_down, final_norm, table, out):
    ctx = ExitStack()
    with ctx:
        ctx.enter_context(nc.allow_non_contiguous_dma("small parameters"))

        def sb(name, shape, dt=F32):
            return ctx.enter_context(nc.sbuf_tensor(name, shape, dt))

        def signal(name, turn, start=0):
            return Signal(ctx.enter_context(nc.semaphore(name)), turn, start)

        def settle(eng):
            eng.sem_inc(settled.sem)

        gate_w = sb("gate_w", [P, 2, DC, HID])
        up_w = sb("up_w", [P, 2, DC, HID])
        down_w = sb("down_w", [P, 2, HC, D])
        piece = [down_w[:, s].rearrange("p c n -> p (c n)").rearrange("p (c n) -> p c n", c=DC) for s in range(2)]
        x = sb("x", [P, T, D])
        h = sb("h", [P, T, D])
        hT = sb("hT", [P, DC, SEQ])
        const = sb("const", [P, CONST_COLS])
        za = sb("za", [P, T, 2 * A_W])
        qkb = sb("qkb", [P, 8, SEQ])
        vb = sb("vb", [P, T, B_W])
        qkc = sb("qkc", [P, 4, SEQ])
        rot = sb("rot", [P, 4, SEQ])
        vgc = sb("vgc", [P, T, 2 * C_W])
        scores = sb("scores", [P, 4, 3 * P])
        probsT = sb("probsT", [P, 2, 3, 4, P])
        work0 = sb("work0", [P, D])
        work1 = sb("work1", [P, D])
        work2 = sb("work2", [P, C_W * T])
        sgate = sb("sgate", [P, T, C_W])
        ws = sb("ws", [P, 4, P])
        wsT = sb("wsT", [P, 4, P])
        ln_g = sb("ln_g", [P, A_W])
        ln_b = sb("ln_b", [P, A_W])
        gn_g = sb("gn_g", [P, C_W])
        bs = sb("bs", [P, 4])
        gain1 = sb("gain1", [P, DC])
        gain2 = sb("gain2", [P, DC])
        rw = sb("rw", [P, DC, ROUTE])
        rb = sb("rb", [P, ROUTE])
        sumsq = sb("sumsq", [P, T])
        meansq = sb("meansq", [P, 8])
        guess = sb("guess", [P, 8])
        rstd = sb("rstd", [P, 8])
        newton = sb("newton", [P, 8])
        loge = sb("loge", [P, 8])
        stats = sb("stats", [P, T, 6])
        moments = sb("moments", [P, T, 2])
        nmax = sb("nmax", [P, 2, 8])
        denom = sb("denom", [P, 2, 8])
        rdenom = sb("rdenom", [P, 2, 8])
        gsum = sb("gsum", [P, 8])
        r = {n: sb("r_" + n, [P, T, w]) for n, w in
             [("logit", ROUTE), ("gmax", 1), ("gsh", 4), ("gexp", 4), ("gsum", 1), ("gw", 1), ("geq", 4), ("gp", 1),
              ("goh", 4), ("gpen", 4), ("sel", EXPERTS), ("m1", 1), ("eq1", EXPERTS), ("p1", 1), ("oh1", EXPERTS),
              ("sel2", EXPERTS), ("m2", 1), ("eq2", EXPERTS), ("p2", 1), ("oh2", EXPERTS), ("d", 1), ("e", 1),
              ("e1", 1), ("w1", 1), ("w2", 1), ("t1", EXPERTS), ("assign", EXPERTS), ("cw", EXPERTS),
              ("rank", EXPERTS)]}
        fullest = sb("fullest", [P, 1])
        more = sb("more", [P, 3])
        more_sum = sb("more_sum", [P, 1])
        last_f = sb("last_f", [P, 1])
        items = sb("items", [P, 2], I32)
        xT = sb("xT", [P, DC, P])
        pick = sb("pick", [P, T, 2, SLOTS])
        pickw = sb("pickw", [P, T, 2, SLOTS])
        pickT = sb("pickT", [P, T, P])
        he, sig = work0[:, 0:HID], work0[:, HID:2 * HID]
        heT = scores.rearrange("p j s -> p (j s)")[:, 0:HID].rearrange("p (c s) -> p c s", c=HC)
        y = work1

        psum = ctx.enter_context(nc.psum_tensor("psum", [P, 8, 512], F32))

        def C(name):
            a, b = CONST_AT[name]
            return const[:, a:b]

        x_loaded, const_loaded = signal("x_loaded", 16), signal("const_loaded", 16)
        params_loaded = signal("params_loaded", 16 * 11)
        piece_loaded = [signal(f"piece_loaded{s}", 16 * 4) for s in range(2)]
        ws_turned, ws_masked = signal("ws_turned", 1), signal("ws_masked", 1)
        norm_ready = signal("norm_ready", 2)
        turned = signal("turned", 12)
        turn_copied_a, turn_copied_d = signal("turn_copied_a", 6), signal("turn_copied_d", 6)
        projected = signal("projected", 6)
        proj_copied_a, proj_copied_d = signal("proj_copied_a", 6), signal("proj_copied_d", 6)
        scored, masked, exped = signal("scored", 2), signal("masked", 2), signal("exped", 2)
        probs_turned = signal("probs_turned", 2)
        probs_copied_a, probs_copied_d = signal("probs_copied_a", 2), signal("probs_copied_d", 2)
        attended, attn_stored = signal("attended", 2), signal("attn_stored", 2)
        swapped, swap_read, rotated = signal("swapped", 1), signal("swap_read", 1), signal("rotated", 1)
        cos_done = signal("cos_done", 1)
        inner_ready, decayed = signal("inner_ready", 1), signal("decayed", 1)
        retained = signal("retained", 1)
        gelu_arg, gelu_exp, gelu_den, gelu_rec = [signal(n, 1) for n in ("gelu_arg", "gelu_exp", "gelu_den", "gelu_rec")]
        gelu_done, ln_scaled, vn_ready = signal("gelu_done", 1), signal("ln_scaled", 1), signal("vn_ready", 1)
        silu_exp, silu_den, silu_rec, sgate_ready = [signal(n, 1) for n in ("silu_exp", "silu_den", "silu_rec", "sgate_ready")]
        spatial_done = signal("spatial_done", 1)
        mix_ready = signal("mix_ready", 1)
        out_done = signal("out_done", 2)
        ms_ready, rstd_guess = signal("ms_ready", 4), signal("rstd_guess", 4)
        routed, route_args, route_exps = signal("routed", 1), signal("route_args", 1), signal("route_exps", 1)
        assigned, ranked, items_ready = signal("assigned", 1), signal("ranked", 1), signal("items_ready", 1)
        range_zeroed = signal("range_zeroed", 1)
        layer_done = signal("layer_done", 1)
        settled = signal("settled", 0)
        params_used = signal("params_used", 1)
        gate_loaded, up_loaded, down_loaded = signal("gate_loaded", 16), signal("up_loaded", 16), signal("down_loaded", 16)
        picked, gathered, xT_ready = signal("picked", 2), signal("gathered", 2), signal("xT_ready", 2)
        pick_turned, pickT_ready = signal("pick_turned", 1), signal("pickT_ready", 1)
        gated, upped, gate_exp = signal("gated", 1, 1), signal("upped", 1, 1), signal("gate_exp", 1)
        he_ready, he_turned, heT_ready = signal("he_ready", 1), signal("he_turned", 1), signal("heT_ready", 1)
        downed, y_ready = signal("downed", 2, 1), signal("y_ready", 2)
        scattered, x_added = signal("scattered", 4), signal("x_added", 4)
        VSTEPS, VITEM, ASTEPS, GSTEPS = 92, 6, 4, 4
        v_step, v_item = signal("v_step", VSTEPS), signal("v_item", VITEM)
        a_step, g_step = signal("a_step", ASTEPS), signal("g_step", GSTEPS)
        out_ready, out_stored = signal("out_ready", 2), signal("out_stored", 16)
        final_loaded = signal("final_loaded", 16)

        w_in_p = w_in.rearrange("l (p c) n -> l p c n", c=DC)
        w_out_p = w_out.rearrange("l (p c) n -> l p c n", c=DC)
        gate_d = w_gate.rearrange("l (q e) (p c) n -> (l q) p e (c n)", e=2, c=DC)
        up_d = w_up.rearrange("l (q e) (p c) n -> (l q) p e (c n)", e=2, c=DC)
        down_d = w_down.rearrange("l (q e) (p c) n -> (l q) p e (c n)", e=2, c=HC)
        BQ, BK, CQK, ZA, BV, CVG = range(6)
        PIECE_COL = {BQ: 2 * A_W, BK: 2 * A_W + B_W, CQK: 2 * A_W + 3 * B_W, ZA: 0, BV: 2 * A_W + 2 * B_W,
                     CVG: 2 * A_W + 3 * B_W + 2 * C_W}

        block = ctx.enter_context(nc.Block())

        @block.sync
        def _(sp):
            sp.dma_start(x[:], x_in.rearrange("b (t p) d -> p (b t) d", p=P)).then_inc(x_loaded.sem, 16)
            sp.wait_ge(range_zeroed.sem, 1)
            with sp.Fori(0, DEPTH) as l:
                first = sp.value_load(items[0:1, 1:2], min_val=0, max_val=4 * PAIRS * DEPTH)

                def load_piece(j, src):
                    s = j % 2
                    if j < 2:
                        sp.wait_ge(downed.sem, downed.at(first, 0))
                        settle(sp)
                    else:
                        sp.wait_ge(projected.sem, projected.at(l, j - 1))
                        settle(sp)
                    sp.dma_start(piece[s], src).then_inc(piece_loaded[s].sem, 16)

                for j in range(6):
                    load_piece(j, w_in_p[bass.ds(l, 1), :, :, PIECE_COL[j]:PIECE_COL[j] + COLS]
                               .rearrange("l p c n -> (l p) c n"))
                    if j == 2:
                        sp.wait_ge(gated.sem, gated.at(first, 0))
                        settle(sp)
                        sp.dma_start(gate_w.rearrange("p e c n -> p e (c n)"),
                                     gate_d[bass.ds(l * PAIRS, 1)].rearrange("q p e n -> (q p) e n")).then_inc(gate_loaded.sem, 16)
                    if j == 4:
                        sp.wait_ge(upped.sem, upped.at(first, 0))
                        settle(sp)
                        sp.dma_start(up_w.rearrange("p e c n -> p e (c n)"),
                                     up_d[bass.ds(l * PAIRS, 1)].rearrange("q p e n -> (q p) e n")).then_inc(up_loaded.sem, 16)
                for n in range(2):
                    load_piece(6 + n, w_out_p[bass.ds(l, 1), :, :, n * COLS:(n + 1) * COLS]
                               .rearrange("l p c n -> (l p) c n"))
                sp.wait_ge(out_done.sem, out_done.at(l, 2))
                settle(sp)
                sp.dma_start(down_w.rearrange("p e c n -> p e (c n)"),
                             down_d[bass.ds(l * PAIRS, 1)].rearrange("q p e n -> (q p) e n")).then_inc(down_loaded.sem, 16)
                sp.wait_ge(items_ready.sem, items_ready.at(l, 1))
                settle(sp)
                last = sp.value_load(items[0:1, 1:2], min_val=PAIRS, max_val=4 * PAIRS * DEPTH)
                with sp.Fori(first + 1, last) as g:
                    q = sp.snap((g & (PAIRS - 1)) + l * PAIRS)
                    sp.wait_ge(gated.sem, gated.at(g, 0))
                    settle(sp)
                    sp.dma_start(gate_w.rearrange("p e c n -> p e (c n)"),
                                 gate_d[bass.ds(q, 1)].rearrange("q p e n -> (q p) e n")).then_inc(gate_loaded.sem, 16)
                    sp.wait_ge(upped.sem, upped.at(g, 0))
                    settle(sp)
                    sp.dma_start(up_w.rearrange("p e c n -> p e (c n)"),
                                 up_d[bass.ds(q, 1)].rearrange("q p e n -> (q p) e n")).then_inc(up_loaded.sem, 16)
                    sp.wait_ge(downed.sem, downed.at(g, 0))
                    settle(sp)
                    sp.dma_start(down_w.rearrange("p e c n -> p e (c n)"),
                                 down_d[bass.ds(q, 1)].rearrange("q p e n -> (q p) e n")).then_inc(down_loaded.sem, 16)
            sp.wait_ge(out_ready.sem, 2)
            sp.dma_start(out.rearrange("b (t p) d -> p (b t) d", p=P), h[:]).then_inc(out_stored.sem, 16)
            sp.wait_ge(out_stored.sem, 16)

        @block.gpsimd
        def _(pool):
            pool.dma_start(const[:], table).then_inc(const_loaded.sem, 16)
            with pool.Fori(0, DEPTH) as l:
                step = [0]

                def link(ins):
                    step[0] += 1
                    ins.then_inc(g_step.sem, 1)
                    pool.wait_ge(g_step.sem, g_step.at(l, step[0]))

                pool.wait_ge(params_used.sem, params_used.at(l, 1))
                row = lambda a: a[bass.ds(l, 1), :]
                for dst, src in [
                        (gain1[:], norm1[bass.ds(l, 1)].rearrange("l (p c) -> (l p) c", c=DC)),
                        (gain2[:], norm2[bass.ds(l, 1)].rearrange("l (p c) -> (l p) c", c=DC)),
                        (ws[:], a_ws[bass.ds(l, 1)].rearrange("l g t s -> (l t) g s")),
                        (bs[:], a_bs[bass.ds(l, 1)].rearrange("l g t -> (l t) g")),
                        (ln_g[:], row(a_ln_g).to_broadcast([P, A_W])),
                        (ln_b[:], row(a_ln_b).to_broadcast([P, A_W])),
                        (gn_g[:], row(ret_gn).to_broadcast([P, C_W])),
                        (rw[:, :, 0:GROUPS], router_g[bass.ds(l, 1)].rearrange("l (p c) n -> (l p) c n", c=DC)),
                        (rw[:, :, GROUPS:ROUTE], router_e[bass.ds(l, 1)].rearrange("l (p c) n -> (l p) c n", c=DC)),
                        (rb[:, 0:GROUPS], row(router_gb).to_broadcast([P, GROUPS])),
                        (rb[:, GROUPS:ROUTE], row(router_eb).to_broadcast([P, EXPERTS]))]:
                    pool.dma_start(dst, src).then_inc(params_loaded.sem, 16)

                pool.wait_ge(const_loaded.sem, 16)
                pool.wait_ge(proj_copied_a.sem, proj_copied_a.at(l, CQK + 1))
                pool.wait_ge(proj_copied_d.sem, proj_copied_d.at(l, CQK + 1))
                pool.tensor_tensor(rot[:], qkc[:], C("cos").unsqueeze(1).to_broadcast([P, 4, SEQ]), ALU.mult).then_inc(cos_done.sem, 1)
                zf = za.rearrange("p t n -> p (t n)")
                pool.wait_ge(proj_copied_a.sem, proj_copied_a.at(l, ZA + 1))
                pool.wait_ge(proj_copied_d.sem, proj_copied_d.at(l, ZA + 1))
                link(pool.tensor_tensor(work0[:], zf, zf, ALU.mult))
                settle(pool)
                link(pool.tensor_scalar(work0[:], work0[:], 0.044715, 1.0, ALU.mult, ALU.add))
                pool.tensor_tensor(work0[:], work0[:], zf, ALU.mult).then_inc(gelu_arg.sem, 1)
                pool.wait_ge(gelu_rec.sem, gelu_rec.at(l, 1))
                pool.tensor_tensor(zf, zf, work1[:], ALU.mult).then_inc(gelu_done.sem, 1)
                pool.wait_ge(ln_scaled.sem, ln_scaled.at(l, 1))
                pool.wait_ge(params_loaded.sem, params_loaded.at(l, params_loaded.turn))
                v = za[:, :, A_W:2 * A_W]
                link(pool.tensor_tensor(v, v, ln_g[:].unsqueeze(1).to_broadcast([P, T, A_W]), ALU.mult))
                pool.tensor_tensor(v, v, ln_b[:].unsqueeze(1).to_broadcast([P, T, A_W]), ALU.add).then_inc(vn_ready.sem, 1)
                pool.wait_ge(silu_rec.sem, silu_rec.at(l, 1))
                w2 = work2.rearrange("p (t n) -> p t n", t=T)
                link(pool.tensor_tensor(sgate[:], vgc[:, :, C_W:2 * C_W], w2, ALU.mult))
                pool.tensor_tensor(sgate[:], sgate[:], gn_g[:].unsqueeze(1).to_broadcast([P, T, C_W]), ALU.mult).then_inc(sgate_ready.sem, 1)
                assert step[0] == GSTEPS, ("GSTEPS", step[0])
            pool.wait_ge(layer_done.sem, DEPTH)
            pool.dma_start(za.rearrange("p t n -> p (t n)"),
                           final_norm.rearrange("(a n) -> a n", a=1).to_broadcast([P, D])).then_inc(final_loaded.sem, 16)

        @block.scalar
        def _(act):
            def rsqrt_guess(n, m):
                act.wait_ge(ms_ready.sem, n)
                act.activation(loge[:, 0:m], meansq[:, 0:m], ACT.Ln).then_inc(a_step.sem, 1)

            with act.Fori(0, DEPTH) as l:
                step = [0]

                def link(ins):
                    step[0] += 1
                    ins.then_inc(a_step.sem, 1)
                    act.wait_ge(a_step.sem, a_step.at(l, step[0]))

                def guess_rstd(k, m):
                    act.wait_ge(ms_ready.sem, ms_ready.at(l, k))
                    link(act.activation(loge[:, 0:m], meansq[:, 0:m], ACT.Ln))
                    act.activation(guess[:, 0:m], loge[:, 0:m], ACT.Exp, scale=-0.5).then_inc(rstd_guess.sem, 1)

                def copy_turned(k, gain):
                    for b in (0, 2):
                        act.wait_ge(turned.sem, turned.at(l, 4 * k + b + 1))
                        for c in (2 * b, 2 * b + 1):
                            src = psum[:, 4 + b, (c % 2) * SEQ:(c % 2 + 1) * SEQ]
                            if gain is None:
                                ins = act.activation(hT[:, c, :], src, ACT.Copy)
                            else:
                                ins = act.activation(hT[:, c, :], src, ACT.Copy, scale=gain[:, c:c + 1])
                        ins.then_inc(turn_copied_a.sem, 1)

                def copy_piece(j, dst):
                    act.wait_ge(projected.sem, projected.at(l, j + 1))
                    act.activation(dst, psum[:, 2 * (j % 2), :], ACT.Copy).then_inc(proj_copied_a.sem, 1)

                def exps(k):
                    act.wait_ge(masked.sem, masked.at(l, k + 1))
                    for j in range(4):
                        act.activation(scores[:, j, 0:P], scores[:, j, 0:P], ACT.Exp, bias=nmax[:, k, j:j + 1],
                                       accum_out=denom[:, k, j:j + 1])
                        ins = act.activation(scores[:, j, P:3 * P], scores[:, j, P:3 * P], ACT.Exp,
                                             bias=nmax[:, k, 4 + j:5 + j], accum_out=denom[:, k, 4 + j:5 + j])
                    ins.then_inc(exped.sem, 1)

                def copy_probs(k):
                    act.wait_ge(probs_turned.sem, probs_turned.at(l, k + 1))
                    for b in (0, 2):
                        ins = act.activation(probsT[:, k, b].rearrange("p j t -> p (j t)"), psum[:, 4 + b, :], ACT.Copy)
                    ins.then_inc(probs_copied_a.sem, 1)

                guess_rstd(1, T)
                act.wait_ge(params_loaded.sem, params_loaded.at(l, params_loaded.turn))
                copy_turned(0, gain1)
                copy_piece(BQ, qkb[:, 0:2, :].rearrange("p c t -> p (c t)"))
                copy_piece(BK, qkb[:, 4:6, :].rearrange("p c t -> p (c t)"))
                exps(0)
                copy_piece(CQK, qkc[:, 0:2, :].rearrange("p c t -> p (c t)"))
                copy_probs(0)
                copy_piece(ZA, za[:, 0, :])
                act.wait_ge(gelu_arg.sem, gelu_arg.at(l, 1))
                act.activation(work1[:], work0[:], ACT.Exp, scale=-2.0 * float(np.sqrt(2.0 / np.pi))).then_inc(gelu_exp.sem, 1)
                exps(1)
                copy_piece(BV, vb[:, 0, :])
                guess_rstd(2, T)
                copy_probs(1)
                copy_piece(CVG, vgc[:, 0, :])
                act.wait_ge(proj_copied_d.sem, proj_copied_d.at(l, CVG + 1))
                act.wait_ge(proj_copied_a.sem, proj_copied_a.at(l, CVG + 1))
                act.activation(work2.rearrange("p (t n) -> p t n", t=T), vgc[:, :, C_W:2 * C_W], ACT.Exp, scale=-1.0).then_inc(silu_exp.sem, 1)
                guess_rstd(3, 8)
                copy_turned(1, None)
                guess_rstd(4, T)
                copy_turned(2, gain2)
                act.wait_ge(route_args.sem, route_args.at(l, 1))
                act.activation(r["gexp"][:], r["gsh"][:], ACT.Exp)
                act.activation(r["e"][:], r["d"][:], ACT.Exp).then_inc(route_exps.sem, 1)

                act.wait_ge(items_ready.sem, items_ready.at(l, 1))
                settle(act)
                first = act.value_load(items[0:1, 0:1], min_val=0, max_val=4 * PAIRS * DEPTH)
                last = act.value_load(items[0:1, 1:2], min_val=PAIRS, max_val=4 * PAIRS * DEPTH)
                with act.Fori(first, last) as g:
                    act.wait_ge(pick_turned.sem, pick_turned.at(g, 1))
                    act.activation(pickT.rearrange("p t n -> p (t n)"), psum[:, 6, 0:SEQ], ACT.Copy).then_inc(pickT_ready.sem, 1)
                    act.wait_ge(gated.sem, gated.at(g, 1))
                    act.activation(sig, psum[:, 0, :], ACT.Exp, scale=-1.0).then_inc(gate_exp.sem, 1)
                    act.wait_ge(he_turned.sem, he_turned.at(g, 1))
                    act.activation(heT.rearrange("p c n -> p (c n)"), psum[:, 0, :], ACT.Copy).then_inc(heT_ready.sem, 1)
                    for n in range(2):
                        act.wait_ge(downed.sem, downed.at(g, n + 1))
                        act.activation(y[:, n * COLS:(n + 1) * COLS], psum[:, 2 + n, :], ACT.Copy).then_inc(y_ready.sem, 1)
                assert step[0] == ASTEPS, ("ASTEPS", step[0])
            act.wait_ge(ms_ready.sem, 4 * DEPTH + 1)
            act.activation(loge[:, 0:T], meansq[:, 0:T], ACT.Ln).then_inc(a_step.sem, 1)
            act.wait_ge(a_step.sem, ASTEPS * DEPTH + 1)
            act.activation(guess[:, 0:T], loge[:, 0:T], ACT.Exp, scale=-0.5).then_inc(rstd_guess.sem, 1)

        @block.tensor
        def _(pe):
            pe.wait_ge(const_loaded.sem, 16)
            pe.nop().then_inc(gated.sem, 1)
            pe.nop().then_inc(upped.sem, 1)
            pe.nop().then_inc(downed.sem, 1)
            ident = C("ident")
            with pe.Fori(0, DEPTH) as l:
                def turn(k):
                    for b in range(4):
                        for c in (2 * b, 2 * b + 1):
                            for t in range(T):
                                at = (c % 2) * SEQ + t * P
                                ins = pe.transpose(psum[:, 4 + b, at:at + P], h[:, t, c::DC], ident)
                        ins.then_inc(turned.sem, 1)

                def wait_turned(k):
                    pe.wait_ge(turn_copied_a.sem, turn_copied_a.at(l, 2 * k + 2))
                    pe.wait_ge(turn_copied_d.sem, turn_copied_d.at(l, 2 * k + 2))

                def piece_arrived(j):
                    pe.wait_ge(piece_loaded[j % 2].sem, piece_loaded[j % 2].at(l, 16 * (j // 2 + 1)))

                def project(j):
                    w, bank = piece[j % 2], 2 * (j % 2)
                    piece_arrived(j)
                    if j >= 2:
                        pe.wait_ge(proj_copied_a.sem, proj_copied_a.at(l, j - 1))
                        pe.wait_ge(proj_copied_d.sem, proj_copied_d.at(l, j - 1))
                    if j in (BQ, BK, CQK):
                        for m in range(4):
                            o = psum[:, bank + m // 2, (m % 2) * SEQ:(m % 2 + 1) * SEQ]
                            for c in range(DC):
                                ins = pe.matmul(o, w[:, c, m * P:(m + 1) * P], hT[:, c, :], start=(c == 0), stop=(c == DC - 1))
                            if m == 3:
                                ins.then_inc(projected.sem, 1)
                    else:
                        for t in range(T):
                            for c in range(DC):
                                ins = pe.matmul(psum[:, bank + t, :], hT[:, c, t * P:(t + 1) * P], w[:, c, :],
                                                start=(c == 0), stop=(c == DC - 1))
                        ins.then_inc(projected.sem, 1)

                def score(k):
                    pe.wait_ge(proj_copied_a.sem, proj_copied_a.at(l, BK + 1))
                    pe.wait_ge(proj_copied_d.sem, proj_copied_d.at(l, BK + 1))
                    if k == 1:
                        pe.wait_ge(probs_copied_a.sem, probs_copied_a.at(l, 1))
                        pe.wait_ge(probs_copied_d.sem, probs_copied_d.at(l, 1))
                    rows = slice(HD * k, HD * (k + 1))
                    for j in range(4):
                        q, kk = qkb[rows, j, :], qkb[rows, 4 + j, :]
                        pe.matmul(psum[:, 4, j * P:(j + 1) * P], q[:, 0:P], kk[:, 0:P], start=True, stop=True)
                        ins = pe.matmul(psum[:, 5 + j // 2, (j % 2) * SEQ:(j % 2 + 1) * SEQ], q[:, P:SEQ], kk,
                                        start=True, stop=True)
                    ins.then_inc(scored.sem, 1)

                def turn_probs(k):
                    pe.wait_ge(exped.sem, exped.at(l, k + 1))
                    for b in range(3):
                        for j in range(4):
                            ins = pe.transpose(psum[:, 4 + b, j * P:(j + 1) * P], scores[:, j, b * P:(b + 1) * P], ident)
                    ins.then_inc(probs_turned.sem, 1)

                def attend(k, bank):
                    pe.wait_ge(probs_copied_a.sem, probs_copied_a.at(l, k + 1))
                    pe.wait_ge(probs_copied_d.sem, probs_copied_d.at(l, k + 1))
                    for j in range(4):
                        cols = slice((2 * j + k) * HD, (2 * j + k + 1) * HD)
                        pe.matmul(psum[:, bank, j * HD:(j + 1) * HD], probsT[:, k, 0, j], vb[:, 0, cols], start=True, stop=True)
                        o = psum[:, bank, (4 + j) * HD:(5 + j) * HD]
                        pe.matmul(o, probsT[:, k, 1, j], vb[:, 0, cols], start=True, stop=False)
                        ins = pe.matmul(o, probsT[:, k, 2, j], vb[:, 1, cols], start=False, stop=True)
                    ins.then_inc(attended.sem, 1)

                pe.wait_ge(params_loaded.sem, params_loaded.at(l, params_loaded.turn))
                for g in range(4):
                    ins = pe.transpose(psum[:, 0, g * P:(g + 1) * P], ws[:, g, :], ident)
                ins.then_inc(ws_turned.sem, 1)
                pe.wait_ge(norm_ready.sem, norm_ready.at(l, 1))
                turn(0)
                wait_turned(0)
                pe.wait_ge(ws_masked.sem, ws_masked.at(l, 1))
                project(BQ)
                project(BK)
                score(0)
                project(CQK)
                turn_probs(0)
                pe.wait_ge(proj_copied_a.sem, proj_copied_a.at(l, CQK + 1))
                pe.wait_ge(proj_copied_d.sem, proj_copied_d.at(l, CQK + 1))
                for n in range(2):
                    ins = pe.matmul(psum[:, n, :], C("swap"), qkc[:, 2 * n:2 * n + 2, :].rearrange("p c t -> p (c t)"),
                                    start=True, stop=True)
                ins.then_inc(swapped.sem, 1)
                project(ZA)
                score(1)
                pe.wait_ge(swap_read.sem, swap_read.at(l, 1))
                project(BV)
                turn_probs(1)
                pe.wait_ge(proj_copied_a.sem, proj_copied_a.at(l, BV + 1))
                pe.wait_ge(proj_copied_d.sem, proj_copied_d.at(l, BV + 1))
                attend(0, 7)
                pe.wait_ge(rotated.sem, rotated.at(l, 1))
                pe.wait_ge(probs_copied_a.sem, probs_copied_a.at(l, 2))
                pe.wait_ge(probs_copied_d.sem, probs_copied_d.at(l, 2))
                for j in range(4):
                    rows = slice(HD * (j % 2), HD * (j % 2 + 1))
                    q, kk = rot[rows, j // 2, :], rot[rows, 2 + j // 2, :]
                    bank = (0, 1, 4, 5)[j]
                    pe.matmul(psum[:, bank, 0:SEQ], kk[:, 0:P], q, start=True, stop=True)
                    ins = pe.matmul(psum[:, bank, SEQ:SEQ + P], kk[:, P:SEQ], q[:, P:SEQ], start=True, stop=True)
                ins.then_inc(inner_ready.sem, 1)
                project(CVG)
                attend(1, 6)
                pe.wait_ge(decayed.sem, decayed.at(l, 1))
                pe.wait_ge(vn_ready.sem, vn_ready.at(l, 1))
                for t in range(T):
                    for g in range(4):
                        ins = pe.matmul(psum[:, 0, t * A_W + g * HD:t * A_W + (g + 1) * HD], wsT[:, g, :],
                                        za[:, t, A_W + g * HD:A_W + (g + 1) * HD], start=True, stop=True)
                ins.then_inc(spatial_done.sem, 1)
                pe.wait_ge(proj_copied_a.sem, proj_copied_a.at(l, CVG + 1))
                pe.wait_ge(proj_copied_d.sem, proj_copied_d.at(l, CVG + 1))
                pe.wait_ge(attn_stored.sem, attn_stored.at(l, 1))
                for j in range(4):
                    v = slice(j * HD, (j + 1) * HD)
                    pe.matmul(psum[:, 7, j * HD:(j + 1) * HD], scores[:, j, 0:P], vgc[:, 0, v], start=True, stop=True)
                    o = psum[:, 7, (4 + j) * HD:(5 + j) * HD]
                    pe.matmul(o, scores[:, j, P:2 * P], vgc[:, 0, v], start=True, stop=False)
                    ins = pe.matmul(o, scores[:, j, 2 * P:3 * P], vgc[:, 1, v], start=False, stop=True)
                ins.then_inc(retained.sem, 1)
                pe.wait_ge(mix_ready.sem, mix_ready.at(l, 1))
                turn(1)
                wait_turned(1)
                for n in range(2):
                    piece_arrived(6 + n)
                    for t in range(T):
                        for c in range(DC):
                            ins = pe.matmul(psum[:, 2 * n + t, :], hT[:, c, t * P:(t + 1) * P], piece[n][:, c, :],
                                            start=(c == 0), stop=(c == DC - 1))
                    ins.then_inc(out_done.sem, 1)
                pe.wait_ge(norm_ready.sem, norm_ready.at(l, 2))
                turn(2)
                wait_turned(2)
                for t in range(T):
                    for c in range(DC):
                        ins = pe.matmul(psum[:, 0, t * ROUTE:(t + 1) * ROUTE], hT[:, c, t * P:(t + 1) * P], rw[:, c, :],
                                        start=(c == 0), stop=(c == DC - 1))
                ins.then_inc(routed.sem, 1)
                pe.wait_ge(assigned.sem, assigned.at(l, 1))
                asg = r["assign"]
                pe.matmul(psum[:, 1, 0:16], C("before"), asg[:, 0, :], start=True, stop=True)
                pe.matmul(psum[:, 1, 16:32], C("ones"), asg[:, 0, :], start=True, stop=False)
                pe.matmul(psum[:, 1, 16:32], C("before"), asg[:, 1, :], start=False, stop=True)
                pe.matmul(psum[:, 1, 32:48], C("ones"), asg[:, 0, :], start=True, stop=False)
                pe.matmul(psum[:, 1, 32:48], C("ones"), asg[:, 1, :], start=False, stop=True).then_inc(ranked.sem, 1)

                pe.wait_ge(items_ready.sem, items_ready.at(l, 1))
                settle(pe)
                first = pe.value_load(items[0:1, 0:1], min_val=0, max_val=4 * PAIRS * DEPTH)
                last = pe.value_load(items[0:1, 1:2], min_val=PAIRS, max_val=4 * PAIRS * DEPTH)
                with pe.Fori(first, last) as g:
                    pe.wait_ge(picked.sem, picked.at(g, 1))
                    for b in range(2):
                        for c in range(4 * b, 4 * b + 4):
                            for t in range(T):
                                ins = pe.matmul(psum[:, 4 + b, (c % 4) * P:(c % 4 + 1) * P], h[:, t, c::DC],
                                                pick[:, t].rearrange("p e s -> p (e s)"), start=(t == 0), stop=(t == T - 1))
                        ins.then_inc(gathered.sem, 1)
                    pe.wait_ge(picked.sem, picked.at(g, 2))
                    for t in range(T):
                        ins = pe.transpose(psum[:, 6, t * P:(t + 1) * P], pickw[:, t].rearrange("p e s -> p (e s)"), ident)
                    ins.then_inc(pick_turned.sem, 1)
                    pe.wait_ge(xT_ready.sem, xT_ready.at(g, 2))
                    for bank, w, loaded, done in ((0, gate_w, gate_loaded, gated), (1, up_w, up_loaded, upped)):
                        pe.wait_ge(loaded.sem, loaded.at(g, 16))
                        for c in range(DC):
                            for e in range(2):
                                ins = pe.matmul(psum[e * SLOTS:(e + 1) * SLOTS, bank, :], xT[:, c, e * SLOTS:(e + 1) * SLOTS],
                                                w[:, e, c, :], start=(c == 0), stop=(c == DC - 1))
                        ins.then_inc(done.sem, 1)
                    pe.wait_ge(he_ready.sem, he_ready.at(g, 1))
                    for c in range(HC):
                        ins = pe.transpose(psum[:, 0, c * P:(c + 1) * P], he[:, c::HC], ident)
                    ins.then_inc(he_turned.sem, 1)
                    pe.wait_ge(heT_ready.sem, heT_ready.at(g, 1))
                    pe.wait_ge(down_loaded.sem, down_loaded.at(g, 16))
                    for n in range(2):
                        for c in range(HC):
                            for e in range(2):
                                ins = pe.matmul(psum[e * SLOTS:(e + 1) * SLOTS, 2 + n, :], heT[:, c, e * SLOTS:(e + 1) * SLOTS],
                                                down_w[:, e, c, n * COLS:(n + 1) * COLS], start=(c == 0), stop=(c == HC - 1))
                        ins.then_inc(downed.sem, 1)
                    pe.wait_ge(pickT_ready.sem, pickT_ready.at(g, 1))
                    for n in range(2):
                        pe.wait_ge(y_ready.sem, y_ready.at(g, n + 1))
                        for t in range(T):
                            k = 2 * n + t
                            if k >= 2:
                                pe.wait_ge(x_added.sem, x_added.at(g, k - 1))
                            pe.matmul(psum[:, 6 + t, :], pickT[:, t, :], y[:, n * COLS:(n + 1) * COLS],
                                      start=True, stop=True).then_inc(scattered.sem, 1)

        @block.vector
        def _(dve):
            V = nc.vector
            V.memset(last_f[:], 0.0).then_inc(v_item.sem, 1)
            V.memset(items[:], 0).then_inc(range_zeroed.sem, 1)
            V.memset(more_sum[:], 0.0).then_inc(params_used.sem, 1)
            dve.wait_ge(x_loaded.sem, 16)
            dve.wait_ge(const_loaded.sem, 16)
            with dve.Fori(0, DEPTH) as l:
                step = [0]

                def link(ins):
                    step[0] += 1
                    ins.then_inc(v_step.sem, 1)
                    dve.wait_ge(v_step.sem, v_step.at(l, step[0]))

                def refine_rstd(k, m):
                    dve.wait_ge(rstd_guess.sem, rstd_guess.at(l, k))
                    link(V.scalar_tensor_tensor(newton[:, 0:m], guess[:, 0:m], -0.5, meansq[:, 0:m], ALU.mult, ALU.mult))
                    link(V.tensor_tensor(newton[:, 0:m], newton[:, 0:m], guess[:, 0:m], ALU.mult))
                    link(V.scalar_tensor_tensor(rstd[:, 0:m], newton[:, 0:m], 1.5, guess[:, 0:m], ALU.add, ALU.mult))

                def normalise(k, n):
                    for t in range(T):
                        ins = V.tensor_tensor_reduce(out=h[:, t, :], in0=x[:, t, :], in1=x[:, t, :], scale=1.0, scalar=0.0,
                                                     op0=ALU.mult, op1=ALU.add, accum_out=sumsq[:, t:t + 1])
                        link(ins)
                    V.tensor_scalar(meansq[:, 0:T], sumsq[:], 1.0 / D, EPS, ALU.mult, ALU.add).then_inc(ms_ready.sem, 1)
                    refine_rstd(k, T)
                    for t in range(T):
                        ins = V.tensor_scalar(h[:, t, :], x[:, t, :], rstd[:, t:t + 1], None, ALU.mult)
                        if t < T - 1:
                            link(ins)
                    ins.then_inc(norm_ready.sem, 1)

                def copy_turned(k, gain):
                    for b in (1, 3):
                        dve.wait_ge(turned.sem, turned.at(l, 4 * k + b + 1))
                        src = psum[:, 4 + b, :].rearrange("p (c t) -> p c t", c=2)
                        if gain is None:
                            ins = V.tensor_copy(hT[:, 2 * b:2 * b + 2, :], src)
                        else:
                            ins = V.tensor_tensor(hT[:, 2 * b:2 * b + 2, :], src,
                                                  gain[:, 2 * b:2 * b + 2].unsqueeze(2).to_broadcast([P, 2, SEQ]), ALU.mult)
                        ins.then_inc(turn_copied_d.sem, 1)

                def copy_piece(j, dst):
                    dve.wait_ge(projected.sem, projected.at(l, j + 1))
                    V.tensor_copy(dst, psum[:, 2 * (j % 2) + 1, :]).then_inc(proj_copied_d.sem, 1)

                def mask(k):
                    dve.wait_ge(scored.sem, scored.at(l, k + 1))
                    logc = C("logc")
                    if k == 1:
                        dve.wait_ge(probs_turned.sem, probs_turned.at(l, 1))
                    link(V.scalar_tensor_tensor(scores[:, :, 0:P], psum[:, 4, :].rearrange("p (j s) -> p j s", j=4), HD ** -0.5,
                                                logc[:, 0:P].unsqueeze(1).to_broadcast([P, 4, P]), ALU.mult, ALU.add))
                    for b in range(2):
                        link(V.scalar_tensor_tensor(scores[:, 2 * b:2 * b + 2, P:3 * P],
                                                    psum[:, 5 + b, :].rearrange("p (j s) -> p j s", j=2), HD ** -0.5,
                                                    logc[:, P:3 * P].unsqueeze(1).to_broadcast([P, 2, SEQ]), ALU.mult, ALU.add))
                    link(V.tensor_reduce(nmax[:, k, 0:4], scores[:, :, 0:P], AX.X, ALU.max, negate=True))
                    V.tensor_reduce(nmax[:, k, 4:8], scores[:, :, P:3 * P], AX.X, ALU.max, negate=True).then_inc(masked.sem, 1)

                def copy_probs(k):
                    dve.wait_ge(probs_turned.sem, probs_turned.at(l, k + 1))
                    V.tensor_copy(probsT[:, k, 1].rearrange("p j t -> p (j t)"), psum[:, 5, :]).then_inc(probs_copied_d.sem, 1)

                def store_attention(k, bank):
                    link(V.reciprocal(rdenom[:, k, :], denom[:, k, :]))
                    dve.wait_ge(attended.sem, attended.at(l, k + 1))
                    dst = h[:, :, A_W:A_W + B_W].rearrange("p t (j e d) -> p t j e d", e=2, d=HD)[:, :, :, k, :]
                    V.tensor_tensor(dst, psum[:, bank, :].rearrange("p (t j d) -> p t j d", t=T, j=4),
                                    rdenom[:, k, :].rearrange("p (t j) -> p t j", t=T).unsqueeze(3).to_broadcast([P, T, 4, HD]),
                                    ALU.mult).then_inc(attn_stored.sem, 1)

                normalise(1, 1)
                dve.wait_ge(ws_turned.sem, ws_turned.at(l, 1))
                V.tensor_tensor(wsT[:], psum[:, 0, :].rearrange("p (g t) -> p g t", g=4),
                                C("causal").unsqueeze(1).to_broadcast([P, 4, P]), ALU.mult).then_inc(ws_masked.sem, 1)
                dve.wait_ge(params_loaded.sem, params_loaded.at(l, params_loaded.turn))
                copy_turned(0, gain1)
                copy_piece(BQ, qkb[:, 2:4, :].rearrange("p c t -> p (c t)"))
                copy_piece(BK, qkb[:, 6:8, :].rearrange("p c t -> p (c t)"))
                mask(0)
                copy_piece(CQK, qkc[:, 2:4, :].rearrange("p c t -> p (c t)"))
                copy_probs(0)
                dve.wait_ge(swapped.sem, swapped.at(l, 1))
                V.tensor_tensor(work1.rearrange("p (c t) -> p c t", c=4), psum[:, 0:2, :].rearrange("p b (c t) -> p (b c) t", c=2),
                                C("sin").unsqueeze(1).to_broadcast([P, 4, SEQ]), ALU.mult).then_inc(swap_read.sem, 1)
                dve.wait_ge(swap_read.sem, swap_read.at(l, 1))
                dve.wait_ge(cos_done.sem, cos_done.at(l, 1))
                V.tensor_tensor(rot[:], rot[:], work1.rearrange("p (c t) -> p c t", c=4), ALU.add).then_inc(rotated.sem, 1)
                copy_piece(ZA, za[:, 1, :])
                mask(1)
                dve.wait_ge(gelu_exp.sem, gelu_exp.at(l, 1))
                link(V.tensor_scalar(work1[:], work1[:], 1.0, None, ALU.add))
                V.reciprocal(work1[:], work1[:]).then_inc(gelu_rec.sem, 1)
                copy_piece(BV, vb[:, 1, :])
                dve.wait_ge(gelu_done.sem, gelu_done.at(l, 1))
                for t in range(T):
                    link(V.bn_stats(stats[:, t, :], za[:, t, A_W:2 * A_W]))
                for t in range(T):
                    settle(dve)
                    link(V.bn_aggr(moments[:, t, :], stats[:, t, :]))
                V.tensor_scalar(meansq[:, 0:T], moments[:, :, 1], EPS, None, ALU.add).then_inc(ms_ready.sem, 1)
                copy_probs(1)
                refine_rstd(2, T)
                for t in range(T):
                    v = za[:, t, A_W:2 * A_W]
                    ins = V.tensor_scalar(v, v, moments[:, t, 0:1], rstd[:, t:t + 1], ALU.subtract, ALU.mult)
                    if t < T - 1:
                        link(ins)
                ins.then_inc(ln_scaled.sem, 1)
                store_attention(0, 7)
                dve.wait_ge(inner_ready.sem, inner_ready.at(l, 1))
                dve.wait_ge(probs_turned.sem, probs_turned.at(l, 2))
                dec = C("decay").rearrange("p (j t) -> p j t", j=4)
                for j, bank in ((0, 0), (2, 4)):
                    link(V.tensor_tensor(scores[:, j:j + 2, 0:SEQ], psum[:, bank:bank + 2, 0:SEQ], dec[:, j:j + 2, :], ALU.mult))
                    ins = V.tensor_tensor(scores[:, j:j + 2, SEQ:SEQ + P], psum[:, bank:bank + 2, SEQ:SEQ + P],
                                          dec[:, j:j + 2, 0:P], ALU.mult)
                    if j == 0:
                        link(ins)
                ins.then_inc(decayed.sem, 1)
                copy_piece(CVG, vgc[:, 1, :])
                dve.wait_ge(silu_exp.sem, silu_exp.at(l, 1))
                link(V.tensor_scalar(work2[:], work2[:], 1.0, None, ALU.add))
                V.reciprocal(work2[:], work2[:]).then_inc(silu_rec.sem, 1)
                store_attention(1, 6)
                dve.wait_ge(spatial_done.sem, spatial_done.at(l, 1))
                w0 = work0[:, 0:T * A_W].rearrange("p (t g d) -> p t g d", t=T, g=4)
                for t in range(T):
                    link(V.tensor_tensor(w0[:, t], psum[:, 0, t * A_W:(t + 1) * A_W].rearrange("p (g d) -> p g d", g=4),
                                         bs[:].unsqueeze(2).to_broadcast([P, 4, HD]), ALU.add))
                link(V.tensor_tensor(h[:, :, 0:A_W], work0[:, 0:T * A_W].rearrange("p (t n) -> p t n", t=T), za[:, :, 0:A_W], ALU.mult))
                dve.wait_ge(retained.sem, retained.at(l, 1))
                o = psum[:, 7, :].rearrange("p (k d) -> p k d", d=HD)
                cen = work1[:, 0:512].rearrange("p (k d) -> p k d", d=HD)
                sq = work1[:, 512:1024].rearrange("p (k d) -> p k d", d=HD)
                link(V.tensor_reduce(gsum[:], o, AX.X, ALU.add))
                link(V.tensor_scalar(gsum[:], gsum[:], 1.0 / HD, None, ALU.mult))
                link(V.tensor_tensor(cen, o, gsum[:].unsqueeze(2).to_broadcast([P, 8, HD]), ALU.subtract))
                link(V.tensor_tensor(sq, cen, cen, ALU.mult))
                link(V.tensor_reduce(gsum[:], sq, AX.X, ALU.add))
                V.tensor_scalar(meansq[:], gsum[:], 1.0 / HD, EPS, ALU.mult, ALU.add).then_inc(ms_ready.sem, 1)
                refine_rstd(3, 8)
                link(V.tensor_tensor(cen, cen, rstd[:].unsqueeze(2).to_broadcast([P, 8, HD]), ALU.mult))
                dve.wait_ge(sgate_ready.sem, sgate_ready.at(l, 1))
                V.tensor_tensor(h[:, :, A_W + B_W:D], work1[:, 0:512].rearrange("p (t n) -> p t n", t=T), sgate[:],
                                ALU.mult).then_inc(mix_ready.sem, 1)
                copy_turned(1, None)
                for n in range(2):
                    dve.wait_ge(out_done.sem, out_done.at(l, n + 1))
                    for t in range(T):
                        xs = x[:, t, n * COLS:(n + 1) * COLS]
                        link(V.tensor_tensor(xs, psum[:, 2 * n + t, :], xs, ALU.add))
                normalise(4, 2)
                copy_turned(2, gain2)

                dve.wait_ge(routed.sem, routed.at(l, 1))
                R = {k: t[:] for k, t in r.items()}
                link(V.tensor_tensor(R["logit"], psum[:, 0, 0:T * ROUTE].rearrange("p (t n) -> p t n", t=T),
                                     rb[:].unsqueeze(1).to_broadcast([P, T, ROUTE]), ALU.add))
                gl, el = r["logit"][:, :, 0:GROUPS], r["logit"][:, :, GROUPS:ROUTE]
                link(V.tensor_reduce(R["gmax"], gl, AX.X, ALU.max))
                link(V.tensor_tensor(R["gsh"], gl, r["gmax"][:].to_broadcast([P, T, 4]), ALU.subtract))
                link(V.tensor_tensor(R["geq"], gl, r["gmax"][:].to_broadcast([P, T, 4]), ALU.is_equal))
                prio4 = C("prio")[:, 0:4].unsqueeze(1).to_broadcast([P, T, 4])
                prio16 = C("prio").unsqueeze(1).to_broadcast([P, T, EXPERTS])
                link(V.tensor_tensor(R["geq"], R["geq"], prio4, ALU.mult))
                link(V.tensor_reduce(R["gp"], R["geq"], AX.X, ALU.max))
                link(V.tensor_tensor(R["goh"], R["geq"], r["gp"][:].to_broadcast([P, T, 4]), ALU.is_equal))
                link(V.tensor_scalar(R["gpen"], R["goh"], -NEG, NEG, ALU.mult, ALU.add))
                for t in range(T):
                    s4 = r["sel"][:, t].rearrange("p (g e) -> p g e", g=GROUPS)
                    link(V.tensor_tensor(s4, r["logit"][:, t, GROUPS:ROUTE].rearrange("p (g e) -> p g e", g=GROUPS),
                                         r["goh"][:, t].unsqueeze(2).to_broadcast([P, GROUPS, PER_GROUP]), ALU.mult))
                    link(V.tensor_tensor(s4, s4, r["gpen"][:, t].unsqueeze(2).to_broadcast([P, GROUPS, PER_GROUP]), ALU.add))
                for m, eq, pr, oh, sel in (("m1", "eq1", "p1", "oh1", "sel"), ("m2", "eq2", "p2", "oh2", "sel2")):
                    if sel == "sel2":
                        link(V.scalar_tensor_tensor(R["sel2"], R["oh1"], 3 * NEG, R["sel"], ALU.mult, ALU.add))
                    link(V.tensor_reduce(R[m], R[sel], AX.X, ALU.max))
                    link(V.tensor_tensor(R[eq], R[sel], r[m][:].to_broadcast([P, T, EXPERTS]), ALU.is_equal))
                    link(V.tensor_tensor(R[eq], R[eq], prio16, ALU.mult))
                    link(V.tensor_reduce(R[pr], R[eq], AX.X, ALU.max))
                    link(V.tensor_tensor(R[oh], R[eq], r[pr][:].to_broadcast([P, T, EXPERTS]), ALU.is_equal))
                V.tensor_tensor(R["assign"], R["oh1"], R["oh2"], ALU.add).then_inc(assigned.sem, 1)
                V.tensor_tensor(R["d"], R["m2"], R["m1"], ALU.subtract).then_inc(route_args.sem, 1)
                dve.wait_ge(route_exps.sem, route_exps.at(l, 1))
                link(V.tensor_reduce(R["gsum"], R["gexp"], AX.X, ALU.add))
                link(V.reciprocal(R["gw"], R["gsum"]))
                link(V.tensor_scalar(R["e1"], R["e"], 1.0, None, ALU.add))
                link(V.reciprocal(R["w1"], R["e1"]))
                link(V.tensor_tensor(R["w1"], R["w1"], R["gw"], ALU.mult))
                link(V.tensor_tensor(R["w2"], R["w1"], R["e"], ALU.mult))
                link(V.tensor_tensor(R["cw"], R["oh1"], r["w1"][:].to_broadcast([P, T, EXPERTS]), ALU.mult))
                link(V.tensor_tensor(R["t1"], R["oh2"], r["w2"][:].to_broadcast([P, T, EXPERTS]), ALU.mult))
                link(V.tensor_tensor(R["cw"], R["cw"], R["t1"], ALU.add))
                dve.wait_ge(ranked.sem, ranked.at(l, 1))
                link(V.scalar_tensor_tensor(R["rank"], psum[:, 1, 0:32].rearrange("p (t e) -> p t e", t=T), 1.0, R["assign"],
                                            ALU.add, ALU.mult))
                link(V.tensor_scalar(R["rank"], R["rank"], -1.0, None, ALU.add))
                link(V.tensor_reduce(fullest[:], psum[:, 1, 32:48], AX.X, ALU.max))
                for k in range(3):
                    link(V.tensor_scalar(more[:, k:k + 1], fullest[:], SLOTS * (k + 1) + 0.5, float(PAIRS), ALU.is_gt, ALU.mult))
                link(V.tensor_reduce(more_sum[:], more[:], AX.X, ALU.add))
                link(V.tensor_copy(items[:, 0:1], last_f[:]))
                link(V.scalar_tensor_tensor(last_f[:], last_f[:], float(PAIRS), more_sum[:], ALU.add, ALU.add))
                V.tensor_copy(items[:, 1:2], last_f[:]).then_inc(items_ready.sem, 1)
                assert step[0] == VSTEPS, ("VSTEPS", step[0])

                dve.wait_ge(items_ready.sem, items_ready.at(l, 1))
                settle(dve)
                first = dve.value_load(items[0:1, 0:1], min_val=0, max_val=4 * PAIRS * DEPTH)
                last = dve.value_load(items[0:1, 1:2], min_val=PAIRS, max_val=4 * PAIRS * DEPTH)
                with dve.Fori(first, last) as g:
                    istep = [0]

                    def ilink(ins):
                        istep[0] += 1
                        ins.then_inc(v_item.sem, 1)
                        dve.wait_ge(v_item.sem, v_item.at(g, istep[0] + 1))

                    p2 = dve.snap((g & (PAIRS - 1)) * 2)
                    pk = pick[:].rearrange("p t e s -> p t (e s)")
                    for t in range(T):
                        ins = V.tensor_tensor(pick[:, t], C("slot").unsqueeze(1).to_broadcast([P, 2, SLOTS]),
                                              r["rank"][:, t, bass.ds(p2, 2)].unsqueeze(2).to_broadcast([P, 2, SLOTS]), ALU.is_equal)
                        if t == 0:
                            ilink(ins)
                    ins.then_inc(picked.sem, 1)
                    dve.wait_ge(picked.sem, picked.at(g, 1))
                    for t in range(T):
                        ins = V.tensor_tensor(pickw[:, t], pick[:, t],
                                              r["cw"][:, t, bass.ds(p2, 2)].unsqueeze(2).to_broadcast([P, 2, SLOTS]), ALU.mult)
                        if t == 0:
                            ilink(ins)
                    ins.then_inc(picked.sem, 1)
                    rk = r["rank"][:, :, bass.ds(p2, 2)]
                    ilink(V.tensor_scalar(rk, rk, -float(SLOTS), None, ALU.add))
                    for b in range(2):
                        dve.wait_ge(gathered.sem, gathered.at(g, b + 1))
                        V.tensor_tensor(xT[:, 4 * b:4 * b + 4, :], psum[:, 4 + b, :].rearrange("p (c s) -> p c s", c=4),
                                        gain2[:, 4 * b:4 * b + 4].unsqueeze(2).to_broadcast([P, 4, P]), ALU.mult).then_inc(xT_ready.sem, 1)
                    dve.wait_ge(gate_exp.sem, gate_exp.at(g, 1))
                    ilink(V.tensor_scalar(sig, sig, 1.0, None, ALU.add))
                    ilink(V.reciprocal(sig, sig))
                    ilink(V.tensor_tensor(sig, sig, psum[:, 0, :], ALU.mult))
                    dve.wait_ge(upped.sem, upped.at(g, 1))
                    V.tensor_tensor(he, sig, psum[:, 1, :], ALU.mult).then_inc(he_ready.sem, 1)
                    for n in range(2):
                        for t in range(T):
                            k = 2 * n + t
                            dve.wait_ge(scattered.sem, scattered.at(g, k + 1))
                            xs = x[:, t, n * COLS:(n + 1) * COLS]
                            V.tensor_tensor(xs, psum[:, 6 + t, :], xs, ALU.add).then_inc(x_added.sem, 1)
                    dve.wait_ge(x_added.sem, x_added.at(g, 4))
                    assert istep[0] == VITEM, ("VITEM", istep[0])
                V.memset(newton[:], 0.0).then_inc(params_used.sem, 1)
                dve.wait_ge(params_used.sem, params_used.at(l, 2))
                V.memset(newton[:], 0.0).then_inc(layer_done.sem, 1)
                dve.wait_ge(layer_done.sem, layer_done.at(l, 1))

            fs = [VSTEPS * DEPTH]

            def flink(ins):
                fs[0] += 1
                ins.then_inc(v_step.sem, 1)
                dve.wait_ge(v_step.sem, fs[0])

            for t in range(T):
                flink(V.tensor_tensor_reduce(out=h[:, t, :], in0=x[:, t, :], in1=x[:, t, :], scale=1.0, scalar=0.0,
                                             op0=ALU.mult, op1=ALU.add, accum_out=sumsq[:, t:t + 1]))
            V.tensor_scalar(meansq[:, 0:T], sumsq[:], 1.0 / D, EPS, ALU.mult, ALU.add).then_inc(ms_ready.sem, 1)
            dve.wait_ge(rstd_guess.sem, 4 * DEPTH + 1)
            flink(V.scalar_tensor_tensor(newton[:, 0:T], guess[:, 0:T], -0.5, meansq[:, 0:T], ALU.mult, ALU.mult))
            flink(V.tensor_tensor(newton[:, 0:T], newton[:, 0:T], guess[:, 0:T], ALU.mult))
            flink(V.scalar_tensor_tensor(rstd[:, 0:T], newton[:, 0:T], 1.5, guess[:, 0:T], ALU.add, ALU.mult))
            dve.wait_ge(final_loaded.sem, 16)
            for t in range(T):
                V.scalar_tensor_tensor(h[:, t, :], x[:, t, :], rstd[:, t:t + 1], za.rearrange("p t n -> p (t n)"),
                                       ALU.mult, ALU.mult).then_inc(out_ready.sem, 1)


NAMES = ["x", "norm1", "w_in", "a_ln_g", "a_ln_b", "a_ws", "a_bs", "ret_gn", "w_out", "norm2", "router_g", "router_gb",
         "router_e", "router_eb", "w_gate", "w_up", "w_down", "final_norm"]


def kernel(**inputs):
    import concourse.bacc as bacc
    from concourse.bass_utils import run_bass_kernel_spmd as run

    nc = bacc.Bacc("TRN2", target_bir_lowering=False, num_devices=1)
    arrays, args = {}, []
    for name in NAMES:
        a = np.ascontiguousarray(inputs[name])
        arrays[f"in_{name}"] = a
        args.append(nc.dram_tensor(f"in_{name}", a.shape, mybir.dt.from_np(a.dtype), kind="ExternalInput").ap())
    arrays["table"] = constant_table()
    args.append(nc.dram_tensor("table", (P, CONST_COLS), F32, kind="ExternalInput").ap())
    args.append(nc.dram_tensor("out", (1, SEQ, D), F32, kind="ExternalOutput").ap())
    hybrid_trunk(nc, *args)
    return run(nc, [arrays], core_ids=[0]).results[0]["out"]
```

```python
import numpy as np
import concourse.bass as bass
from concourse import mybir
from contextlib import ExitStack

F32 = mybir.dt.float32
I32 = mybir.dt.int32
ALU = mybir.AluOpType
ACT = mybir.ActivationFunctionType
AX = mybir.AxisListType

P = 128
D = 1024
SEQ = 256
DEPTH = 2
T = SEQ // P
DC = D // P
HD = 64
COLS = 512
HID = D // 2
HC = HID // P
A_W, B_W, C_W = D // 4, D // 2, D // 4
GROUPS, PER_GROUP = 4, 4
EXPERTS = GROUPS * PER_GROUP
PAIRS = EXPERTS // 2
SLOTS = P // 2
ROUTE = GROUPS + EXPERTS
EPS = 1e-6
NEG = -1e30
ROOT_MAGIC = float(0x5f3759df)

CONST_PARTS = [("ident", P), ("ones", P), ("logc", 3 * P), ("decay", 4 * 2 * P), ("cos", SEQ), ("sin", SEQ), ("swap", P),
               ("before", P), ("slot", SLOTS), ("prio", EXPERTS), ("causal", P)]
CONST_AT, _n = {}, 0
for _name, _w in CONST_PARTS:
    CONST_AT[_name] = (_n, _n + _w)
    _n += _w
CONST_COLS = _n
CONST_FIRST = 2 * P


def constant_table():
    c = np.zeros((P, CONST_COLS), np.float32)

    def put(name, v):
        a, b = CONST_AT[name]
        c[:, a:b] = v.reshape(P, b - a)

    i = np.arange(P)
    put("ident", np.eye(P))
    def logc(t, s):
        d = t[:, None] - s[None, :]
        n = ((d >= 0) & (d <= 128)) * 1.0 + ((d >= 0) & (d % 4 == 0)) + ((d >= 0) & (d % 16 == 0))
        return np.where(n > 0, np.log(np.maximum(n, 1)), NEG)
    put("logc", np.concatenate([logc(i, i), logc(i + P, np.arange(SEQ))], 1))
    g = 1.0 - 2.0 ** (-5.0 - np.arange(4))
    dist = np.concatenate([i[None, :] - i[:, None], P + i[None, :] - i[:, None]], 1)
    put("decay", np.where(dist[:, None, :] >= 0, g[None, :, None] ** np.maximum(dist, 0)[:, None, :], 0) * HD ** -0.5)
    half = HD // 2
    inv = np.float32(10000.0) ** (-np.arange(half, dtype=np.float32) / np.float32(half))
    ang = (np.arange(SEQ, dtype=np.float32)[None, :] * inv.astype(np.float32)[i % half, None]).astype(np.float32)
    put("cos", np.cos(ang.astype(np.float64)))
    put("sin", np.sin(ang.astype(np.float64)))
    sw = np.zeros((P, P))
    for m in range(P):
        if m % HD < half:
            sw[m + half, m] = -1.0
        else:
            sw[m - half, m] = 1.0
    put("swap", sw)
    put("before", (i[:, None] < i[None, :]) * 1.0)
    put("ones", np.ones((P, P)))
    put("slot", np.tile(1 + np.arange(SLOTS), (P, 1)))
    put("prio", np.tile(EXPERTS - np.arange(EXPERTS), (P, 1)))
    put("causal", (i[:, None] <= i[None, :]) * 1.0)
    return c


class Signal:

    def __init__(self, sem, turn, start=0):
        self.sem, self.turn, self.start = sem, turn, start

    def at(self, i, k):
        return i * self.turn + (k + self.start)


def hybrid_trunk(nc, x_in, norm1, w_in, a_ln_g, a_ln_b, a_ws, a_bs, ret_gn, w_out, norm2, router_g, router_gb,
                 router_e, router_eb, w_gate, w_up, w_down, final_norm, table, out):
    ctx = ExitStack()
    with ctx:
        ctx.enter_context(nc.allow_non_contiguous_dma("small parameters"))

        def sb(name, shape, dt=F32):
            return ctx.enter_context(nc.sbuf_tensor(name, shape, dt))

        def signal(name, turn, start=0):
            return Signal(ctx.enter_context(nc.semaphore(name)), turn, start)

        def settle(eng):
            eng.sem_inc(settled.sem)

        gate_b = sb("gate_b", [P, 2 * DC * HID])
        gate_w = [sb("gate_w", [P, 2, DC, HID]), gate_b.rearrange("p (e c n) -> p e c n", e=2, c=DC)]
        up_w = sb("up_w", [P, 2, DC, HID])
        down_w = sb("down_w", [P, 2, HC, D])
        piece = [down_w[:, s].rearrange("p c n -> p (c n)").rearrange("p (c n) -> p c n", c=DC) for s in range(2)]
        x = sb("x", [P, T, D])
        h = sb("h", [P, T, D])
        hT = sb("hT", [P, DC, SEQ])
        const = sb("const", [P, CONST_COLS])
        za = sb("za", [P, T, 2 * A_W])
        at = 0

        def shared(cols):
            nonlocal at
            at += cols
            return gate_b[:, at - cols:at]

        qkb = shared(8 * SEQ).rearrange("p (c t) -> p c t", c=8)
        vb = shared(T * B_W).rearrange("p (t n) -> p t n", t=T)
        qkc = shared(4 * SEQ).rearrange("p (c t) -> p c t", c=4)
        rot = shared(4 * SEQ).rearrange("p (c t) -> p c t", c=4)
        probsT = shared(2 * 12 * P).rearrange("p (k b j t) -> p k b j t", k=2, b=3, j=4)
        vgc = sb("vgc", [P, T, 2 * C_W])
        scores = sb("scores", [P, 4, 3 * P])
        work0 = sb("work0", [P, D])
        work1 = sb("work1", [P, D])
        work2 = sb("work2", [P, C_W * T])
        sgate = sb("sgate", [P, T, C_W])
        ws = sb("ws", [P, 4, P])
        wsT = sb("wsT", [P, 4, P])
        ln_g = sb("ln_g", [P, A_W])
        ln_b = sb("ln_b", [P, A_W])
        gn_g = sb("gn_g", [P, C_W])
        bs = sb("bs", [P, 4])
        gain1 = sb("gain1", [P, DC])
        gain2 = sb("gain2", [P, DC])
        rw = sb("rw", [P, DC, ROUTE])
        rb = sb("rb", [P, ROUTE])
        sumsq = sb("sumsq", [P, T])
        meansq = sb("meansq", [P, 8])
        rstd = sb("rstd", [P, 8])
        newton = sb("newton", [P, 8])
        half_bits = sb("half_bits", [P, 8], I32)
        guess_bits = sb("guess_bits", [P, 8], I32)
        stats = sb("stats", [P, T, 6])
        moments = sb("moments", [P, T, 2])
        nmax = sb("nmax", [P, 2, 8])
        denom = sb("denom", [P, 2, 8])
        rdenom = sb("rdenom", [P, 2, 8])
        gsum = sb("gsum", [P, 8])
        r = {n: sb("r_" + n, [P, T, w]) for n, w in
             [("logit", ROUTE), ("gmax", 1), ("gsh", 4), ("gexp", 4), ("gsum", 1), ("gw", 1), ("geq", 4), ("gp", 1),
              ("goh", 4), ("gpen", 4), ("sel", EXPERTS), ("m1", 1), ("eq1", EXPERTS), ("p1", 1), ("oh1", EXPERTS),
              ("sel2", EXPERTS), ("m2", 1), ("eq2", EXPERTS), ("p2", 1), ("oh2", EXPERTS), ("d", 1), ("e", 1),
              ("e1", 1), ("w1", 1), ("w2", 1), ("t1", EXPERTS), ("assign", EXPERTS), ("cw", EXPERTS),
              ("rank", EXPERTS)]}
        fullest = sb("fullest", [P, 1])
        more = sb("more", [P, 3])
        more_sum = sb("more_sum", [P, 1])
        last_f = sb("last_f", [P, 1])
        items = sb("items", [P, 2], I32)
        xT = sb("xT", [P, 2, DC, P])
        pick = wsT.rearrange("p g t -> p (g t)").rearrange("p (o t e s) -> p o t e s", o=2, t=T, e=2)
        pickw = sgate.rearrange("p t n -> p (t n)").rearrange("p (o t e s) -> p o t e s", o=2, t=T, e=2)
        pickT = work2.rearrange("p (o t s) -> p o t s", o=2, t=T)
        spread = work2[:, 0:SEQ]
        rstd_row = work2[:, SEQ:2 * SEQ]
        he, sig = work0[:, 0:HID], work0[:, HID:2 * HID]
        heT = scores.rearrange("p j s -> p (j s)")[:, 0:HID].rearrange("p (c s) -> p c s", c=HC)
        y = work1

        psum = ctx.enter_context(nc.psum_tensor("psum", [P, 8, 512], F32))

        def C(name):
            a, b = CONST_AT[name]
            return const[:, a:b]

        x_loaded, ident_loaded, const_loaded = [signal(n, 16) for n in ("x_loaded", "ident_loaded", "const_loaded")]
        gain1_loaded, ws_loaded = signal("gain1_loaded", 16), signal("ws_loaded", 16)
        mix_params_loaded, route_params_loaded = signal("mix_params_loaded", 16 * 4), signal("route_params_loaded", 16 * 5)
        rw_scaled = signal("rw_scaled", 1)
        piece_loaded = [signal(f"piece_loaded{s}", 16 * 4) for s in range(2)]
        ws_turned, ws_masked = signal("ws_turned", 1), signal("ws_masked", 1)
        x_mixed = signal("x_mixed", T)
        squared, summed = signal("squared", 1 + T), signal("summed", 1)
        spread_ready, rstd_spread = signal("spread_ready", 1), signal("rstd_spread", 1)
        turned = signal("turned", 12)
        turn_copied_a, turn_copied_d = signal("turn_copied_a", 6), signal("turn_copied_d", DC + T)
        projected = signal("projected", 6)
        proj_copied_a, proj_copied_d = signal("proj_copied_a", 6), signal("proj_copied_d", 6)
        scored, masked, exped = signal("scored", 2), signal("masked", 2), signal("exped", 2)
        probs_turned = signal("probs_turned", 2)
        probs_copied_a, probs_copied_d = signal("probs_copied_a", 2), signal("probs_copied_d", 2)
        attended, attn_stored = signal("attended", 2), signal("attn_stored", 2)
        swapped, swap_read, rotated = signal("swapped", 1), signal("swap_read", 1), signal("rotated", 1)
        cos_done = signal("cos_done", 1)
        inner_ready, decayed = signal("inner_ready", 1), signal("decayed", 1)
        retained = signal("retained", 1)
        gelu_arg, gelu_exp, gelu_den, gelu_rec = [signal(n, 1) for n in ("gelu_arg", "gelu_exp", "gelu_den", "gelu_rec")]
        gelu_done, ln_scaled, vn_ready = signal("gelu_done", 1), signal("ln_scaled", 1), signal("vn_ready", 1)
        silu_exp, silu_den, silu_rec, sgate_ready = [signal(n, 1) for n in ("silu_exp", "silu_den", "silu_rec", "sgate_ready")]
        spatial_done = signal("spatial_done", 1)
        mix_ready = signal("mix_ready", 1)
        out_done = signal("out_done", 2 * T)
        rstd_ready, tokens_ready = signal("rstd_ready", 1), signal("tokens_ready", 1)
        routed, route_args, route_exps = signal("routed", 1), signal("route_args", 1), signal("route_exps", 1)
        assigned, ranked, items_ready = signal("assigned", 1), signal("ranked", 2), signal("items_ready", 1)
        range_zeroed = signal("range_zeroed", 1)
        settled = signal("settled", 0)
        picked, gathered, xT_ready = signal("picked", 2), signal("gathered", 2), signal("xT_ready", 2)
        pick_turned, pickT_ready, v_pick = signal("pick_turned", 1), signal("pickT_ready", 1), signal("v_pick", 3)
        gate_loaded = [[signal(f"gate_loaded{o}{b}", 16) for b in range(2)] for o in range(2)]
        up_loaded = [signal(f"up_loaded{b}", 16) for b in range(2)]
        down_loaded = [signal(f"down_loaded{b}", 32) for b in range(2)]
        gated, upped, gate_exp = signal("gated", 2, 4), signal("upped", 2, 4), signal("gate_exp", 1)
        he_ready, he_turned, heT_ready = signal("he_ready", 1), signal("he_turned", 1), signal("heT_ready", 1)
        downed, y_ready = signal("downed", 2, 4), signal("y_ready", 2)
        scattered, x_added = signal("scattered", 4), signal("x_added", 4, 2)
        VSTEPS, VITEM, GSTEPS = 107, 3, 4
        v_step, v_item = signal("v_step", VSTEPS), signal("v_item", VITEM)
        v_last, g_step = signal("v_last", 0), signal("g_step", GSTEPS)
        out_ready, out_stored = signal("out_ready", T), [signal(f"out_stored{t}", 16) for t in range(T)]
        final_loaded = signal("final_loaded", 16)

        w_in_p = w_in.rearrange("l (p c) n -> l p c n", c=DC)
        w_out_p = w_out.rearrange("l (p c) n -> l p c n", c=DC)
        gate_d = w_gate.rearrange("l (q e) (p c) n -> (l q) p e c n", e=2, c=DC)
        up_d = w_up.rearrange("l (q e) (p c) n -> (l q) p e c n", e=2, c=DC)
        down_d = w_down.rearrange("l (q e) (p c) n -> (l q) p e c n", e=2, c=HC)
        BQ, BK, ZA, CQK, CVG, BV = range(6)
        PIECE_BANK = (0, 2, 0, 2, 0, 0)
        PIECE_AFTER = {ZA: BQ + 1, CQK: BK + 1, CVG: ZA + 1, BV: CVG + 1}
        PIECE_COL = {BQ: 2 * A_W, BK: 2 * A_W + B_W, CQK: 2 * A_W + 3 * B_W, ZA: 0, BV: 2 * A_W + 2 * B_W,
                     CVG: 2 * A_W + 3 * B_W + 2 * C_W}

        block = ctx.enter_context(nc.Block())

        @block.sync
        def _(sp):
            sp.dma_start(x[:], x_in.rearrange("b (t p) d -> p (b t) d", p=P)).then_inc(x_loaded.sem, 16)
            sp.wait_ge(range_zeroed.sem, 1)
            with sp.Fori(0, DEPTH) as l:
                first = sp.value_load(items[0:1, 1:2], min_val=0, max_val=4 * PAIRS * DEPTH)

                def load_piece(j, src):
                    s = j % 2
                    if j < 2:
                        sp.wait_ge(downed.sem, downed.at(first, 0))
                    else:
                        sp.wait_ge(projected.sem, projected.at(l, j - 1))
                    settle(sp)
                    sp.dma_start(piece[s], src).then_inc(piece_loaded[s].sem, 16)

                def load_halves(dst, src, loaded, used, g, q, back=0, halves=(0, 1)):
                    for b in halves:
                        if used is not None:
                            sp.wait_ge(used.sem, used.at(g, b + 1 - back * used.turn))
                            settle(sp)
                        if dst is down_w:
                            cols = slice(b * COLS, (b + 1) * COLS)
                            for e in range(2):
                                sp.dma_start(dst[:, e, :, cols], src[bass.ds(q, 1), :, e, :, cols]
                                             .rearrange("q p c n -> (q p) c n")).then_inc(loaded[b].sem, 16)
                        else:
                            sp.dma_start(dst[:, :, 4 * b:4 * b + 4, :], src[bass.ds(q, 1), :, :, 4 * b:4 * b + 4, :]
                                         .rearrange("q p e c n -> (q p) e c n")).then_inc(loaded[b].sem, 16)

                for j in range(6):
                    load_piece(j, w_in_p[bass.ds(l, 1), :, :, PIECE_COL[j]:PIECE_COL[j] + COLS]
                               .rearrange("l p c n -> (l p) c n"))
                    if j == 2:
                        load_halves(gate_w[0], gate_d, gate_loaded[0], gated, first, l * PAIRS, 1)
                    if j == 4:
                        load_halves(up_w, up_d, up_loaded, upped, first, l * PAIRS, 1)
                for n in range(2):
                    load_piece(6 + n, w_out_p[bass.ds(l, 1), :, :, n * COLS:(n + 1) * COLS]
                               .rearrange("l p c n -> (l p) c n"))
                sp.wait_ge(attended.sem, attended.at(l, 2))
                settle(sp)
                load_halves(gate_w[1], gate_d, gate_loaded[1], None, None, l * PAIRS + 1)
                sp.wait_ge(out_done.sem, out_done.at(l, 2 * T))
                settle(sp)
                load_halves(down_w, down_d, down_loaded, None, None, l * PAIRS)
                sp.wait_ge(items_ready.sem, items_ready.at(l, 1))
                settle(sp)
                last = sp.value_load(items[0:1, 1:2], min_val=PAIRS, max_val=4 * PAIRS * DEPTH)

                def pair(g):
                    return sp.snap((g & (PAIRS - 1)) + l * PAIRS)

                with sp.Fori(first, last - 2, 2) as g0:
                    for o in range(2):
                        g = g0 + o
                        load_halves(gate_w[o], gate_d, gate_loaded[o], gated, g, pair(g + 2), halves=(0,))
                        load_halves(up_w, up_d, up_loaded, upped, g, pair(g + 1))
                        load_halves(down_w, down_d, down_loaded, downed, g, pair(g + 1))
                        load_halves(gate_w[o], gate_d, gate_loaded[o], gated, g, pair(g + 2), halves=(1,))
                load_halves(up_w, up_d, up_loaded, upped, last, l * PAIRS + PAIRS - 1, 2)
                load_halves(down_w, down_d, down_loaded, downed, last, l * PAIRS + PAIRS - 1, 2)
            out_t = out.rearrange("b (t p) d -> p (b t) d", p=P)
            for t in range(T):
                sp.wait_ge(out_ready.sem, t + 1)
                sp.dma_start(out_t[:, t, :], h[:, t, :]).then_inc(out_stored[t].sem, 16)
            for t in range(T):
                sp.wait_ge(out_stored[t].sem, 16)

        @block.gpsimd
        def _(pool):
            def load_mix_params(l):
                row = lambda a: a[bass.ds(l, 1), :]
                pool.dma_start(gain1[:], norm1[bass.ds(l, 1)].rearrange("l (p c) -> (l p) c", c=DC)).then_inc(gain1_loaded.sem, 16)
                pool.dma_start(ws[:], a_ws[bass.ds(l, 1)].rearrange("l g t s -> (l t) g s")).then_inc(ws_loaded.sem, 16)
                for dst, src in [
                        (bs[:], a_bs[bass.ds(l, 1)].rearrange("l g t -> (l t) g")),
                        (ln_g[:], row(a_ln_g).to_broadcast([P, A_W])),
                        (ln_b[:], row(a_ln_b).to_broadcast([P, A_W])),
                        (gn_g[:], row(ret_gn).to_broadcast([P, C_W]))]:
                    pool.dma_start(dst, src).then_inc(mix_params_loaded.sem, 16)

            load_mix_params(0)
            with pool.Fori(0, DEPTH) as l:
                step = [0]

                def link(ins):
                    step[0] += 1
                    ins.then_inc(g_step.sem, 1)
                    pool.wait_ge(g_step.sem, g_step.at(l, step[0]))

                pool.wait_ge(summed.sem, summed.at(l, 1))
                row = lambda a: a[bass.ds(l, 1), :]
                for dst, src in [
                        (gain2[:], norm2[bass.ds(l, 1)].rearrange("l (p c) -> (l p) c", c=DC)),
                        (rw[:, :, 0:GROUPS], router_g[bass.ds(l, 1)].rearrange("l (p c) n -> (l p) c n", c=DC)),
                        (rw[:, :, GROUPS:ROUTE], router_e[bass.ds(l, 1)].rearrange("l (p c) n -> (l p) c n", c=DC)),
                        (rb[:, 0:GROUPS], row(router_gb).to_broadcast([P, GROUPS])),
                        (rb[:, GROUPS:ROUTE], row(router_eb).to_broadcast([P, EXPERTS]))]:
                    pool.dma_start(dst, src).then_inc(route_params_loaded.sem, 16)
                pool.wait_ge(route_params_loaded.sem, route_params_loaded.at(l, route_params_loaded.turn))
                pool.tensor_tensor(rw[:], rw[:], gain2[:].unsqueeze(2).to_broadcast([P, DC, ROUTE]), ALU.mult).then_inc(rw_scaled.sem, 1)

                zf = za.rearrange("p t n -> p (t n)")
                pool.wait_ge(proj_copied_a.sem, proj_copied_a.at(l, ZA + 1))
                pool.wait_ge(proj_copied_d.sem, proj_copied_d.at(l, ZA + 1))
                link(pool.tensor_tensor(work0[:], zf, zf, ALU.mult))
                settle(pool)
                link(pool.tensor_scalar(work0[:], work0[:], 0.044715, 1.0, ALU.mult, ALU.add))
                pool.tensor_tensor(work0[:], work0[:], zf, ALU.mult).then_inc(gelu_arg.sem, 1)
                pool.wait_ge(gelu_rec.sem, gelu_rec.at(l, 1))
                pool.tensor_tensor(zf, zf, work1[:], ALU.mult).then_inc(gelu_done.sem, 1)
                pool.wait_ge(proj_copied_a.sem, proj_copied_a.at(l, CQK + 1))
                pool.wait_ge(proj_copied_d.sem, proj_copied_d.at(l, CQK + 1))
                pool.wait_ge(const_loaded.sem, 16)
                pool.tensor_tensor(rot[:], qkc[:], C("cos").unsqueeze(1).to_broadcast([P, 4, SEQ]), ALU.mult).then_inc(cos_done.sem, 1)
                pool.wait_ge(ln_scaled.sem, ln_scaled.at(l, 1))
                pool.wait_ge(mix_params_loaded.sem, mix_params_loaded.at(l, mix_params_loaded.turn))
                v = za[:, :, A_W:2 * A_W]
                link(pool.tensor_tensor(v, v, ln_g[:].unsqueeze(1).to_broadcast([P, T, A_W]), ALU.mult))
                pool.tensor_tensor(v, v, ln_b[:].unsqueeze(1).to_broadcast([P, T, A_W]), ALU.add).then_inc(vn_ready.sem, 1)
                pool.wait_ge(silu_rec.sem, silu_rec.at(l, 1))
                w2 = work2.rearrange("p (t n) -> p t n", t=T)
                link(pool.tensor_tensor(sgate[:], vgc[:, :, C_W:2 * C_W], w2, ALU.mult))
                pool.tensor_tensor(sgate[:], sgate[:], gn_g[:].unsqueeze(1).to_broadcast([P, T, C_W]), ALU.mult).then_inc(sgate_ready.sem, 1)
                pool.wait_ge(turned.sem, turned.at(l, 8))
                pool.wait_ge(rstd_ready.sem, rstd_ready.at(l, 1))
                settle(pool)
                for t in range(T):
                    ins = pool.tensor_scalar(h[:, t, :], x[:, t, :], rstd[:, t:t + 1], None, ALU.mult)
                ins.then_inc(tokens_ready.sem, 1)
                load_mix_params(pool.snap((l + 1) & (DEPTH - 1)))
                assert step[0] == GSTEPS, ("GSTEPS", step[0])
            pool.wait_ge(summed.sem, DEPTH + 1)
            pool.wait_ge(mix_params_loaded.sem, 16 * 4 * (DEPTH + 1))
            pool.wait_ge(gain1_loaded.sem, 16 * (DEPTH + 1))
            pool.wait_ge(ws_loaded.sem, 16 * (DEPTH + 1))
            pool.dma_start(za.rearrange("p t n -> p (t n)"),
                           final_norm.rearrange("(a n) -> a n", a=1).to_broadcast([P, D])).then_inc(final_loaded.sem, 16)

        @block.scalar
        def _(act):
            act.dma_start(const[:, 0:CONST_FIRST], table[:, 0:CONST_FIRST]).then_inc(ident_loaded.sem, 16)

            def square(t, dst):
                act.activation(dst[:], x[:, t, :], ACT.Square, accum_out=sumsq[:, t:t + 1]).then_inc(squared.sem, 1)

            act.wait_ge(x_loaded.sem, 16)
            square(0, work0)
            act.wait_ge(piece_loaded[0].sem, 16)
            act.dma_start(const[:, CONST_FIRST:], table[:, CONST_FIRST:]).then_inc(const_loaded.sem, 16)
            with act.Fori(0, DEPTH) as l:
                def copy_turned(bank, count):
                    t, b = bank // 2, bank % 2
                    act.wait_ge(turned.sem, turned.at(l, count))
                    act.activation(hT[:, 4 * b:4 * b + 4, t * P:(t + 1) * P], psum[:, 4 + bank, :].rearrange("p (c t) -> p c t", c=4),
                                   ACT.Copy).then_inc(turn_copied_a.sem, 1)

                def copy_piece(j, dst):
                    act.wait_ge(projected.sem, projected.at(l, j + 1))
                    act.activation(dst, psum[:, PIECE_BANK[j], :], ACT.Copy).then_inc(proj_copied_a.sem, 1)

                def exps(k):
                    act.wait_ge(masked.sem, masked.at(l, k + 1))
                    for j in range(4):
                        act.activation(scores[:, j, 0:P], scores[:, j, 0:P], ACT.Exp, bias=nmax[:, k, j:j + 1],
                                       accum_out=denom[:, k, j:j + 1])
                        ins = act.activation(scores[:, j, P:3 * P], scores[:, j, P:3 * P], ACT.Exp,
                                             bias=nmax[:, k, 4 + j:5 + j], accum_out=denom[:, k, 4 + j:5 + j])
                    ins.then_inc(exped.sem, 1)

                def copy_probs(k):
                    act.wait_ge(probs_turned.sem, probs_turned.at(l, k + 1))
                    for b in (0, 2):
                        ins = act.activation(probsT[:, k, b].rearrange("p j t -> p (j t)"), psum[:, 4 + b, :], ACT.Copy)
                    ins.then_inc(probs_copied_a.sem, 1)

                copy_piece(BQ, qkb[:, 0:2, :].rearrange("p c t -> p (c t)"))
                copy_piece(BK, qkb[:, 4:6, :].rearrange("p c t -> p (c t)"))
                exps(0)
                copy_piece(ZA, za[:, 0, :])
                copy_probs(0)
                act.wait_ge(gelu_arg.sem, gelu_arg.at(l, 1))
                act.activation(work1[:], work0[:], ACT.Exp, scale=-2.0 * float(np.sqrt(2.0 / np.pi))).then_inc(gelu_exp.sem, 1)
                copy_piece(CQK, qkc[:, 0:2, :].rearrange("p c t -> p (c t)"))
                exps(1)
                copy_piece(CVG, vgc[:, 0, :])
                copy_probs(1)
                act.wait_ge(proj_copied_d.sem, proj_copied_d.at(l, CVG + 1))
                act.wait_ge(proj_copied_a.sem, proj_copied_a.at(l, CVG + 1))
                act.activation(work2.rearrange("p (t n) -> p t n", t=T), vgc[:, :, C_W:2 * C_W], ACT.Exp, scale=-1.0).then_inc(silu_exp.sem, 1)
                copy_piece(BV, vb[:, 0, :])
                copy_turned(0, 5)
                copy_turned(2, 7)
                for t in range(T):
                    act.wait_ge(x_mixed.sem, x_mixed.at(l, t + 1))
                    square(t, (work0, work1)[t])
                    copy_turned(2 * t, 9 + 2 * t)
                    copy_turned(2 * t + 1, 10 + 2 * t)
                act.wait_ge(route_args.sem, route_args.at(l, 1))
                act.activation(r["gexp"][:], r["gsh"][:], ACT.Exp)
                act.activation(r["e"][:], r["d"][:], ACT.Exp).then_inc(route_exps.sem, 1)

                def copy_pick(n, o):
                    act.wait_ge(pick_turned.sem, pick_turned.at(n, 1))
                    act.activation(pickT[:, o].rearrange("p t n -> p (t n)"), psum[:, 6, 0:SEQ], ACT.Copy).then_inc(pickT_ready.sem, 1)

                act.wait_ge(items_ready.sem, items_ready.at(l, 1))
                settle(act)
                first = act.value_load(items[0:1, 0:1], min_val=0, max_val=4 * PAIRS * DEPTH)
                last = act.value_load(items[0:1, 1:2], min_val=PAIRS, max_val=4 * PAIRS * DEPTH)
                copy_pick(first + l, 0)

                def item(g, o):
                    act.wait_ge(gated.sem, gated.at(g, 2))
                    act.activation(sig, psum[:, 0, :], ACT.Exp, scale=-1.0).then_inc(gate_exp.sem, 1)
                    act.wait_ge(he_turned.sem, he_turned.at(g, 1))
                    act.activation(heT.rearrange("p c n -> p (c n)"), psum[:, 0, :], ACT.Copy).then_inc(heT_ready.sem, 1)
                    copy_pick(g + l + 1, 1 - o)
                    for n in range(2):
                        act.wait_ge(downed.sem, downed.at(g, n + 1))
                        act.activation(y[:, n * COLS:(n + 1) * COLS], psum[:, 2 + n, :], ACT.Copy).then_inc(y_ready.sem, 1)

                with act.Fori(first, last, 2) as g0:
                    for o in range(2):
                        item(act.snap(g0 + o), o)
                act.wait_ge(x_added.sem, x_added.at(last, -1))
                square(0, work0)

        @block.tensor
        def _(pe):
            for used in (gated, upped, downed):
                for _ in range(used.start):
                    pe.nop().then_inc(used.sem, 1)
            ident = C("ident")
            pe.wait_ge(ident_loaded.sem, 16)
            pe.wait_ge(x_loaded.sem, 16)
            pe.wait_ge(range_zeroed.sem, 1)
            with pe.Fori(0, DEPTH) as l:
                prev = pe.value_load(items[0:1, 1:2], min_val=0, max_val=4 * PAIRS * DEPTH)

                def turn(src, t):
                    for b in range(2):
                        for c in range(4 * b, 4 * b + 4):
                            ins = pe.transpose(psum[:, 4 + 2 * t + b, (c % 4) * P:(c % 4 + 1) * P], src[:, t, c::DC], ident)
                        ins.then_inc(turned.sem, 1)

                def piece_arrived(j):
                    pe.wait_ge(piece_loaded[j % 2].sem, piece_loaded[j % 2].at(l, 16 * (j // 2 + 1)))

                def project(j, between=None):
                    w, bank = piece[j % 2], PIECE_BANK[j]
                    piece_arrived(j)
                    if j in PIECE_AFTER:
                        pe.wait_ge(proj_copied_a.sem, proj_copied_a.at(l, PIECE_AFTER[j]))
                        pe.wait_ge(proj_copied_d.sem, proj_copied_d.at(l, PIECE_AFTER[j]))
                    if j in (BQ, BK, CQK):
                        for m in range(4):
                            o = psum[:, bank + m // 2, (m % 2) * SEQ:(m % 2 + 1) * SEQ]
                            for c in range(DC):
                                if j == BQ and m == 0:
                                    pe.wait_ge(turn_copied_d.sem, turn_copied_d.at(l, c + 1))
                                ins = pe.matmul(o, w[:, c, m * P:(m + 1) * P], hT[:, c, :], start=(c == 0), stop=(c == DC - 1))
                            if m == 3:
                                ins.then_inc(projected.sem, 1)
                    else:
                        for t in range(T):
                            if t == 1 and between is not None:
                                between()
                            for c in range(DC):
                                ins = pe.matmul(psum[:, bank + t, :], hT[:, c, t * P:(t + 1) * P], w[:, c, :],
                                                start=(c == 0), stop=(c == DC - 1))
                        ins.then_inc(projected.sem, 1)

                def score(k):
                    pe.wait_ge(proj_copied_a.sem, proj_copied_a.at(l, BK + 1))
                    pe.wait_ge(proj_copied_d.sem, proj_copied_d.at(l, BK + 1))
                    if k == 1:
                        pe.wait_ge(probs_copied_a.sem, probs_copied_a.at(l, 1))
                        pe.wait_ge(probs_copied_d.sem, probs_copied_d.at(l, 1))
                    rows = slice(HD * k, HD * (k + 1))
                    for j in range(4):
                        q, kk = qkb[rows, j, :], qkb[rows, 4 + j, :]
                        pe.matmul(psum[:, 4, j * P:(j + 1) * P], q[:, 0:P], kk[:, 0:P], start=True, stop=True)
                        ins = pe.matmul(psum[:, 5 + j // 2, (j % 2) * SEQ:(j % 2 + 1) * SEQ], q[:, P:SEQ], kk,
                                        start=True, stop=True)
                    ins.then_inc(scored.sem, 1)

                def turn_probs(k):
                    pe.wait_ge(exped.sem, exped.at(l, k + 1))
                    for b in range(3):
                        for j in range(4):
                            ins = pe.transpose(psum[:, 4 + b, j * P:(j + 1) * P], scores[:, j, b * P:(b + 1) * P], ident)
                    ins.then_inc(probs_turned.sem, 1)

                def attend(k, bank):
                    pe.wait_ge(probs_copied_a.sem, probs_copied_a.at(l, k + 1))
                    pe.wait_ge(probs_copied_d.sem, probs_copied_d.at(l, k + 1))
                    for j in range(4):
                        cols = slice((2 * j + k) * HD, (2 * j + k + 1) * HD)
                        pe.matmul(psum[:, bank, j * HD:(j + 1) * HD], probsT[:, k, 0, j], vb[:, 0, cols], start=True, stop=True)
                        o = psum[:, bank, (4 + j) * HD:(5 + j) * HD]
                        pe.matmul(o, probsT[:, k, 1, j], vb[:, 0, cols], start=True, stop=False)
                        ins = pe.matmul(o, probsT[:, k, 2, j], vb[:, 1, cols], start=False, stop=True)
                    ins.then_inc(attended.sem, 1)

                def retain():
                    pe.wait_ge(decayed.sem, decayed.at(l, 1))
                    for j in range(4):
                        v = slice(j * HD, (j + 1) * HD)
                        pe.matmul(psum[:, 2, j * HD:(j + 1) * HD], scores[:, j, 0:P], vgc[:, 0, v], start=True, stop=True)
                        o = psum[:, 2, (4 + j) * HD:(5 + j) * HD]
                        pe.matmul(o, scores[:, j, P:2 * P], vgc[:, 0, v], start=True, stop=False)
                        ins = pe.matmul(o, scores[:, j, 2 * P:3 * P], vgc[:, 1, v], start=False, stop=True)
                    ins.then_inc(retained.sem, 1)

                for t in range(T):
                    pe.wait_ge(x_added.sem, x_added.at(prev, t - 1))
                    turn(x, t)
                pe.wait_ge(spread_ready.sem, spread_ready.at(l, 1))
                pe.matmul(psum[:, 3, 0:SEQ], C("ones"), spread, start=True, stop=True).then_inc(rstd_spread.sem, 1)
                project(BQ)
                pe.wait_ge(const_loaded.sem, 16)
                pe.wait_ge(ws_loaded.sem, ws_loaded.at(l, 16))
                for g in range(4):
                    ins = pe.transpose(psum[:, 7, g * P:(g + 1) * P], ws[:, g, :], ident)
                ins.then_inc(ws_turned.sem, 1)
                project(BK)
                score(0)
                project(ZA)
                turn_probs(0)
                project(CQK)
                score(1)
                pe.wait_ge(proj_copied_a.sem, proj_copied_a.at(l, CQK + 1))
                pe.wait_ge(proj_copied_d.sem, proj_copied_d.at(l, CQK + 1))
                for n in range(2):
                    ins = pe.matmul(psum[:, 2 + n, :], C("swap"), qkc[:, 2 * n:2 * n + 2, :].rearrange("p c t -> p (c t)"),
                                    start=True, stop=True)
                ins.then_inc(swapped.sem, 1)
                project(CVG)
                turn_probs(1)
                pe.wait_ge(ws_masked.sem, ws_masked.at(l, 1))
                pe.wait_ge(rotated.sem, rotated.at(l, 1))
                pe.wait_ge(probs_copied_a.sem, probs_copied_a.at(l, 2))
                for j in range(4):
                    rows = slice(HD * (j % 2), HD * (j % 2 + 1))
                    q, kk = rot[rows, j // 2, :], rot[rows, 2 + j // 2, :]
                    bank = (2, 3, 6, 7)[j]
                    pe.matmul(psum[:, bank, 0:SEQ], kk[:, 0:P], q, start=True, stop=True)
                    ins = pe.matmul(psum[:, bank, SEQ:SEQ + P], kk[:, P:SEQ], q[:, P:SEQ], start=True, stop=True)
                ins.then_inc(inner_ready.sem, 1)
                project(BV, retain)
                pe.wait_ge(vn_ready.sem, vn_ready.at(l, 1))
                for t in range(T):
                    for g in range(4):
                        ins = pe.matmul(psum[:, 3, t * A_W + g * HD:t * A_W + (g + 1) * HD], wsT[:, g, :],
                                        za[:, t, A_W + g * HD:A_W + (g + 1) * HD], start=True, stop=True)
                ins.then_inc(spatial_done.sem, 1)
                pe.wait_ge(proj_copied_a.sem, proj_copied_a.at(l, BV + 1))
                pe.wait_ge(proj_copied_d.sem, proj_copied_d.at(l, BV + 1))
                attend(0, 4)
                attend(1, 5)
                pe.wait_ge(mix_ready.sem, mix_ready.at(l, 1))
                for t in range(T):
                    turn(h, t)
                for t in range(T):
                    pe.wait_ge(turn_copied_a.sem, turn_copied_a.at(l, t + 1))
                    pe.wait_ge(turn_copied_d.sem, turn_copied_d.at(l, DC + t + 1))
                    for n in range(2):
                        if t == 0:
                            piece_arrived(6 + n)
                        for c in range(DC):
                            ins = pe.matmul(psum[:, 2 * t + n, :], hT[:, c, t * P:(t + 1) * P], piece[n][:, c, :],
                                            start=(c == 0), stop=(c == DC - 1))
                        ins.then_inc(out_done.sem, 1)
                for t in range(T):
                    pe.wait_ge(x_mixed.sem, x_mixed.at(l, t + 1))
                    turn(x, t)
                pe.wait_ge(rw_scaled.sem, rw_scaled.at(l, 1))
                for t in range(T):
                    pe.wait_ge(turn_copied_a.sem, turn_copied_a.at(l, 4 + 2 * t))
                    for c in range(DC):
                        ins = pe.matmul(psum[:, 0, t * ROUTE:(t + 1) * ROUTE], hT[:, c, t * P:(t + 1) * P], rw[:, c, :],
                                        start=(c == 0), stop=(c == DC - 1))
                ins.then_inc(routed.sem, 1)
                pe.wait_ge(assigned.sem, assigned.at(l, 1))
                asg = r["assign"]
                pe.matmul(psum[:, 1, 0:32], C("before"), asg[:].rearrange("p t e -> p (t e)"), start=True, stop=False)
                pe.matmul(psum[:, 1, 16:32], C("ones"), asg[:, 0, :], start=False, stop=True).then_inc(ranked.sem, 1)
                pe.matmul(psum[:, 2, 0:EXPERTS], C("ones"), asg[:, 0, :], start=True, stop=False)
                pe.matmul(psum[:, 2, 0:EXPERTS], C("ones"), asg[:, 1, :], start=False, stop=True).then_inc(ranked.sem, 1)
                pe.wait_ge(tokens_ready.sem, tokens_ready.at(l, 1))

                def gather(n, o, b):
                    for c in range(4 * b, 4 * b + 4):
                        for t in range(T):
                            ins = pe.matmul(psum[:, 4 + b, (c % 4) * P:(c % 4 + 1) * P], h[:, t, c::DC],
                                            pick[:, o, t].rearrange("p e s -> p (e s)"), start=(t == 0), stop=(t == T - 1))
                    ins.then_inc(gathered.sem, 1)

                def turn_pick(n, o):
                    pe.wait_ge(picked.sem, picked.at(n, 2))
                    for t in range(T):
                        ins = pe.transpose(psum[:, 6, t * P:(t + 1) * P], pickw[:, o, t].rearrange("p e s -> p (e s)"), ident)
                    ins.then_inc(pick_turned.sem, 1)

                def item(g, u, o):
                    for bank, w, loaded, turn_of, done in ((0, gate_w[o], gate_loaded[o], u, gated), (1, up_w, up_loaded, g, upped)):
                        for c in range(DC):
                            if c % 4 == 0:
                                if bank == 0:
                                    pe.wait_ge(xT_ready.sem, xT_ready.at(g + l, c // 4 + 1))
                                pe.wait_ge(loaded[c // 4].sem, loaded[c // 4].at(turn_of, 16))
                            for e in range(2):
                                ins = pe.matmul(psum[e * SLOTS:(e + 1) * SLOTS, bank, :], xT[:, o, c, e * SLOTS:(e + 1) * SLOTS],
                                                w[:, e, c, :], start=(c == 0), stop=(c == DC - 1))
                            if c % 4 == 3:
                                ins.then_inc(done.sem, 1)
                    n = g + l + 1
                    pe.wait_ge(picked.sem, picked.at(n, 1))
                    gather(n, 1 - o, 0)
                    pe.wait_ge(he_ready.sem, he_ready.at(g, 1))
                    for c in range(HC):
                        ins = pe.transpose(psum[:, 0, c * P:(c + 1) * P], he[:, c::HC], ident)
                    ins.then_inc(he_turned.sem, 1)
                    gather(n, 1 - o, 1)
                    pe.wait_ge(x_added.sem, x_added.at(g, 0))
                    turn_pick(n, 1 - o)
                    pe.wait_ge(heT_ready.sem, heT_ready.at(g, 1))
                    for n2 in range(2):
                        pe.wait_ge(down_loaded[n2].sem, down_loaded[n2].at(g, 32))
                        for c in range(HC):
                            for e in range(2):
                                ins = pe.matmul(psum[e * SLOTS:(e + 1) * SLOTS, 2 + n2, :], heT[:, c, e * SLOTS:(e + 1) * SLOTS],
                                                down_w[:, e, c, n2 * COLS:(n2 + 1) * COLS], start=(c == 0), stop=(c == HC - 1))
                        ins.then_inc(downed.sem, 1)
                    pe.wait_ge(pickT_ready.sem, pickT_ready.at(n, 1))
                    for n2 in range(2):
                        pe.wait_ge(y_ready.sem, y_ready.at(g, n2 + 1))
                        for t in range(T):
                            pe.wait_ge(x_added.sem, x_added.at(g, 2 * n2 + t - 1))
                            pe.matmul(psum[:, 6 + t, :], pickT[:, o, t, :], y[:, n2 * COLS:(n2 + 1) * COLS],
                                      start=True, stop=True).then_inc(scattered.sem, 1)

                pe.wait_ge(picked.sem, picked.at(prev + l, 1))
                gather(None, 0, 0)
                gather(None, 0, 1)
                turn_pick(prev + l, 0)
                pe.wait_ge(items_ready.sem, items_ready.at(l, 1))
                settle(pe)
                first = pe.value_load(items[0:1, 0:1], min_val=0, max_val=4 * PAIRS * DEPTH)
                last = pe.value_load(items[0:1, 1:2], min_val=PAIRS, max_val=4 * PAIRS * DEPTH)
                with pe.Fori(first, last, 2) as g0:
                    u = pe.snap(g0 >> 1)
                    item(g0, u, 0)
                    item(pe.snap(g0 + 1), u, 1)

        @block.vector
        def _(dve):
            V = nc.vector

            def inverse_roots(m, link):
                link(V.tensor_scalar(half_bits[:, 0:m], meansq[:, 0:m].bitcast(I32), 1, None, ALU.logical_shift_right))
                link(V.tensor_scalar(guess_bits[:, 0:m], half_bits[:, 0:m], -1.0, ROOT_MAGIC, ALU.mult, ALU.add))
                y0 = guess_bits[:, 0:m].bitcast(F32)
                for n in range(3):
                    link(V.scalar_tensor_tensor(newton[:, 0:m], y0, -0.5, meansq[:, 0:m], ALU.mult, ALU.mult))
                    link(V.tensor_tensor(newton[:, 0:m], newton[:, 0:m], y0, ALU.mult))
                    ins = V.scalar_tensor_tensor(rstd[:, 0:m], newton[:, 0:m], 1.5, y0, ALU.add, ALU.mult)
                    if n < 2:
                        link(ins)
                    y0 = rstd[:, 0:m]
                return ins


            V.memset(last_f[:], 0.0).then_inc(v_item.sem, 1)
            V.memset(items[:], 0).then_inc(range_zeroed.sem, 1)
            for k in range(x_added.start):
                V.memset(more[:, k:k + 1], 0.0).then_inc(x_added.sem, 1)

            def square():
                V.tensor_tensor_reduce(out=h[:, 1, :], in0=x[:, 1, :], in1=x[:, 1, :], scale=1.0, scalar=0.0,
                                       op0=ALU.mult, op1=ALU.add, accum_out=sumsq[:, 1:2]).then_inc(summed.sem, 1)

            dve.wait_ge(x_loaded.sem, 16)
            square()
            dve.wait_ge(ident_loaded.sem, 16)
            dve.wait_ge(range_zeroed.sem, 1)
            with dve.Fori(0, DEPTH) as l:
                step = [0]

                def link(ins):
                    step[0] += 1
                    ins.then_inc(v_step.sem, 1)
                    dve.wait_ge(v_step.sem, v_step.at(l, step[0]))

                def copy_piece(j, dst):
                    dve.wait_ge(projected.sem, projected.at(l, j + 1))
                    V.tensor_copy(dst, psum[:, PIECE_BANK[j] + 1, :]).then_inc(proj_copied_d.sem, 1)

                def mask(k):
                    dve.wait_ge(scored.sem, scored.at(l, k + 1))
                    logc = C("logc")
                    if k == 1:
                        dve.wait_ge(probs_turned.sem, probs_turned.at(l, 1))
                    link(V.scalar_tensor_tensor(scores[:, :, 0:P], psum[:, 4, :].rearrange("p (j s) -> p j s", j=4), HD ** -0.5,
                                                logc[:, 0:P].unsqueeze(1).to_broadcast([P, 4, P]), ALU.mult, ALU.add))
                    for b in range(2):
                        link(V.scalar_tensor_tensor(scores[:, 2 * b:2 * b + 2, P:3 * P],
                                                    psum[:, 5 + b, :].rearrange("p (j s) -> p j s", j=2), HD ** -0.5,
                                                    logc[:, P:3 * P].unsqueeze(1).to_broadcast([P, 2, SEQ]), ALU.mult, ALU.add))
                    link(V.tensor_reduce(nmax[:, k, 0:4], scores[:, :, 0:P], AX.X, ALU.max, negate=True))
                    V.tensor_reduce(nmax[:, k, 4:8], scores[:, :, P:3 * P], AX.X, ALU.max, negate=True).then_inc(masked.sem, 1)

                def copy_probs(k):
                    dve.wait_ge(probs_turned.sem, probs_turned.at(l, k + 1))
                    V.tensor_copy(probsT[:, k, 1].rearrange("p j t -> p (j t)"), psum[:, 5, :]).then_inc(probs_copied_d.sem, 1)

                def store_attention(k, bank):
                    link(V.reciprocal(rdenom[:, k, :], denom[:, k, :]))
                    dve.wait_ge(attended.sem, attended.at(l, k + 1))
                    dst = h[:, :, A_W:A_W + B_W].rearrange("p t (j e d) -> p t j e d", e=2, d=HD)[:, :, :, k, :]
                    V.tensor_tensor(dst, psum[:, bank, :].rearrange("p (t j d) -> p t j d", t=T, j=4),
                                    rdenom[:, k, :].rearrange("p (t j) -> p t j", t=T).unsqueeze(3).to_broadcast([P, T, 4, HD]),
                                    ALU.mult).then_inc(attn_stored.sem, 1)

                def pick_next(n, col, o, between=None):
                    def plink(k, ins):
                        ins.then_inc(v_pick.sem, 1)
                        dve.wait_ge(v_pick.sem, v_pick.at(n, k))

                    cols = slice(0, 2) if isinstance(col, int) else bass.ds(col, 2)
                    for t in range(T):
                        ins = V.tensor_tensor(pick[:, o, t], C("slot").unsqueeze(1).to_broadcast([P, 2, SLOTS]),
                                              r["rank"][:, t, cols].unsqueeze(2).to_broadcast([P, 2, SLOTS]), ALU.is_equal)
                        if t == 0:
                            plink(1, ins)
                    ins.then_inc(picked.sem, 1)
                    dve.wait_ge(picked.sem, picked.at(n, 1))
                    if between is not None:
                        between()
                    for t in range(T):
                        ins = V.tensor_tensor(pickw[:, o, t], pick[:, o, t],
                                              r["cw"][:, t, cols].unsqueeze(2).to_broadcast([P, 2, SLOTS]), ALU.mult)
                        if t == 0:
                            plink(2, ins)
                    ins.then_inc(picked.sem, 1)
                    rk = r["rank"][:, :, cols]
                    plink(3, V.tensor_scalar(rk, rk, -float(SLOTS), None, ALU.add))

                def copy_tokens(n, o):
                    for b in range(2):
                        dve.wait_ge(gathered.sem, gathered.at(n, b + 1))
                        V.tensor_tensor(xT[:, o, 4 * b:4 * b + 4, :], psum[:, 4 + b, :].rearrange("p (c s) -> p c s", c=4),
                                        gain2[:, 4 * b:4 * b + 4].unsqueeze(2).to_broadcast([P, 4, P]), ALU.mult).then_inc(xT_ready.sem, 1)

                dve.wait_ge(squared.sem, squared.at(l, 1))
                dve.wait_ge(summed.sem, summed.at(l, 1))
                link(V.tensor_scalar(meansq[:, 0:T], sumsq[:], 1.0 / D, EPS, ALU.mult, ALU.add))
                link(inverse_roots(T, link))
                V.tensor_tensor(spread.rearrange("p (t q) -> p t q", t=T), C("ident").unsqueeze(1).to_broadcast([P, T, P]),
                                rstd[:, 0:T].unsqueeze(2).to_broadcast([P, T, P]), ALU.mult).then_inc(spread_ready.sem, 1)
                dve.wait_ge(gain1_loaded.sem, gain1_loaded.at(l, 16))
                dve.wait_ge(turned.sem, turned.at(l, 4))
                dve.wait_ge(rstd_spread.sem, rstd_spread.at(l, 1))
                link(V.tensor_copy(rstd_row, psum[:, 3, 0:SEQ]))
                for c in range(DC):
                    for t in range(T):
                        ins = V.scalar_tensor_tensor(hT[:, c, t * P:(t + 1) * P],
                                                     psum[:, 4 + 2 * t + c // 4, (c % 4) * P:(c % 4 + 1) * P], gain1[:, c:c + 1],
                                                     rstd_row[:, t * P:(t + 1) * P], ALU.mult, ALU.mult)
                    ins.then_inc(turn_copied_d.sem, 1)
                prev = dve.value_load(items[0:1, 1:2], min_val=0, max_val=4 * PAIRS * DEPTH)
                dve.wait_ge(const_loaded.sem, 16)
                copy_piece(BQ, qkb[:, 2:4, :].rearrange("p c t -> p (c t)"))
                dve.wait_ge(ws_turned.sem, ws_turned.at(l, 1))
                V.tensor_tensor(wsT[:], psum[:, 7, :].rearrange("p (g t) -> p g t", g=4),
                                C("causal").unsqueeze(1).to_broadcast([P, 4, P]), ALU.mult).then_inc(ws_masked.sem, 1)
                copy_piece(BK, qkb[:, 6:8, :].rearrange("p c t -> p (c t)"))
                mask(0)
                copy_piece(ZA, za[:, 1, :])
                copy_probs(0)
                dve.wait_ge(gelu_exp.sem, gelu_exp.at(l, 1))
                link(V.tensor_scalar(work1[:], work1[:], 1.0, None, ALU.add))
                V.reciprocal(work1[:], work1[:]).then_inc(gelu_rec.sem, 1)
                copy_piece(CQK, qkc[:, 2:4, :].rearrange("p c t -> p (c t)"))
                mask(1)
                partner = xT[:, 0].rearrange("p c s -> p (c s)").rearrange("p (c t) -> p c t", c=4)
                dve.wait_ge(swapped.sem, swapped.at(l, 1))
                V.tensor_tensor(partner, psum[:, 2:4, :].rearrange("p b (c t) -> p (b c) t", c=2),
                                C("sin").unsqueeze(1).to_broadcast([P, 4, SEQ]), ALU.mult).then_inc(swap_read.sem, 1)
                dve.wait_ge(swap_read.sem, swap_read.at(l, 1))
                dve.wait_ge(cos_done.sem, cos_done.at(l, 1))
                V.tensor_tensor(rot[:], rot[:], partner, ALU.add).then_inc(rotated.sem, 1)
                dve.wait_ge(gelu_done.sem, gelu_done.at(l, 1))
                for t in range(T):
                    link(V.bn_stats(stats[:, t, :], za[:, t, A_W:2 * A_W]))
                for t in range(T):
                    settle(dve)
                    link(V.bn_aggr(moments[:, t, :], stats[:, t, :]))
                link(V.tensor_scalar(meansq[:, 0:T], moments[:, :, 1], EPS, None, ALU.add))
                link(inverse_roots(T, link))
                for t in range(T):
                    v = za[:, t, A_W:2 * A_W]
                    ins = V.tensor_scalar(v, v, moments[:, t, 0:1], rstd[:, t:t + 1], ALU.subtract, ALU.mult)
                    if t < T - 1:
                        link(ins)
                ins.then_inc(ln_scaled.sem, 1)
                copy_piece(CVG, vgc[:, 1, :])
                copy_probs(1)
                dve.wait_ge(inner_ready.sem, inner_ready.at(l, 1))
                dve.wait_ge(probs_turned.sem, probs_turned.at(l, 2))
                dec = C("decay").rearrange("p (j t) -> p j t", j=4)
                for j, bank in ((0, 2), (2, 6)):
                    link(V.tensor_tensor(scores[:, j:j + 2, 0:SEQ], psum[:, bank:bank + 2, 0:SEQ], dec[:, j:j + 2, :], ALU.mult))
                    ins = V.tensor_tensor(scores[:, j:j + 2, SEQ:SEQ + P], psum[:, bank:bank + 2, SEQ:SEQ + P],
                                          dec[:, j:j + 2, 0:P], ALU.mult)
                    if j == 0:
                        link(ins)
                ins.then_inc(decayed.sem, 1)
                dve.wait_ge(silu_exp.sem, silu_exp.at(l, 1))
                link(V.tensor_scalar(work2[:], work2[:], 1.0, None, ALU.add))
                V.reciprocal(work2[:], work2[:]).then_inc(silu_rec.sem, 1)
                dve.wait_ge(retained.sem, retained.at(l, 1))
                o = psum[:, 2, :].rearrange("p (k d) -> p k d", d=HD)
                cen = work1[:, 0:512].rearrange("p (k d) -> p k d", d=HD)
                sq = work1[:, 512:1024].rearrange("p (k d) -> p k d", d=HD)
                link(V.tensor_reduce(gsum[:], o, AX.X, ALU.add))
                link(V.tensor_scalar(gsum[:], gsum[:], 1.0 / HD, None, ALU.mult))
                link(V.tensor_tensor(cen, o, gsum[:].unsqueeze(2).to_broadcast([P, 8, HD]), ALU.subtract))
                link(V.tensor_tensor(sq, cen, cen, ALU.mult))
                link(V.tensor_reduce(gsum[:], sq, AX.X, ALU.add))
                link(V.tensor_scalar(meansq[:], gsum[:], 1.0 / HD, EPS, ALU.mult, ALU.add))
                link(inverse_roots(8, link))
                link(V.tensor_tensor(cen, cen, rstd[:].unsqueeze(2).to_broadcast([P, 8, HD]), ALU.mult))
                copy_piece(BV, vb[:, 1, :])
                dve.wait_ge(sgate_ready.sem, sgate_ready.at(l, 1))
                link(V.tensor_tensor(h[:, :, A_W + B_W:D], work1[:, 0:512].rearrange("p (t n) -> p t n", t=T), sgate[:], ALU.mult))
                dve.wait_ge(spatial_done.sem, spatial_done.at(l, 1))
                w0 = work0[:, 0:T * A_W].rearrange("p (t g d) -> p t g d", t=T, g=4)
                for t in range(T):
                    link(V.tensor_tensor(w0[:, t], psum[:, 3, t * A_W:(t + 1) * A_W].rearrange("p (g d) -> p g d", g=4),
                                         bs[:].unsqueeze(2).to_broadcast([P, 4, HD]), ALU.add))
                link(V.tensor_tensor(h[:, :, 0:A_W], work0[:, 0:T * A_W].rearrange("p (t n) -> p t n", t=T), za[:, :, 0:A_W], ALU.mult))
                for k in range(2):
                    store_attention(k, 4 + k)
                dve.wait_ge(attn_stored.sem, attn_stored.at(l, 2))
                V.memset(newton[:], 0.0).then_inc(mix_ready.sem, 1)
                for t in range(T):
                    dve.wait_ge(turned.sem, turned.at(l, 6 + 2 * t))
                    V.tensor_copy(hT[:, 4:8, t * P:(t + 1) * P],
                                  psum[:, 5 + 2 * t, :].rearrange("p (c t) -> p c t", c=4)).then_inc(turn_copied_d.sem, 1)
                for t in range(T):
                    for n in range(2):
                        dve.wait_ge(out_done.sem, out_done.at(l, 2 * t + n + 1))
                        xs = x[:, t, n * COLS:(n + 1) * COLS]
                        ins = V.tensor_tensor(xs, psum[:, 2 * t + n, :], xs, ALU.add)
                        if n == 0:
                            link(ins)
                    ins.then_inc(x_mixed.sem, 1)
                dve.wait_ge(squared.sem, squared.at(l, 1 + T))
                link(V.tensor_scalar(meansq[:, 0:T], sumsq[:], 1.0 / D, EPS, ALU.mult, ALU.add))
                inverse_roots(T, link).then_inc(rstd_ready.sem, 1)
                dve.wait_ge(rstd_ready.sem, rstd_ready.at(l, 1))

                dve.wait_ge(routed.sem, routed.at(l, 1))
                R = {k: t[:] for k, t in r.items()}
                def both(op):
                    op(0)
                    link(op(1))

                both(lambda t: V.scalar_tensor_tensor(r["logit"][:, t, :], psum[:, 0, t * ROUTE:(t + 1) * ROUTE], rstd[:, t:t + 1],
                                                      rb[:], ALU.mult, ALU.add))
                gl = r["logit"][:, :, 0:GROUPS]
                link(V.tensor_reduce(R["gmax"], gl, AX.X, ALU.max))
                V.tensor_tensor(R["gsh"], gl, r["gmax"][:].to_broadcast([P, T, 4]), ALU.subtract)
                both(lambda t: V.scalar_tensor_tensor(r["geq"][:, t, :], r["logit"][:, t, 0:GROUPS], r["gmax"][:, t, :],
                                                      C("prio")[:, 0:GROUPS], ALU.is_equal, ALU.mult))
                link(V.tensor_reduce(R["gp"], R["geq"], AX.X, ALU.max))
                link(V.tensor_tensor(R["goh"], R["geq"], r["gp"][:].to_broadcast([P, T, 4]), ALU.is_equal))
                link(V.tensor_scalar(R["gpen"], R["goh"], -NEG, NEG, ALU.mult, ALU.add))
                both(lambda t: V.tensor_tensor(r["sel"][:, t].rearrange("p (g e) -> p g e", g=GROUPS),
                                               r["logit"][:, t, GROUPS:ROUTE].rearrange("p (g e) -> p g e", g=GROUPS),
                                               r["gpen"][:, t].unsqueeze(2).to_broadcast([P, GROUPS, PER_GROUP]), ALU.add))
                for m, eq, pr, oh, sel in (("m1", "eq1", "p1", "oh1", "sel"), ("m2", "eq2", "p2", "oh2", "sel2")):
                    if sel == "sel2":
                        link(V.scalar_tensor_tensor(R["sel2"], R["oh1"], 3 * NEG, R["sel"], ALU.mult, ALU.add))
                    link(V.tensor_reduce(R[m], R[sel], AX.X, ALU.max))
                    both(lambda t: V.scalar_tensor_tensor(r[eq][:, t, :], r[sel][:, t, :], r[m][:, t, :], C("prio"),
                                                          ALU.is_equal, ALU.mult))
                    link(V.tensor_reduce(R[pr], R[eq], AX.X, ALU.max))
                    link(V.tensor_tensor(R[oh], R[eq], r[pr][:].to_broadcast([P, T, EXPERTS]), ALU.is_equal))
                V.tensor_tensor(R["assign"], R["oh1"], R["oh2"], ALU.add).then_inc(assigned.sem, 1)
                V.tensor_tensor(R["d"], R["m2"], R["m1"], ALU.subtract).then_inc(route_args.sem, 1)
                dve.wait_ge(assigned.sem, assigned.at(l, 1))
                dve.wait_ge(ranked.sem, ranked.at(l, 1))
                link(V.scalar_tensor_tensor(R["rank"], psum[:, 1, 0:32].rearrange("p (t e) -> p t e", t=T), 1.0, R["assign"],
                                            ALU.add, ALU.mult))

                def combine_weights():
                    dve.wait_ge(route_exps.sem, route_exps.at(l, 1))
                    V.tensor_scalar(R["e1"], R["e"], 1.0, None, ALU.add)
                    link(V.tensor_reduce(R["gsum"], R["gexp"], AX.X, ALU.add))
                    V.reciprocal(R["gw"], R["gsum"])
                    link(V.reciprocal(R["w1"], R["e1"]))
                    link(V.tensor_tensor(R["w1"], R["w1"], R["gw"], ALU.mult))
                    V.tensor_tensor(R["cw"], R["oh1"], r["w1"][:].to_broadcast([P, T, EXPERTS]), ALU.mult)
                    link(V.tensor_tensor(R["w2"], R["w1"], R["e"], ALU.mult))
                    link(V.tensor_tensor(R["t1"], R["oh2"], r["w2"][:].to_broadcast([P, T, EXPERTS]), ALU.mult))
                    link(V.tensor_tensor(R["cw"], R["cw"], R["t1"], ALU.add))

                pick_next(prev + l, 0, 0, combine_weights)
                dve.wait_ge(ranked.sem, ranked.at(l, 2))
                link(V.tensor_reduce(fullest[:], psum[:, 2, 0:EXPERTS], AX.X, ALU.max))
                V.tensor_copy(items[:, 0:1], last_f[:])
                for k in range(3):
                    ins = V.tensor_scalar(more[:, k:k + 1], fullest[:], SLOTS * (k + 1) + 0.5, float(PAIRS), ALU.is_gt, ALU.mult)
                link(ins)
                link(V.tensor_reduce(more_sum[:], more[:], AX.X, ALU.add))
                link(V.scalar_tensor_tensor(last_f[:], last_f[:], float(PAIRS), more_sum[:], ALU.add, ALU.add))
                V.tensor_copy(items[:, 1:2], last_f[:]).then_inc(items_ready.sem, 1)
                assert step[0] == VSTEPS, ("VSTEPS", step[0])

                dve.wait_ge(items_ready.sem, items_ready.at(l, 1))
                settle(dve)
                first = dve.value_load(items[0:1, 0:1], min_val=0, max_val=4 * PAIRS * DEPTH)
                last = dve.value_load(items[0:1, 1:2], min_val=PAIRS, max_val=4 * PAIRS * DEPTH)
                copy_tokens(first + l, 0)

                def item(g, o):
                    istep = [0]

                    def ilink(ins):
                        istep[0] += 1
                        ins.then_inc(v_item.sem, 1)
                        dve.wait_ge(v_item.sem, v_item.at(g, istep[0] + 1))

                    pick_next(g + l + 1, dve.snap(((g + 1) & (PAIRS - 1)) * 2), 1 - o)
                    dve.wait_ge(gate_exp.sem, gate_exp.at(g, 1))
                    ilink(V.tensor_scalar(sig, sig, 1.0, None, ALU.add))
                    ilink(V.reciprocal(sig, sig))
                    ilink(V.tensor_tensor(sig, sig, psum[:, 0, :], ALU.mult))
                    dve.wait_ge(upped.sem, upped.at(g, 2))
                    V.tensor_tensor(he, sig, psum[:, 1, :], ALU.mult).then_inc(he_ready.sem, 1)
                    copy_tokens(g + l + 1, 1 - o)
                    for n in range(2):
                        for t in range(T):
                            k = 2 * n + t
                            dve.wait_ge(scattered.sem, scattered.at(g, k + 1))
                            xs = x[:, t, n * COLS:(n + 1) * COLS]
                            V.tensor_tensor(xs, psum[:, 6 + t, :], xs, ALU.add).then_inc(x_added.sem, 1)
                    dve.wait_ge(x_added.sem, x_added.at(g, 4))
                    assert istep[0] == VITEM, ("VITEM", istep[0])

                with dve.Fori(first, last, 2) as g0:
                    for o in range(2):
                        item(dve.snap(g0 + o), o)
                square()

            step = [0]

            def link(ins):
                step[0] += 1
                ins.then_inc(v_last.sem, 1)
                dve.wait_ge(v_last.sem, step[0])

            dve.wait_ge(squared.sem, squared.at(DEPTH, 1))
            dve.wait_ge(summed.sem, summed.at(DEPTH, 1))
            link(V.tensor_scalar(meansq[:, 0:T], sumsq[:], 1.0 / D, EPS, ALU.mult, ALU.add))
            link(inverse_roots(T, link))
            dve.wait_ge(final_loaded.sem, 16)
            for t in range(T):
                V.scalar_tensor_tensor(h[:, t, :], x[:, t, :], rstd[:, t:t + 1], za.rearrange("p t n -> p (t n)"),
                                       ALU.mult, ALU.mult).then_inc(out_ready.sem, 1)


NAMES = ["x", "norm1", "w_in", "a_ln_g", "a_ln_b", "a_ws", "a_bs", "ret_gn", "w_out", "norm2", "router_g", "router_gb",
         "router_e", "router_eb", "w_gate", "w_up", "w_down", "final_norm"]


def kernel(**inputs):
    import concourse.bacc as bacc
    from concourse.bass_utils import run_bass_kernel_spmd as run

    nc = bacc.Bacc("TRN2", target_bir_lowering=False, num_devices=1)
    arrays, args = {}, []
    for name in NAMES:
        a = np.ascontiguousarray(inputs[name])
        arrays[f"in_{name}"] = a
        args.append(nc.dram_tensor(f"in_{name}", a.shape, mybir.dt.from_np(a.dtype), kind="ExternalInput").ap())
    arrays["table"] = constant_table()
    args.append(nc.dram_tensor("table", (P, CONST_COLS), F32, kind="ExternalInput").ap())
    args.append(nc.dram_tensor("out", (1, SEQ, D), F32, kind="ExternalOutput").ap())
    hybrid_trunk(nc, *args)
    return run(nc, [arrays], core_ids=[0]).results[0]["out"]
```

```python
import numpy as np
import concourse.bass as bass
from concourse import mybir
from contextlib import ExitStack

F32 = mybir.dt.float32
F32R = mybir.dt.float32r
I32 = mybir.dt.int32
ALU = mybir.AluOpType
ACT = mybir.ActivationFunctionType
AX = mybir.AxisListType

P = 128
D = 1024
SEQ = 256
DEPTH = 2
T = SEQ // P
DC = D // P
HD = 64
COLS = 512
HID = D // 2
HC = HID // P
A_W, B_W, C_W = D // 4, D // 2, D // 4
GROUPS, PER_GROUP = 4, 4
EXPERTS = GROUPS * PER_GROUP
PAIRS = EXPERTS // 2
SLOTS = P // 2
ROUTE = GROUPS + EXPERTS
EPS = 1e-6
NEG = -1e30
ROOT_MAGIC = float(0x5f3759df)

CONST_PARTS = [("ident", P), ("ones", P), ("logc", 3 * P), ("decay", 4 * 2 * P), ("cos", SEQ), ("sin", SEQ), ("swap", P),
               ("before", P), ("slot", SLOTS), ("prio", EXPERTS), ("causal", P)]
CONST_AT, _n = {}, 0
for _name, _w in CONST_PARTS:
    CONST_AT[_name] = (_n, _n + _w)
    _n += _w
CONST_COLS = _n
CONST_FIRST = 2 * P


def constant_table():
    c = np.zeros((P, CONST_COLS), np.float32)

    def put(name, v):
        a, b = CONST_AT[name]
        c[:, a:b] = v.reshape(P, b - a)

    i = np.arange(P)
    put("ident", np.eye(P))
    def logc(t, s):
        d = t[:, None] - s[None, :]
        n = ((d >= 0) & (d <= 128)) * 1.0 + ((d >= 0) & (d % 4 == 0)) + ((d >= 0) & (d % 16 == 0))
        return np.where(n > 0, np.log(np.maximum(n, 1)), NEG)
    put("logc", np.concatenate([logc(i, i), logc(i + P, np.arange(SEQ))], 1))
    g = 1.0 - 2.0 ** (-5.0 - np.arange(4))
    dist = np.concatenate([i[None, :] - i[:, None], P + i[None, :] - i[:, None]], 1)
    put("decay", np.where(dist[:, None, :] >= 0, g[None, :, None] ** np.maximum(dist, 0)[:, None, :], 0) * HD ** -0.5)
    half = HD // 2
    inv = np.float32(10000.0) ** (-np.arange(half, dtype=np.float32) / np.float32(half))
    ang = (np.arange(SEQ, dtype=np.float32)[None, :] * inv.astype(np.float32)[i % half, None]).astype(np.float32)
    put("cos", np.cos(ang.astype(np.float64)))
    put("sin", np.sin(ang.astype(np.float64)))
    sw = np.zeros((P, P))
    for m in range(P):
        if m % HD < half:
            sw[m + half, m] = -1.0
        else:
            sw[m - half, m] = 1.0
    put("swap", sw)
    put("before", (i[:, None] < i[None, :]) * 1.0)
    put("ones", np.ones((P, P)))
    put("slot", np.tile(1 + np.arange(SLOTS), (P, 1)))
    put("prio", np.tile(EXPERTS - np.arange(EXPERTS), (P, 1)))
    put("causal", (i[:, None] <= i[None, :]) * 1.0)
    return c


class Signal:

    def __init__(self, sem, turn, start=0):
        self.sem, self.turn, self.start = sem, turn, start

    def at(self, i, k):
        return i * self.turn + (k + self.start)


def hybrid_trunk(nc, x_in, norm1, w_in, a_ln_g, a_ln_b, a_ws, a_bs, ret_gn, w_out, norm2, router_g, router_gb,
                 router_e, router_eb, w_gate, w_up, w_down, final_norm, table, out):
    ctx = ExitStack()
    with ctx:
        ctx.enter_context(nc.allow_non_contiguous_dma("small parameters"))

        def sb(name, shape, dt=F32):
            return ctx.enter_context(nc.sbuf_tensor(name, shape, dt))

        def signal(name, turn, start=0):
            return Signal(ctx.enter_context(nc.semaphore(name)), turn, start)

        def settle(eng):
            eng.sem_inc(settled.sem)

        def over(name, shape, offset):
            return nc.alloc_sbuf_tensor_at(name, shape, F32R, offset=offset)

        gate_b = sb("gate_b", [P, 2 * DC * HID])
        gate_a = sb("gate_a", [P, 2, DC, HID])
        gate_w = [gate_b.rearrange("p (e c n) -> p e c n", e=2, c=DC), gate_a]
        gate_a_at = nc.sbuf_base - 4 * 2 * DC * HID
        hT_parts = [over(f"hT_part{k}", [P, DC, SEQ], gate_a_at + 4 * k * DC * SEQ) for k in range(2)]
        piece_hi = [over("piece_hi0", [P, DC, COLS], gate_a_at + 4 * 2 * DC * SEQ)]
        up_w = sb("up_w", [P, 2, DC, HID])
        down_w = sb("down_w", [P, 2, HC, D])
        down_at = nc.sbuf_base - 4 * 2 * HC * D
        piece_lo = [over(f"piece_lo{s}", [P, DC, COLS], down_at + 4 * s * DC * COLS) for s in range(2)]
        piece = [down_w[:, s].rearrange("p c n -> p (c n)").rearrange("p (c n) -> p c n", c=DC) for s in range(2)]
        x = sb("x", [P, T, D])
        h = sb("h", [P, T, D])
        hT = sb("hT", [P, DC, SEQ])
        xT = sb("xT", [P, 2, DC, P])
        piece_hi.append(over("piece_hi1", [P, DC, COLS], nc.sbuf_base - 4 * DC * (SEQ + 2 * P)))
        const = sb("const", [P, CONST_COLS])
        za = sb("za", [P, T, 2 * A_W])
        at = 0

        def shared(cols):
            nonlocal at
            at += cols
            return gate_b[:, at - cols:at]

        qkb = shared(8 * SEQ).rearrange("p (c t) -> p c t", c=8)
        vb = shared(T * B_W).rearrange("p (t n) -> p t n", t=T)
        qkc = shared(4 * SEQ).rearrange("p (c t) -> p c t", c=4)
        rot = shared(4 * SEQ).rearrange("p (c t) -> p c t", c=4)
        probsT = shared(2 * 12 * P).rearrange("p (k b j t) -> p k b j t", k=2, b=3, j=4)
        vgc = sb("vgc", [P, T, 2 * C_W])
        scores = sb("scores", [P, 4, 3 * P])
        work0 = sb("work0", [P, D])
        work1 = sb("work1", [P, D])
        work2 = sb("work2", [P, C_W * T])
        sgate = sb("sgate", [P, T, C_W])
        ws = sb("ws", [P, 4, P])
        wsT = sb("wsT", [P, 4, P])
        ln_g = sb("ln_g", [P, A_W])
        ln_b = sb("ln_b", [P, A_W])
        gn_g = sb("gn_g", [P, C_W])
        bs = sb("bs", [P, 4])
        gain1 = sb("gain1", [P, DC])
        gain2 = sb("gain2", [P, DC])
        rw = sb("rw", [P, DC, ROUTE])
        rb = sb("rb", [P, ROUTE])
        sumsq = sb("sumsq", [P, T])
        meansq = sb("meansq", [P, 8])
        rstd = sb("rstd", [P, 8])
        newton = sb("newton", [P, 8])
        half_bits = sb("half_bits", [P, 8], I32)
        guess_bits = sb("guess_bits", [P, 8], I32)
        stats = sb("stats", [P, T, 6])
        moments = sb("moments", [P, T, 2])
        nmax = sb("nmax", [P, 2, 8])
        denom = sb("denom", [P, 2, 8])
        rdenom = sb("rdenom", [P, 2, 8])
        gsum = sb("gsum", [P, 8])
        r = {n: sb("r_" + n, [P, T, w]) for n, w in
             [("logit", ROUTE), ("gmax", 1), ("gsh", 4), ("gexp", 4), ("gsum", 1), ("gw", 1), ("geq", 4), ("gp", 1),
              ("goh", 4), ("gpen", 4), ("sel", EXPERTS), ("m1", 1), ("eq1", EXPERTS), ("p1", 1), ("oh1", EXPERTS),
              ("sel2", EXPERTS), ("m2", 1), ("eq2", EXPERTS), ("p2", 1), ("oh2", EXPERTS), ("d", 1), ("e", 1),
              ("e1", 1), ("w1", 1), ("w2", 1), ("t1", EXPERTS), ("assign", EXPERTS), ("cw", EXPERTS),
              ("rank", EXPERTS)]}
        fullest = sb("fullest", [P, 1])
        more = sb("more", [P, 3])
        more_sum = sb("more_sum", [P, 1])
        last_f = sb("last_f", [P, 1])
        items = sb("items", [P, 2], I32)
        pick = wsT.rearrange("p g t -> p (g t)").rearrange("p (o t e s) -> p o t e s", o=2, t=T, e=2)
        pickw = sgate.rearrange("p t n -> p (t n)").rearrange("p (o t e s) -> p o t e s", o=2, t=T, e=2)
        pickT = work2.rearrange("p (o t s) -> p o t s", o=2, t=T)
        spread = work2[:, 0:SEQ]
        rstd_row = work2[:, SEQ:2 * SEQ]
        he, sig = work0[:, 0:HID], work0[:, HID:2 * HID]
        heT = scores.rearrange("p j s -> p (j s)")[:, 0:HID].rearrange("p (c s) -> p c s", c=HC)
        y = work1

        psum = ctx.enter_context(nc.psum_tensor("psum", [P, 8, 512], F32))

        def C(name):
            a, b = CONST_AT[name]
            return const[:, a:b]

        x_loaded, ident_loaded, const_loaded = [signal(n, 16) for n in ("x_loaded", "ident_loaded", "const_loaded")]
        gain1_loaded, ws_loaded = signal("gain1_loaded", 16), signal("ws_loaded", 16)
        mix_params_loaded, route_params_loaded = signal("mix_params_loaded", 16 * 4), signal("route_params_loaded", 16 * 5)
        rw_scaled = signal("rw_scaled", 1)
        piece_loaded = [signal(f"piece_loaded{s}", 16 * 4) for s in range(2)]
        ws_turned, ws_masked = signal("ws_turned", 1), signal("ws_masked", 1)
        x_mixed = signal("x_mixed", T)
        squared, summed = signal("squared", 1 + T), signal("summed", 1)
        spread_ready, rstd_spread = signal("spread_ready", 1), signal("rstd_spread", 1)
        turned = signal("turned", 12)
        turn_copied_a, turn_copied_d = signal("turn_copied_a", 4), signal("turn_copied_d", DC + 4)
        hT_hi_ready, hT_split = signal("hT_hi_ready", 5), signal("hT_split", 1)
        piece_hi_ready, piece_split = signal("piece_hi_ready", 10), signal("piece_split", 8)
        piece6_split = signal("piece6_split", 2)
        projected = signal("projected", 6)
        proj_copied_a, proj_copied_d = signal("proj_copied_a", 7), signal("proj_copied_d", 5)
        scored, masked, exped = signal("scored", 2), signal("masked", 2), signal("exped", 2)
        probs_turned = signal("probs_turned", 2)
        probs_copied_a, probs_copied_d = signal("probs_copied_a", 2), signal("probs_copied_d", 2)
        attended, attn_stored = signal("attended", 2), signal("attn_stored", 2)
        swapped, swap_read, rotated = signal("swapped", 1), signal("swap_read", 1), signal("rotated", 1)
        cos_done = signal("cos_done", 1)
        inner_ready, decayed = signal("inner_ready", 1), signal("decayed", 1)
        retained = signal("retained", 1)
        gelu_arg, gelu_exp, gelu_rec = [signal(n, 1) for n in ("gelu_arg", "gelu_exp", "gelu_rec")]
        gelu_done, ln_scaled, vn_ready = signal("gelu_done", 1), signal("ln_scaled", 1), signal("vn_ready", 1)
        silu_exp, silu_rec, sgate_ready = [signal(n, 1) for n in ("silu_exp", "silu_rec", "sgate_ready")]
        spatial_done = signal("spatial_done", 1)
        out_done = signal("out_done", 2 * T)
        rstd_ready, tokens_ready = signal("rstd_ready", 1), signal("tokens_ready", 1)
        routed, route_args, route_exps = signal("routed", 1), signal("route_args", 1), signal("route_exps", 1)
        assigned, ranked, items_ready = signal("assigned", 1), signal("ranked", 2), signal("items_ready", 1)
        range_zeroed = signal("range_zeroed", 1)
        settled = signal("settled", 0)
        picked, gathered, xT_ready = signal("picked", 2), signal("gathered", 2), signal("xT_ready", 2)
        pick_turned, pickT_ready, v_pick = signal("pick_turned", 1), signal("pickT_ready", 1), signal("v_pick", 3)
        gate_loaded = [[signal(f"gate_loaded{o}{b}", 32) for b in range(2)] for o in range(2)]
        up_loaded = [signal(f"up_loaded{b}", 16) for b in range(2)]
        down_loaded = [signal(f"down_loaded{b}", 32) for b in range(2)]
        gated, upped, gate_exp = signal("gated", 2, 8), signal("upped", 2, 8), signal("gate_exp", 1)
        he_ready, he_turned, heT_ready = signal("he_ready", 1), signal("he_turned", 1), signal("heT_ready", 1)
        downed, y_ready = signal("downed", 2, 8), signal("y_ready", 2)
        scattered, x_added = signal("scattered", 4), signal("x_added", 4, 2)
        VSTEPS, VITEM, GSTEPS = 107, 3, 4
        v_step, v_item = signal("v_step", VSTEPS), signal("v_item", VITEM)
        v_last, g_step = signal("v_last", 0), signal("g_step", GSTEPS)
        gained, last_rstd = signal("gained", 1), signal("last_rstd", 1)
        out_ready, out_stored = [signal(f"out_ready{t}", 1) for t in range(T)], [signal(f"out_stored{t}", 16) for t in range(T)]
        final_loaded = signal("final_loaded", 16)

        w_in_p = w_in.rearrange("l (p c) n -> l p c n", c=DC)
        w_out_p = w_out.rearrange("l (p c) n -> l p c n", c=DC)
        gate_d = w_gate.rearrange("l (q e) (p c) n -> (l q) p e c n", e=2, c=DC)
        up_d = w_up.rearrange("l (q e) (p c) n -> (l q) p e c n", e=2, c=DC)
        down_d = w_down.rearrange("l (q e) (p c) n -> (l q) p e c n", e=2, c=HC)
        BQ, BK, ZA, CQK, CVG, BV = range(6)
        PIECE_BANK = (0, 2, 0, 2, 0, 0)
        PIECE_AFTER = {ZA: BQ + 1, CQK: BK + 1, CVG: ZA + 1, BV: CVG + 1}
        PIECE_COL = {BQ: 2 * A_W, BK: 2 * A_W + B_W, CQK: 2 * A_W + 3 * B_W, ZA: 0, BV: 2 * A_W + 2 * B_W,
                     CVG: 2 * A_W + 3 * B_W + 2 * C_W}

        SPLIT = {ZA: 0, CVG: 1, BV: 2, 6: 3, 7: 4}
        HI_BUFFER = {ZA: 0, CVG: 0, BV: 1, 6: 0, 7: 1}
        HI_AFTER = {CVG: ZA + 1, BV: CQK + 1, 6: CVG + 1, 7: BV + 1}

        def part_of(k):
            t, b = k // 2, k % 2
            return slice(None), slice(4 * b, 4 * b + 4), slice(t * P, (t + 1) * P)

        block = ctx.enter_context(nc.Block())

        @block.sync
        def _(sp):
            sp.dma_start(x[:], x_in.rearrange("b (t p) d -> p (b t) d", p=P)).then_inc(x_loaded.sem, 16)
            sp.wait_ge(range_zeroed.sem, 1)
            with sp.Fori(0, DEPTH) as l:
                first = sp.value_load(items[0:1, 1:2], min_val=0, max_val=4 * PAIRS * DEPTH)

                def load_piece(j, src):
                    s = j % 2
                    if j < 2:
                        sp.wait_ge(downed.sem, downed.at(first, 0))
                    else:
                        sp.wait_ge(projected.sem, projected.at(l, j - 1))
                    settle(sp)
                    sp.dma_start(piece[s], src).then_inc(piece_loaded[s].sem, 16)

                def load_halves(dst, src, loaded, used, g, q, back=0, halves=(0, 1), experts=(0, 1)):
                    for b in halves:
                        if used is not None:
                            sp.wait_ge(used.sem, used.at(g, b + 1 - back * used.turn))
                            settle(sp)
                        if dst is up_w:
                            sp.dma_start(dst[:, :, 4 * b:4 * b + 4, :], src[bass.ds(q, 1), :, :, 4 * b:4 * b + 4, :]
                                         .rearrange("q p e c n -> (q p) e c n")).then_inc(loaded[b].sem, 16)
                            continue
                        if dst is down_w:
                            part = slice(None), slice(b * COLS, (b + 1) * COLS)
                        else:
                            part = slice(4 * b, 4 * b + 4), slice(None)
                        for e in experts:
                            sp.dma_start(dst[:, e, part[0], part[1]], src[bass.ds(q, 1), :, e, part[0], part[1]]
                                         .rearrange("q p c n -> (q p) c n")).then_inc(loaded[b].sem, 16)

                for j in range(6):
                    load_piece(j, w_in_p[bass.ds(l, 1), :, :, PIECE_COL[j]:PIECE_COL[j] + COLS]
                               .rearrange("l p c n -> (l p) c n"))
                    if j == 4:
                        load_halves(up_w, up_d, up_loaded, upped, first, l * PAIRS, 1)
                for n in range(2):
                    load_piece(6 + n, w_out_p[bass.ds(l, 1), :, :, n * COLS:(n + 1) * COLS]
                               .rearrange("l p c n -> (l p) c n"))
                sp.wait_ge(attended.sem, attended.at(l, 2))
                settle(sp)
                load_halves(gate_w[0], gate_d, gate_loaded[0], None, None, l * PAIRS)
                for n in range(2):
                    sp.wait_ge(out_done.sem, out_done.at(l, (n + 1) * T))
                    settle(sp)
                    load_halves(down_w, down_d, down_loaded, None, None, l * PAIRS, experts=(n,))
                    load_halves(gate_w[1], gate_d, gate_loaded[1], None, None, l * PAIRS + 1, experts=(1 - n,))
                sp.wait_ge(items_ready.sem, items_ready.at(l, 1))
                settle(sp)
                last = sp.value_load(items[0:1, 1:2], min_val=PAIRS, max_val=4 * PAIRS * DEPTH)

                def pair(g):
                    return sp.snap((g & (PAIRS - 1)) + l * PAIRS)

                def load_next(g, q, back=0):
                    load_halves(up_w, up_d, up_loaded, upped, g, q, back)
                    load_halves(down_w, down_d, down_loaded, downed, g, q, back)

                def load_gate(g, o, q, halves, back=0):
                    load_halves(gate_w[o], gate_d, gate_loaded[o], gated, g, q, back, halves)

                load_gate(first, 0, pair(first + 2), (0,))
                with sp.Fori(first, last - 4, 2) as g0:
                    for o in range(2):
                        g = g0 + o
                        load_next(g, pair(g + 1))
                        load_gate(g, o, pair(g + 2), (1,))
                        load_gate(g + 1, 1 - o, pair(g + 3), (0,))
                end = l * PAIRS + PAIRS
                load_next(last, end - 3, 4)
                load_gate(last, 0, end - 2, (1,), 4)
                load_next(last, end - 2, 3)
                load_gate(last, 1, end - 1, (0, 1), 3)
                load_next(last, end - 1, 2)
            out_t = out.rearrange("b (t p) d -> p (b t) d", p=P)
            for t in range(T):
                sp.wait_ge(out_ready[t].sem, 1)
                sp.dma_start(out_t[:, t, :], h[:, t, :]).then_inc(out_stored[t].sem, 16)
            for t in range(T):
                sp.wait_ge(out_stored[t].sem, 16)

        @block.gpsimd
        def _(pool):
            def load_mix_params(l):
                row = lambda a: a[bass.ds(l, 1), :]
                pool.dma_start(gain1[:], norm1[bass.ds(l, 1)].rearrange("l (p c) -> (l p) c", c=DC)).then_inc(gain1_loaded.sem, 16)
                pool.dma_start(ws[:], a_ws[bass.ds(l, 1)].rearrange("l g t s -> (l t) g s")).then_inc(ws_loaded.sem, 16)
                for dst, src in [
                        (bs[:], a_bs[bass.ds(l, 1)].rearrange("l g t -> (l t) g")),
                        (ln_g[:], row(a_ln_g).to_broadcast([P, A_W])),
                        (ln_b[:], row(a_ln_b).to_broadcast([P, A_W])),
                        (gn_g[:], row(ret_gn).to_broadcast([P, C_W]))]:
                    pool.dma_start(dst, src).then_inc(mix_params_loaded.sem, 16)

            load_mix_params(0)
            with pool.Fori(0, DEPTH) as l:
                step = [0]

                def link(ins):
                    step[0] += 1
                    ins.then_inc(g_step.sem, 1)
                    pool.wait_ge(g_step.sem, g_step.at(l, step[0]))

                pool.wait_ge(summed.sem, summed.at(l, 1))
                row = lambda a: a[bass.ds(l, 1), :]
                for dst, src in [
                        (gain2[:], norm2[bass.ds(l, 1)].rearrange("l (p c) -> (l p) c", c=DC)),
                        (rw[:, :, 0:GROUPS], router_g[bass.ds(l, 1)].rearrange("l (p c) n -> (l p) c n", c=DC)),
                        (rw[:, :, GROUPS:ROUTE], router_e[bass.ds(l, 1)].rearrange("l (p c) n -> (l p) c n", c=DC)),
                        (rb[:, 0:GROUPS], row(router_gb).to_broadcast([P, GROUPS])),
                        (rb[:, GROUPS:ROUTE], row(router_eb).to_broadcast([P, EXPERTS]))]:
                    pool.dma_start(dst, src).then_inc(route_params_loaded.sem, 16)
                pool.wait_ge(route_params_loaded.sem, route_params_loaded.at(l, route_params_loaded.turn))
                pool.tensor_tensor(rw[:], rw[:], gain2[:].unsqueeze(2).to_broadcast([P, DC, ROUTE]), ALU.mult).then_inc(rw_scaled.sem, 1)

                zf = za.rearrange("p t n -> p (t n)")
                pool.wait_ge(proj_copied_a.sem, proj_copied_a.at(l, ZA + 1))
                pool.wait_ge(proj_copied_d.sem, proj_copied_d.at(l, ZA + 1))
                link(pool.tensor_tensor(work0[:], zf, zf, ALU.mult))
                settle(pool)
                link(pool.tensor_scalar(work0[:], work0[:], 0.044715, 1.0, ALU.mult, ALU.add))
                pool.tensor_tensor(work0[:], work0[:], zf, ALU.mult).then_inc(gelu_arg.sem, 1)
                pool.wait_ge(gelu_rec.sem, gelu_rec.at(l, 1))
                pool.tensor_tensor(zf, zf, work1[:], ALU.mult).then_inc(gelu_done.sem, 1)
                pool.wait_ge(proj_copied_a.sem, proj_copied_a.at(l, CQK + 1))
                pool.wait_ge(proj_copied_d.sem, proj_copied_d.at(l, CQK + 1))
                pool.wait_ge(const_loaded.sem, 16)
                pool.tensor_tensor(rot[:], qkc[:], C("cos").unsqueeze(1).to_broadcast([P, 4, SEQ]), ALU.mult).then_inc(cos_done.sem, 1)
                pool.wait_ge(ln_scaled.sem, ln_scaled.at(l, 1))
                pool.wait_ge(mix_params_loaded.sem, mix_params_loaded.at(l, mix_params_loaded.turn))
                v = za[:, :, A_W:2 * A_W]
                link(pool.tensor_tensor(v, v, ln_g[:].unsqueeze(1).to_broadcast([P, T, A_W]), ALU.mult))
                pool.tensor_tensor(v, v, ln_b[:].unsqueeze(1).to_broadcast([P, T, A_W]), ALU.add).then_inc(vn_ready.sem, 1)
                pool.wait_ge(silu_rec.sem, silu_rec.at(l, 1))
                w2 = work2.rearrange("p (t n) -> p t n", t=T)
                link(pool.tensor_tensor(sgate[:], vgc[:, :, C_W:2 * C_W], w2, ALU.mult))
                pool.tensor_tensor(sgate[:], sgate[:], gn_g[:].unsqueeze(1).to_broadcast([P, T, C_W]), ALU.mult).then_inc(sgate_ready.sem, 1)
                for b in range(2):
                    part = slice(None), slice(4 * b, 4 * b + 4)
                    pool.wait_ge(piece_hi_ready.sem, piece_hi_ready.at(l, 2 * SPLIT[6] + b + 1))
                    pool.tensor_tensor(piece_lo[0][part], piece[0][part], piece_hi[HI_BUFFER[6]][part].bitcast(F32),
                                       ALU.subtract).then_inc(piece6_split.sem, 1)
                pool.wait_ge(turned.sem, turned.at(l, 8))
                pool.wait_ge(rstd_ready.sem, rstd_ready.at(l, 1))
                settle(pool)
                for t in range(T):
                    ins = pool.tensor_scalar(h[:, t, :], x[:, t, :], rstd[:, t:t + 1], None, ALU.mult)
                ins.then_inc(tokens_ready.sem, 1)
                load_mix_params(pool.snap((l + 1) & (DEPTH - 1)))
                assert step[0] == GSTEPS, ("GSTEPS", step[0])
            pool.wait_ge(mix_params_loaded.sem, 16 * 4 * (DEPTH + 1))
            pool.wait_ge(gain1_loaded.sem, 16 * (DEPTH + 1))
            pool.wait_ge(ws_loaded.sem, 16 * (DEPTH + 1))
            pool.dma_start(za.rearrange("p t n -> p (t n)"),
                           final_norm.rearrange("(a n) -> a n", a=1).to_broadcast([P, D])).then_inc(final_loaded.sem, 16)
            pool.wait_ge(final_loaded.sem, 16)
            pool.wait_ge(summed.sem, DEPTH + 1)
            pool.tensor_tensor(work1[:], x[:, 0, :], za.rearrange("p t n -> p (t n)"), ALU.mult).then_inc(gained.sem, 1)

        @block.scalar
        def _(act):
            act.dma_start(const[:, 0:CONST_FIRST], table[:, 0:CONST_FIRST]).then_inc(ident_loaded.sem, 16)

            def square(t, dst):
                act.activation(dst[:], x[:, t, :], ACT.Square, accum_out=sumsq[:, t:t + 1]).then_inc(squared.sem, 1)

            act.wait_ge(x_loaded.sem, 16)
            square(0, work0)
            act.wait_ge(piece_loaded[0].sem, 16)
            act.dma_start(const[:, CONST_FIRST:], table[:, CONST_FIRST:]).then_inc(const_loaded.sem, 16)
            with act.Fori(0, DEPTH) as l:
                def copy_turned(bank, count):
                    t, b = bank // 2, bank % 2
                    act.wait_ge(turned.sem, turned.at(l, count))
                    act.activation(hT[:, 4 * b:4 * b + 4, t * P:(t + 1) * P], psum[:, 4 + bank, :].rearrange("p (c t) -> p c t", c=4),
                                   ACT.Copy).then_inc(turn_copied_a.sem, 1)

                def split_hi(j):
                    act.wait_ge(piece_loaded[j % 2].sem, piece_loaded[j % 2].at(l, 16 * (j // 2 + 1)))
                    if j in HI_AFTER:
                        act.wait_ge(projected.sem, projected.at(l, HI_AFTER[j]))
                    for b in range(2):
                        act.activation(piece_hi[HI_BUFFER[j]][:, 4 * b:4 * b + 4, :], piece[j % 2][:, 4 * b:4 * b + 4, :],
                                       ACT.Copy).then_inc(piece_hi_ready.sem, 1)

                def copy_piece(j, dst):
                    act.wait_ge(projected.sem, projected.at(l, j + 1))
                    act.activation(dst, psum[:, PIECE_BANK[j], :], ACT.Copy).then_inc(proj_copied_a.sem, 1)

                def exps(k):
                    act.wait_ge(masked.sem, masked.at(l, k + 1))
                    for j in range(4):
                        act.activation(scores[:, j, 0:P], scores[:, j, 0:P], ACT.Exp, bias=nmax[:, k, j:j + 1],
                                       accum_out=denom[:, k, j:j + 1])
                        ins = act.activation(scores[:, j, P:3 * P], scores[:, j, P:3 * P], ACT.Exp,
                                             bias=nmax[:, k, 4 + j:5 + j], accum_out=denom[:, k, 4 + j:5 + j])
                    ins.then_inc(exped.sem, 1)

                def copy_probs(k):
                    act.wait_ge(probs_turned.sem, probs_turned.at(l, k + 1))
                    for b in (0, 2):
                        ins = act.activation(probsT[:, k, b].rearrange("p j t -> p (j t)"), psum[:, 4 + b, :], ACT.Copy)
                    ins.then_inc(probs_copied_a.sem, 1)

                act.wait_ge(turn_copied_d.sem, turn_copied_d.at(l, DC))
                act.activation(hT_parts[0][:], hT[:], ACT.Copy).then_inc(hT_hi_ready.sem, 1)
                copy_piece(BQ, qkb[:, 0:2, :].rearrange("p c t -> p (c t)"))
                split_hi(ZA)
                copy_piece(BK, qkb[:, 4:6, :].rearrange("p c t -> p (c t)"))
                exps(0)
                copy_piece(ZA, za[:, 0, :])
                copy_probs(0)
                act.wait_ge(gelu_arg.sem, gelu_arg.at(l, 1))
                act.activation(work1[:], work0[:], ACT.Exp, scale=-2.0 * float(np.sqrt(2.0 / np.pi))).then_inc(gelu_exp.sem, 1)
                split_hi(CVG)
                copy_piece(CQK, qkc[:, 0:2, :].rearrange("p c t -> p (c t)"))
                exps(1)
                split_hi(BV)
                copy_piece(CVG, vgc[:, 0, :])
                copy_probs(1)
                act.wait_ge(proj_copied_d.sem, proj_copied_d.at(l, CVG + 1))
                act.wait_ge(proj_copied_a.sem, proj_copied_a.at(l, CVG + 1))
                act.activation(work2.rearrange("p (t n) -> p t n", t=T), vgc[:, :, C_W:2 * C_W], ACT.Exp, scale=-1.0).then_inc(silu_exp.sem, 1)
                split_hi(6)
                copy_piece(BV, vb[:, 0, :])
                act.activation(vb[:, 1, :], psum[:, PIECE_BANK[BV] + 1, :], ACT.Copy).then_inc(proj_copied_a.sem, 1)
                for k in range(4):
                    act.wait_ge(turned.sem, turned.at(l, 5 + k))
                    act.activation(hT_parts[0][part_of(k)], psum[:, 4 + k, :].rearrange("p (c t) -> p c t", c=4),
                                   ACT.Copy).then_inc(hT_hi_ready.sem, 1)
                split_hi(7)
                for t in range(T):
                    act.wait_ge(x_mixed.sem, x_mixed.at(l, t + 1))
                    square(t, (work0, work1)[t])
                    copy_turned(2 * t, 9 + 2 * t)
                    copy_turned(2 * t + 1, 10 + 2 * t)
                act.wait_ge(route_args.sem, route_args.at(l, 1))
                act.activation(r["gexp"][:], r["gsh"][:], ACT.Exp)
                act.activation(r["e"][:], r["d"][:], ACT.Exp).then_inc(route_exps.sem, 1)

                def copy_pick(n, o):
                    act.wait_ge(pick_turned.sem, pick_turned.at(n, 1))
                    act.activation(pickT[:, o].rearrange("p t n -> p (t n)"), psum[:, 6, 0:SEQ], ACT.Copy).then_inc(pickT_ready.sem, 1)

                act.wait_ge(items_ready.sem, items_ready.at(l, 1))
                settle(act)
                first = act.value_load(items[0:1, 0:1], min_val=0, max_val=4 * PAIRS * DEPTH)
                last = act.value_load(items[0:1, 1:2], min_val=PAIRS, max_val=4 * PAIRS * DEPTH)
                copy_pick(first + l, 0)

                def item(g, o):
                    act.wait_ge(gated.sem, gated.at(g, 2))
                    act.activation(sig, psum[:, 0, :], ACT.Exp, scale=-1.0).then_inc(gate_exp.sem, 1)
                    act.wait_ge(he_turned.sem, he_turned.at(g, 1))
                    act.activation(heT.rearrange("p c n -> p (c n)"), psum[:, 0, :], ACT.Copy).then_inc(heT_ready.sem, 1)
                    copy_pick(g + l + 1, 1 - o)
                    for n in range(2):
                        act.wait_ge(downed.sem, downed.at(g, n + 1))
                        act.activation(y[:, n * COLS:(n + 1) * COLS], psum[:, 2 + n, :], ACT.Copy).then_inc(y_ready.sem, 1)

                with act.Fori(first, last, 2) as g0:
                    for o in range(2):
                        item(act.snap(g0 + o), o)
                act.wait_ge(x_added.sem, x_added.at(last, -1))
                square(0, work0)
            act.wait_ge(gained.sem, 1)
            act.wait_ge(last_rstd.sem, 1)
            act.activation(h[:, 0, :], work1[:], ACT.Copy, scale=rstd[:, 0:1]).then_inc(out_ready[0].sem, 1)

        @block.tensor
        def _(pe):
            for used in (gated, upped, downed):
                for _ in range(used.start):
                    pe.nop().then_inc(used.sem, 1)
            ident = C("ident")
            pe.wait_ge(ident_loaded.sem, 16)
            pe.wait_ge(x_loaded.sem, 16)
            pe.wait_ge(range_zeroed.sem, 1)
            with pe.Fori(0, DEPTH) as l:
                prev = pe.value_load(items[0:1, 1:2], min_val=0, max_val=4 * PAIRS * DEPTH)

                def turn(src, t):
                    for b in range(2):
                        for c in range(4 * b, 4 * b + 4):
                            ins = pe.transpose(psum[:, 4 + 2 * t + b, (c % 4) * P:(c % 4 + 1) * P], src[:, t, c::DC], ident)
                        ins.then_inc(turned.sem, 1)

                def keep_warm(n, bank):
                    for _ in range(n):
                        pe.matmul(psum[:, bank, :], ident, x[:, 0, 0:COLS], start=True, stop=True)

                def piece_arrived(j):
                    pe.wait_ge(piece_loaded[j % 2].sem, piece_loaded[j % 2].at(l, 16 * (j // 2 + 1)))

                def three_products(j, o, t, wait=False):
                    w = piece_hi[HI_BUFFER[j]], piece_lo[j % 2]
                    parts = ((0, 0), (1, 0), (0, 1))
                    for c in range(DC):
                        if wait and c % 4 == 0:
                            if j == 6:
                                pe.wait_ge(piece6_split.sem, piece6_split.at(l, c // 4 + 1))
                            else:
                                pe.wait_ge(piece_split.sem, piece_split.at(l, 2 * min(SPLIT[j], 3) + c // 4 + 1))
                        for n, (a, b) in enumerate(parts):
                            ins = pe.matmul(o, hT_parts[a][:, c, t * P:(t + 1) * P], w[b][:, c, :], start=(c == 0 and n == 0),
                                            stop=(c == DC - 1 and n == len(parts) - 1))
                    return ins

                def project(j, between=None):
                    w, bank = piece[j % 2], PIECE_BANK[j]
                    piece_arrived(j)
                    if j in PIECE_AFTER:
                        pe.wait_ge(proj_copied_a.sem, proj_copied_a.at(l, PIECE_AFTER[j]))
                        pe.wait_ge(proj_copied_d.sem, proj_copied_d.at(l, PIECE_AFTER[j]))
                    if j in (BQ, BK, CQK):
                        for m in range(4):
                            o = psum[:, bank + m // 2, (m % 2) * SEQ:(m % 2 + 1) * SEQ]
                            for c in range(DC):
                                if j == BQ and m == 0:
                                    pe.wait_ge(turn_copied_d.sem, turn_copied_d.at(l, c + 1))
                                ins = pe.matmul(o, w[:, c, m * P:(m + 1) * P], hT[:, c, :], start=(c == 0), stop=(c == DC - 1))
                            if m == 3:
                                ins.then_inc(projected.sem, 1)
                    else:
                        pe.wait_ge(hT_split.sem, hT_split.at(l, 1))
                        for t in range(T):
                            if t == 1 and between is not None:
                                between()
                            ins = three_products(j, psum[:, bank + t, :], t, wait=(t == 0))
                        ins.then_inc(projected.sem, 1)

                def score(k):
                    pe.wait_ge(proj_copied_a.sem, proj_copied_a.at(l, BK + 1))
                    pe.wait_ge(proj_copied_d.sem, proj_copied_d.at(l, BK + 1))
                    if k == 1:
                        pe.wait_ge(probs_copied_a.sem, probs_copied_a.at(l, 1))
                        pe.wait_ge(probs_copied_d.sem, probs_copied_d.at(l, 1))
                    rows = slice(HD * k, HD * (k + 1))
                    for j in range(4):
                        q, kk = qkb[rows, j, :], qkb[rows, 4 + j, :]
                        pe.matmul(psum[:, 4, j * P:(j + 1) * P], q[:, 0:P], kk[:, 0:P], start=True, stop=True)
                        ins = pe.matmul(psum[:, 5 + j // 2, (j % 2) * SEQ:(j % 2 + 1) * SEQ], q[:, P:SEQ], kk,
                                        start=True, stop=True)
                    ins.then_inc(scored.sem, 1)

                def turn_probs(k):
                    pe.wait_ge(exped.sem, exped.at(l, k + 1))
                    for b in range(3):
                        for j in range(4):
                            ins = pe.transpose(psum[:, 4 + b, j * P:(j + 1) * P], scores[:, j, b * P:(b + 1) * P], ident)
                    ins.then_inc(probs_turned.sem, 1)

                def attend(k, bank):
                    pe.wait_ge(probs_copied_a.sem, probs_copied_a.at(l, k + 1))
                    pe.wait_ge(probs_copied_d.sem, probs_copied_d.at(l, k + 1))
                    for j in range(4):
                        cols = slice((2 * j + k) * HD, (2 * j + k + 1) * HD)
                        pe.matmul(psum[:, bank, j * HD:(j + 1) * HD], probsT[:, k, 0, j], vb[:, 0, cols], start=True, stop=True)
                        o = psum[:, bank, (4 + j) * HD:(5 + j) * HD]
                        pe.matmul(o, probsT[:, k, 1, j], vb[:, 0, cols], start=True, stop=False)
                        ins = pe.matmul(o, probsT[:, k, 2, j], vb[:, 1, cols], start=False, stop=True)
                    ins.then_inc(attended.sem, 1)

                def retain():
                    pe.wait_ge(decayed.sem, decayed.at(l, 1))
                    for j in range(4):
                        v = slice(j * HD, (j + 1) * HD)
                        pe.matmul(psum[:, 2, j * HD:(j + 1) * HD], scores[:, j, 0:P], vgc[:, 0, v], start=True, stop=True)
                        o = psum[:, 2, (4 + j) * HD:(5 + j) * HD]
                        pe.matmul(o, scores[:, j, P:2 * P], vgc[:, 0, v], start=True, stop=False)
                        ins = pe.matmul(o, scores[:, j, 2 * P:3 * P], vgc[:, 1, v], start=False, stop=True)
                    ins.then_inc(retained.sem, 1)

                for t in range(T):
                    pe.wait_ge(x_added.sem, x_added.at(prev, t - 1))
                    turn(x, t)
                pe.wait_ge(spread_ready.sem, spread_ready.at(l, 1))
                pe.matmul(psum[:, 3, 0:SEQ], C("ones"), spread, start=True, stop=True).then_inc(rstd_spread.sem, 1)
                project(BQ)
                pe.wait_ge(const_loaded.sem, 16)
                pe.wait_ge(ws_loaded.sem, ws_loaded.at(l, 16))
                for g in range(4):
                    ins = pe.transpose(psum[:, 7, g * P:(g + 1) * P], ws[:, g, :], ident)
                ins.then_inc(ws_turned.sem, 1)
                project(BK)
                score(0)
                project(ZA)
                turn_probs(0)
                project(CQK)
                score(1)
                pe.wait_ge(proj_copied_a.sem, proj_copied_a.at(l, CQK + 1))
                pe.wait_ge(proj_copied_d.sem, proj_copied_d.at(l, CQK + 1))
                for n in range(2):
                    ins = pe.matmul(psum[:, 2 + n, :], C("swap"), qkc[:, 2 * n:2 * n + 2, :].rearrange("p c t -> p (c t)"),
                                    start=True, stop=True)
                ins.then_inc(swapped.sem, 1)
                project(CVG)
                turn_probs(1)
                pe.wait_ge(ws_masked.sem, ws_masked.at(l, 1))
                pe.wait_ge(rotated.sem, rotated.at(l, 1))
                for c in range(2):
                    if c == 1:
                        pe.wait_ge(probs_copied_a.sem, probs_copied_a.at(l, 2))
                    for tile in range(2):
                        for j in range(2):
                            rows = slice(HD * j, HD * (j + 1))
                            q, kk = rot[rows, c, :], rot[rows, 2 + c, :]
                            bank = (2, 3, 6, 7)[2 * c + j]
                            ins = pe.matmul(psum[:, bank, 0:SEQ] if tile == 0 else psum[:, bank, SEQ:SEQ + P],
                                            kk[:, tile * P:(tile + 1) * P], q[:, tile * P:], start=True, stop=True)
                ins.then_inc(inner_ready.sem, 1)
                project(BV, retain)
                pe.wait_ge(vn_ready.sem, vn_ready.at(l, 1))
                for t in range(T):
                    for g in range(4):
                        ins = pe.matmul(psum[:, 3, t * A_W + g * HD:t * A_W + (g + 1) * HD], wsT[:, g, :],
                                        za[:, t, A_W + g * HD:A_W + (g + 1) * HD], start=True, stop=True)
                ins.then_inc(spatial_done.sem, 1)
                pe.wait_ge(proj_copied_a.sem, proj_copied_a.at(l, BV + 2))
                attend(0, 4)
                attend(1, 5)
                pe.wait_ge(attn_stored.sem, attn_stored.at(l, 2))
                for t in range(T):
                    turn(h, t)
                for n in range(2):
                    for t in range(T):
                        pe.wait_ge(turn_copied_d.sem, turn_copied_d.at(l, DC + 2 * t + 2))
                        three_products(6 + n, psum[:, 2 * t + n, :], t, wait=(t == 0)).then_inc(out_done.sem, 1)
                for t in range(T):
                    pe.wait_ge(x_mixed.sem, x_mixed.at(l, t + 1))
                    turn(x, t)
                pe.wait_ge(rw_scaled.sem, rw_scaled.at(l, 1))
                for t in range(T):
                    pe.wait_ge(turn_copied_a.sem, turn_copied_a.at(l, 2 + 2 * t))
                    for c in range(DC):
                        ins = pe.matmul(psum[:, 0, t * ROUTE:(t + 1) * ROUTE], hT[:, c, t * P:(t + 1) * P], rw[:, c, :],
                                        start=(c == 0), stop=(c == DC - 1))
                ins.then_inc(routed.sem, 1)
                keep_warm(3, 3)
                pe.wait_ge(assigned.sem, assigned.at(l, 1))
                asg = r["assign"]
                pe.matmul(psum[:, 1, 0:32], C("before"), asg[:].rearrange("p t e -> p (t e)"), start=True, stop=False)
                pe.matmul(psum[:, 1, 16:32], C("ones"), asg[:, 0, :], start=False, stop=True).then_inc(ranked.sem, 1)
                pe.matmul(psum[:, 2, 0:EXPERTS], C("ones"), asg[:, 0, :], start=True, stop=False)
                pe.matmul(psum[:, 2, 0:EXPERTS], C("ones"), asg[:, 1, :], start=False, stop=True).then_inc(ranked.sem, 1)
                pe.wait_ge(tokens_ready.sem, tokens_ready.at(l, 1))

                def gather(n, o, b):
                    for c in range(4 * b, 4 * b + 4):
                        for t in range(T):
                            ins = pe.matmul(psum[:, 4 + b, (c % 4) * P:(c % 4 + 1) * P], h[:, t, c::DC],
                                            pick[:, o, t].rearrange("p e s -> p (e s)"), start=(t == 0), stop=(t == T - 1))
                    ins.then_inc(gathered.sem, 1)

                def turn_pick(n, o):
                    pe.wait_ge(picked.sem, picked.at(n, 2))
                    for t in range(T):
                        ins = pe.transpose(psum[:, 6, t * P:(t + 1) * P], pickw[:, o, t].rearrange("p e s -> p (e s)"), ident)
                    ins.then_inc(pick_turned.sem, 1)

                def item(g, u, o):
                    for bank, w, loaded, turn_of, done in ((0, gate_w[o], gate_loaded[o], u, gated), (1, up_w, up_loaded, g, upped)):
                        for c in range(DC):
                            if c % 4 == 0:
                                if bank == 0:
                                    pe.wait_ge(xT_ready.sem, xT_ready.at(g + l, c // 4 + 1))
                                pe.wait_ge(loaded[c // 4].sem, loaded[c // 4].at(turn_of, loaded[0].turn))
                            for e in range(2):
                                ins = pe.matmul(psum[e * SLOTS:(e + 1) * SLOTS, bank, :], xT[:, o, c, e * SLOTS:(e + 1) * SLOTS],
                                                w[:, e, c, :], start=(c == 0), stop=(c == DC - 1))
                            if c % 4 == 3:
                                ins.then_inc(done.sem, 1)
                    n = g + l + 1
                    pe.wait_ge(picked.sem, picked.at(n, 1))
                    gather(n, 1 - o, 0)
                    pe.wait_ge(he_ready.sem, he_ready.at(g, 1))
                    for c in range(HC):
                        ins = pe.transpose(psum[:, 0, c * P:(c + 1) * P], he[:, c::HC], ident)
                    ins.then_inc(he_turned.sem, 1)
                    gather(n, 1 - o, 1)
                    pe.wait_ge(x_added.sem, x_added.at(g, 0))
                    turn_pick(n, 1 - o)
                    pe.wait_ge(heT_ready.sem, heT_ready.at(g, 1))
                    for n2 in range(2):
                        pe.wait_ge(down_loaded[n2].sem, down_loaded[n2].at(g, 32))
                        for c in range(HC):
                            for e in range(2):
                                ins = pe.matmul(psum[e * SLOTS:(e + 1) * SLOTS, 2 + n2, :], heT[:, c, e * SLOTS:(e + 1) * SLOTS],
                                                down_w[:, e, c, n2 * COLS:(n2 + 1) * COLS], start=(c == 0), stop=(c == HC - 1))
                        ins.then_inc(downed.sem, 1)
                    pe.wait_ge(pickT_ready.sem, pickT_ready.at(n, 1))
                    for n2 in range(2):
                        pe.wait_ge(y_ready.sem, y_ready.at(g, n2 + 1))
                        for t in range(T):
                            pe.wait_ge(x_added.sem, x_added.at(g, 2 * n2 + t - 1))
                            pe.matmul(psum[:, 6 + t, :], pickT[:, o, t, :], y[:, n2 * COLS:(n2 + 1) * COLS],
                                      start=True, stop=True).then_inc(scattered.sem, 1)

                pe.wait_ge(picked.sem, picked.at(prev + l, 1))
                gather(None, 0, 0)
                gather(None, 0, 1)
                pe.wait_ge(items_ready.sem, items_ready.at(l, 1))
                settle(pe)
                last = pe.value_load(items[0:1, 1:2], min_val=PAIRS, max_val=4 * PAIRS * DEPTH)
                turn_pick(prev + l, 0)
                with pe.Fori(prev, last, 2) as g0:
                    u = pe.snap(g0 >> 1)
                    item(g0, u, 0)
                    item(pe.snap(g0 + 1), u, 1)

        @block.vector
        def _(dve):
            V = nc.vector

            def inverse_roots(m, link):
                link(V.tensor_scalar(half_bits[:, 0:m], meansq[:, 0:m].bitcast(I32), 1, None, ALU.logical_shift_right))
                link(V.tensor_scalar(guess_bits[:, 0:m], half_bits[:, 0:m], -1.0, ROOT_MAGIC, ALU.mult, ALU.add))
                y0 = guess_bits[:, 0:m].bitcast(F32)
                for n in range(3):
                    link(V.scalar_tensor_tensor(newton[:, 0:m], y0, -0.5, meansq[:, 0:m], ALU.mult, ALU.mult))
                    link(V.tensor_tensor(newton[:, 0:m], newton[:, 0:m], y0, ALU.mult))
                    ins = V.scalar_tensor_tensor(rstd[:, 0:m], newton[:, 0:m], 1.5, y0, ALU.add, ALU.mult)
                    if n < 2:
                        link(ins)
                    y0 = rstd[:, 0:m]
                return ins


            V.memset(last_f[:], 0.0).then_inc(v_item.sem, 1)
            V.memset(items[:], 0).then_inc(range_zeroed.sem, 1)
            for k in range(x_added.start):
                V.memset(more[:, k:k + 1], 0.0).then_inc(x_added.sem, 1)

            def square():
                V.tensor_tensor_reduce(out=h[:, 1, :], in0=x[:, 1, :], in1=x[:, 1, :], scale=1.0, scalar=0.0,
                                       op0=ALU.mult, op1=ALU.add, accum_out=sumsq[:, 1:2]).then_inc(summed.sem, 1)

            dve.wait_ge(x_loaded.sem, 16)
            square()
            dve.wait_ge(ident_loaded.sem, 16)
            dve.wait_ge(range_zeroed.sem, 1)
            with dve.Fori(0, DEPTH) as l:
                step = [0]

                def link(ins):
                    step[0] += 1
                    ins.then_inc(v_step.sem, 1)
                    dve.wait_ge(v_step.sem, v_step.at(l, step[0]))

                def split_lo(j, b):
                    part = slice(None), slice(4 * b, 4 * b + 4)
                    dve.wait_ge(piece_hi_ready.sem, piece_hi_ready.at(l, 2 * SPLIT[j] + b + 1))
                    V.tensor_tensor(piece_lo[j % 2][part], piece[j % 2][part], piece_hi[HI_BUFFER[j]][part].bitcast(F32),
                                    ALU.subtract).then_inc(piece_split.sem, 1)

                def copy_piece(j, dst):
                    dve.wait_ge(projected.sem, projected.at(l, j + 1))
                    V.tensor_copy(dst, psum[:, PIECE_BANK[j] + 1, :]).then_inc(proj_copied_d.sem, 1)

                def mask(k):
                    dve.wait_ge(scored.sem, scored.at(l, k + 1))
                    logc = C("logc")
                    if k == 1:
                        dve.wait_ge(probs_turned.sem, probs_turned.at(l, 1))
                    link(V.scalar_tensor_tensor(scores[:, :, 0:P], psum[:, 4, :].rearrange("p (j s) -> p j s", j=4), HD ** -0.5,
                                                logc[:, 0:P].unsqueeze(1).to_broadcast([P, 4, P]), ALU.mult, ALU.add))
                    for b in range(2):
                        link(V.scalar_tensor_tensor(scores[:, 2 * b:2 * b + 2, P:3 * P],
                                                    psum[:, 5 + b, :].rearrange("p (j s) -> p j s", j=2), HD ** -0.5,
                                                    logc[:, P:3 * P].unsqueeze(1).to_broadcast([P, 2, SEQ]), ALU.mult, ALU.add))
                    link(V.tensor_reduce(nmax[:, k, 0:4], scores[:, :, 0:P], AX.X, ALU.max, negate=True))
                    V.tensor_reduce(nmax[:, k, 4:8], scores[:, :, P:3 * P], AX.X, ALU.max, negate=True).then_inc(masked.sem, 1)

                def copy_probs(k):
                    dve.wait_ge(probs_turned.sem, probs_turned.at(l, k + 1))
                    V.tensor_copy(probsT[:, k, 1].rearrange("p j t -> p (j t)"), psum[:, 5, :]).then_inc(probs_copied_d.sem, 1)

                def store_attention(k, bank):
                    link(V.reciprocal(rdenom[:, k, :], denom[:, k, :]))
                    dve.wait_ge(attended.sem, attended.at(l, k + 1))
                    dst = h[:, :, A_W:A_W + B_W].rearrange("p t (j e d) -> p t j e d", e=2, d=HD)[:, :, :, k, :]
                    V.tensor_tensor(dst, psum[:, bank, :].rearrange("p (t j d) -> p t j d", t=T, j=4),
                                    rdenom[:, k, :].rearrange("p (t j) -> p t j", t=T).unsqueeze(3).to_broadcast([P, T, 4, HD]),
                                    ALU.mult).then_inc(attn_stored.sem, 1)

                def pick_next(n, col, o, between=None):
                    def plink(k, ins):
                        ins.then_inc(v_pick.sem, 1)
                        dve.wait_ge(v_pick.sem, v_pick.at(n, k))

                    cols = slice(0, 2) if isinstance(col, int) else bass.ds(col, 2)
                    for t in range(T):
                        ins = V.tensor_tensor(pick[:, o, t], C("slot").unsqueeze(1).to_broadcast([P, 2, SLOTS]),
                                              r["rank"][:, t, cols].unsqueeze(2).to_broadcast([P, 2, SLOTS]), ALU.is_equal)
                        if t == 0:
                            plink(1, ins)
                    ins.then_inc(picked.sem, 1)
                    dve.wait_ge(picked.sem, picked.at(n, 1))
                    if between is not None:
                        between()
                    for t in range(T):
                        ins = V.tensor_tensor(pickw[:, o, t], pick[:, o, t],
                                              r["cw"][:, t, cols].unsqueeze(2).to_broadcast([P, 2, SLOTS]), ALU.mult)
                        if t == 0:
                            plink(2, ins)
                    ins.then_inc(picked.sem, 1)
                    rk = r["rank"][:, :, cols]
                    plink(3, V.tensor_scalar(rk, rk, -float(SLOTS), None, ALU.add))

                def copy_tokens(n, o):
                    for b in range(2):
                        dve.wait_ge(gathered.sem, gathered.at(n, b + 1))
                        V.tensor_tensor(xT[:, o, 4 * b:4 * b + 4, :], psum[:, 4 + b, :].rearrange("p (c s) -> p c s", c=4),
                                        gain2[:, 4 * b:4 * b + 4].unsqueeze(2).to_broadcast([P, 4, P]), ALU.mult).then_inc(xT_ready.sem, 1)

                dve.wait_ge(squared.sem, squared.at(l, 1))
                dve.wait_ge(summed.sem, summed.at(l, 1))
                link(V.tensor_scalar(meansq[:, 0:T], sumsq[:], 1.0 / D, EPS, ALU.mult, ALU.add))
                link(inverse_roots(T, link))
                V.tensor_tensor(spread.rearrange("p (t q) -> p t q", t=T), C("ident").unsqueeze(1).to_broadcast([P, T, P]),
                                rstd[:, 0:T].unsqueeze(2).to_broadcast([P, T, P]), ALU.mult).then_inc(spread_ready.sem, 1)
                dve.wait_ge(gain1_loaded.sem, gain1_loaded.at(l, 16))
                dve.wait_ge(turned.sem, turned.at(l, 4))
                dve.wait_ge(rstd_spread.sem, rstd_spread.at(l, 1))
                link(V.tensor_copy(rstd_row, psum[:, 3, 0:SEQ]))
                for c in range(DC):
                    for t in range(T):
                        ins = V.scalar_tensor_tensor(hT[:, c, t * P:(t + 1) * P],
                                                     psum[:, 4 + 2 * t + c // 4, (c % 4) * P:(c % 4 + 1) * P], gain1[:, c:c + 1],
                                                     rstd_row[:, t * P:(t + 1) * P], ALU.mult, ALU.mult)
                    ins.then_inc(turn_copied_d.sem, 1)
                prev = dve.value_load(items[0:1, 1:2], min_val=0, max_val=4 * PAIRS * DEPTH)
                dve.wait_ge(const_loaded.sem, 16)
                dve.wait_ge(hT_hi_ready.sem, hT_hi_ready.at(l, 1))
                V.tensor_tensor(hT_parts[1][:], hT[:], hT_parts[0][:].bitcast(F32), ALU.subtract).then_inc(hT_split.sem, 1)
                copy_piece(BQ, qkb[:, 2:4, :].rearrange("p c t -> p (c t)"))
                dve.wait_ge(ws_turned.sem, ws_turned.at(l, 1))
                V.tensor_tensor(wsT[:], psum[:, 7, :].rearrange("p (g t) -> p g t", g=4),
                                C("causal").unsqueeze(1).to_broadcast([P, 4, P]), ALU.mult).then_inc(ws_masked.sem, 1)
                split_lo(ZA, 0)
                copy_piece(BK, qkb[:, 6:8, :].rearrange("p c t -> p (c t)"))
                split_lo(ZA, 1)
                mask(0)
                copy_piece(ZA, za[:, 1, :])
                copy_probs(0)
                dve.wait_ge(gelu_exp.sem, gelu_exp.at(l, 1))
                link(V.tensor_scalar(work1[:], work1[:], 1.0, None, ALU.add))
                V.reciprocal(work1[:], work1[:]).then_inc(gelu_rec.sem, 1)
                split_lo(CVG, 0)
                copy_piece(CQK, qkc[:, 2:4, :].rearrange("p c t -> p (c t)"))
                split_lo(CVG, 1)
                mask(1)
                partner = work1.rearrange("p (c t) -> p c t", c=4)
                dve.wait_ge(gelu_done.sem, gelu_done.at(l, 1))
                dve.wait_ge(swapped.sem, swapped.at(l, 1))
                V.tensor_tensor(partner, psum[:, 2:4, :].rearrange("p b (c t) -> p (b c) t", c=2),
                                C("sin").unsqueeze(1).to_broadcast([P, 4, SEQ]), ALU.mult).then_inc(swap_read.sem, 1)
                dve.wait_ge(swap_read.sem, swap_read.at(l, 1))
                dve.wait_ge(cos_done.sem, cos_done.at(l, 1))
                V.tensor_tensor(rot[:], rot[:], partner, ALU.add).then_inc(rotated.sem, 1)
                for t in range(T):
                    link(V.bn_stats(stats[:, t, :], za[:, t, A_W:2 * A_W]))
                for t in range(T):
                    settle(dve)
                    link(V.bn_aggr(moments[:, t, :], stats[:, t, :]))
                link(V.tensor_scalar(meansq[:, 0:T], moments[:, :, 1], EPS, None, ALU.add))
                link(inverse_roots(T, link))
                for t in range(T):
                    v = za[:, t, A_W:2 * A_W]
                    ins = V.tensor_scalar(v, v, moments[:, t, 0:1], rstd[:, t:t + 1], ALU.subtract, ALU.mult)
                    if t < T - 1:
                        link(ins)
                ins.then_inc(ln_scaled.sem, 1)
                split_lo(BV, 0)
                copy_piece(CVG, vgc[:, 1, :])
                copy_probs(1)
                split_lo(BV, 1)
                dve.wait_ge(inner_ready.sem, inner_ready.at(l, 1))
                dve.wait_ge(probs_turned.sem, probs_turned.at(l, 2))
                dec = C("decay").rearrange("p (j t) -> p j t", j=4)
                for j, bank in ((0, 2), (2, 6)):
                    link(V.tensor_tensor(scores[:, j:j + 2, 0:SEQ], psum[:, bank:bank + 2, 0:SEQ], dec[:, j:j + 2, :], ALU.mult))
                    ins = V.tensor_tensor(scores[:, j:j + 2, SEQ:SEQ + P], psum[:, bank:bank + 2, SEQ:SEQ + P],
                                          dec[:, j:j + 2, 0:P], ALU.mult)
                    if j == 0:
                        link(ins)
                ins.then_inc(decayed.sem, 1)
                dve.wait_ge(silu_exp.sem, silu_exp.at(l, 1))
                link(V.tensor_scalar(work2[:], work2[:], 1.0, None, ALU.add))
                V.reciprocal(work2[:], work2[:]).then_inc(silu_rec.sem, 1)
                dve.wait_ge(retained.sem, retained.at(l, 1))
                o = psum[:, 2, :].rearrange("p (k d) -> p k d", d=HD)
                cen = work1[:, 0:512].rearrange("p (k d) -> p k d", d=HD)
                sq = work1[:, 512:1024].rearrange("p (k d) -> p k d", d=HD)
                link(V.tensor_reduce(gsum[:], o, AX.X, ALU.add))
                link(V.tensor_scalar(gsum[:], gsum[:], 1.0 / HD, None, ALU.mult))
                link(V.tensor_tensor(cen, o, gsum[:].unsqueeze(2).to_broadcast([P, 8, HD]), ALU.subtract))
                link(V.tensor_tensor(sq, cen, cen, ALU.mult))
                link(V.tensor_reduce(gsum[:], sq, AX.X, ALU.add))
                link(V.tensor_scalar(meansq[:], gsum[:], 1.0 / HD, EPS, ALU.mult, ALU.add))
                link(inverse_roots(8, link))
                link(V.tensor_tensor(cen, cen, rstd[:].unsqueeze(2).to_broadcast([P, 8, HD]), ALU.mult))
                dve.wait_ge(sgate_ready.sem, sgate_ready.at(l, 1))
                link(V.tensor_tensor(h[:, :, A_W + B_W:D], work1[:, 0:512].rearrange("p (t n) -> p t n", t=T), sgate[:], ALU.mult))
                dve.wait_ge(spatial_done.sem, spatial_done.at(l, 1))
                w0 = work0[:, 0:T * A_W].rearrange("p (t g d) -> p t g d", t=T, g=4)
                for t in range(T):
                    link(V.tensor_tensor(w0[:, t], psum[:, 3, t * A_W:(t + 1) * A_W].rearrange("p (g d) -> p g d", g=4),
                                         bs[:].unsqueeze(2).to_broadcast([P, 4, HD]), ALU.add))
                link(V.tensor_tensor(h[:, :, 0:A_W], work0[:, 0:T * A_W].rearrange("p (t n) -> p t n", t=T), za[:, :, 0:A_W], ALU.mult))
                for k in range(2):
                    store_attention(k, 4 + k)
                for k in range(4):
                    dve.wait_ge(hT_hi_ready.sem, hT_hi_ready.at(l, 2 + k))
                    V.tensor_tensor(hT_parts[1][part_of(k)], psum[:, 4 + k, :].rearrange("p (c t) -> p c t", c=4),
                                    hT_parts[0][part_of(k)].bitcast(F32), ALU.subtract).then_inc(turn_copied_d.sem, 1)
                split_lo(7, 0)
                split_lo(7, 1)
                for n in range(2):
                    for t in range(T):
                        dve.wait_ge(out_done.sem, out_done.at(l, n * T + t + 1))
                        xs = x[:, t, n * COLS:(n + 1) * COLS]
                        ins = V.tensor_tensor(xs, psum[:, 2 * t + n, :], xs, ALU.add)
                        if n == 0:
                            link(ins)
                        else:
                            ins.then_inc(x_mixed.sem, 1)
                dve.wait_ge(squared.sem, squared.at(l, 1 + T))
                link(V.tensor_scalar(meansq[:, 0:T], sumsq[:], 1.0 / D, EPS, ALU.mult, ALU.add))
                inverse_roots(T, link).then_inc(rstd_ready.sem, 1)
                dve.wait_ge(rstd_ready.sem, rstd_ready.at(l, 1))

                dve.wait_ge(routed.sem, routed.at(l, 1))
                R = {k: t[:] for k, t in r.items()}
                def both(op):
                    op(0)
                    link(op(1))

                both(lambda t: V.scalar_tensor_tensor(r["logit"][:, t, :], psum[:, 0, t * ROUTE:(t + 1) * ROUTE], rstd[:, t:t + 1],
                                                      rb[:], ALU.mult, ALU.add))
                gl = r["logit"][:, :, 0:GROUPS]
                link(V.tensor_reduce(R["gmax"], gl, AX.X, ALU.max))
                V.tensor_tensor(R["gsh"], gl, r["gmax"][:].to_broadcast([P, T, 4]), ALU.subtract)
                both(lambda t: V.scalar_tensor_tensor(r["geq"][:, t, :], r["logit"][:, t, 0:GROUPS], r["gmax"][:, t, :],
                                                      C("prio")[:, 0:GROUPS], ALU.is_equal, ALU.mult))
                link(V.tensor_reduce(R["gp"], R["geq"], AX.X, ALU.max))
                link(V.tensor_tensor(R["goh"], R["geq"], r["gp"][:].to_broadcast([P, T, 4]), ALU.is_equal))
                link(V.tensor_scalar(R["gpen"], R["goh"], -NEG, NEG, ALU.mult, ALU.add))
                both(lambda t: V.tensor_tensor(r["sel"][:, t].rearrange("p (g e) -> p g e", g=GROUPS),
                                               r["logit"][:, t, GROUPS:ROUTE].rearrange("p (g e) -> p g e", g=GROUPS),
                                               r["gpen"][:, t].unsqueeze(2).to_broadcast([P, GROUPS, PER_GROUP]), ALU.add))
                for m, eq, pr, oh, sel in (("m1", "eq1", "p1", "oh1", "sel"), ("m2", "eq2", "p2", "oh2", "sel2")):
                    if sel == "sel2":
                        link(V.scalar_tensor_tensor(R["sel2"], R["oh1"], 3 * NEG, R["sel"], ALU.mult, ALU.add))
                    link(V.tensor_reduce(R[m], R[sel], AX.X, ALU.max))
                    both(lambda t: V.scalar_tensor_tensor(r[eq][:, t, :], r[sel][:, t, :], r[m][:, t, :], C("prio"),
                                                          ALU.is_equal, ALU.mult))
                    link(V.tensor_reduce(R[pr], R[eq], AX.X, ALU.max))
                    link(V.tensor_tensor(R[oh], R[eq], r[pr][:].to_broadcast([P, T, EXPERTS]), ALU.is_equal))
                V.tensor_tensor(R["assign"], R["oh1"], R["oh2"], ALU.add).then_inc(assigned.sem, 1)
                V.tensor_tensor(R["d"], R["m2"], R["m1"], ALU.subtract).then_inc(route_args.sem, 1)
                dve.wait_ge(assigned.sem, assigned.at(l, 1))
                dve.wait_ge(ranked.sem, ranked.at(l, 1))
                link(V.scalar_tensor_tensor(R["rank"], psum[:, 1, 0:32].rearrange("p (t e) -> p t e", t=T), 1.0, R["assign"],
                                            ALU.add, ALU.mult))

                def combine_weights():
                    dve.wait_ge(route_exps.sem, route_exps.at(l, 1))
                    V.tensor_scalar(R["e1"], R["e"], 1.0, None, ALU.add)
                    link(V.tensor_reduce(R["gsum"], R["gexp"], AX.X, ALU.add))
                    V.reciprocal(R["gw"], R["gsum"])
                    link(V.reciprocal(R["w1"], R["e1"]))
                    link(V.tensor_tensor(R["w1"], R["w1"], R["gw"], ALU.mult))
                    V.tensor_tensor(R["cw"], R["oh1"], r["w1"][:].to_broadcast([P, T, EXPERTS]), ALU.mult)
                    link(V.tensor_tensor(R["w2"], R["w1"], R["e"], ALU.mult))
                    link(V.tensor_tensor(R["t1"], R["oh2"], r["w2"][:].to_broadcast([P, T, EXPERTS]), ALU.mult))
                    link(V.tensor_tensor(R["cw"], R["cw"], R["t1"], ALU.add))

                def count_items():
                    dve.wait_ge(ranked.sem, ranked.at(l, 2))
                    link(V.tensor_reduce(fullest[:], psum[:, 2, 0:EXPERTS], AX.X, ALU.max))
                    V.tensor_copy(items[:, 0:1], last_f[:])
                    for k in range(3):
                        ins = V.tensor_scalar(more[:, k:k + 1], fullest[:], SLOTS * (k + 1) + 0.5, float(PAIRS), ALU.is_gt, ALU.mult)
                    link(ins)
                    link(V.tensor_reduce(more_sum[:], more[:], AX.X, ALU.add))
                    link(V.scalar_tensor_tensor(last_f[:], last_f[:], float(PAIRS), more_sum[:], ALU.add, ALU.add))
                    V.tensor_copy(items[:, 1:2], last_f[:]).then_inc(items_ready.sem, 1)

                def after_pick():
                    count_items()
                    combine_weights()

                pick_next(prev + l, 0, 0, after_pick)
                assert step[0] == VSTEPS, ("VSTEPS", step[0])

                copy_tokens(prev + l, 0)
                dve.wait_ge(items_ready.sem, items_ready.at(l, 1))
                settle(dve)
                last = dve.value_load(items[0:1, 1:2], min_val=PAIRS, max_val=4 * PAIRS * DEPTH)

                def item(g, o):
                    istep = [0]

                    def ilink(ins):
                        istep[0] += 1
                        ins.then_inc(v_item.sem, 1)
                        dve.wait_ge(v_item.sem, v_item.at(g, istep[0] + 1))

                    pick_next(g + l + 1, dve.snap(((g + 1) & (PAIRS - 1)) * 2), 1 - o)
                    dve.wait_ge(gate_exp.sem, gate_exp.at(g, 1))
                    ilink(V.tensor_scalar(sig, sig, 1.0, None, ALU.add))
                    ilink(V.reciprocal(sig, sig))
                    ilink(V.tensor_tensor(sig, sig, psum[:, 0, :], ALU.mult))
                    dve.wait_ge(upped.sem, upped.at(g, 2))
                    V.tensor_tensor(he, sig, psum[:, 1, :], ALU.mult).then_inc(he_ready.sem, 1)
                    copy_tokens(g + l + 1, 1 - o)
                    for n in range(2):
                        for t in range(T):
                            k = 2 * n + t
                            dve.wait_ge(scattered.sem, scattered.at(g, k + 1))
                            xs = x[:, t, n * COLS:(n + 1) * COLS]
                            V.tensor_tensor(xs, psum[:, 6 + t, :], xs, ALU.add).then_inc(x_added.sem, 1)
                    dve.wait_ge(x_added.sem, x_added.at(g, 4))
                    assert istep[0] == VITEM, ("VITEM", istep[0])

                with dve.Fori(prev, last, 2) as g0:
                    for o in range(2):
                        item(dve.snap(g0 + o), o)
                square()

            step = [0]

            def link(ins):
                step[0] += 1
                ins.then_inc(v_last.sem, 1)
                dve.wait_ge(v_last.sem, step[0])

            dve.wait_ge(squared.sem, squared.at(DEPTH, 1))
            dve.wait_ge(summed.sem, summed.at(DEPTH, 1))
            link(V.tensor_scalar(meansq[:, 0:T], sumsq[:], 1.0 / D, EPS, ALU.mult, ALU.add))
            inverse_roots(T, link).then_inc(last_rstd.sem, 1)
            dve.wait_ge(last_rstd.sem, 1)
            dve.wait_ge(final_loaded.sem, 16)
            V.scalar_tensor_tensor(h[:, 1, :], x[:, 1, :], rstd[:, 1:2], za.rearrange("p t n -> p (t n)"),
                                   ALU.mult, ALU.mult).then_inc(out_ready[1].sem, 1)


NAMES = ["x", "norm1", "w_in", "a_ln_g", "a_ln_b", "a_ws", "a_bs", "ret_gn", "w_out", "norm2", "router_g", "router_gb",
         "router_e", "router_eb", "w_gate", "w_up", "w_down", "final_norm"]


def kernel(**inputs):
    import concourse.bacc as bacc
    from concourse.bass_utils import run_bass_kernel_spmd as run

    nc = bacc.Bacc("TRN2", target_bir_lowering=False, num_devices=1)
    arrays, args = {}, []
    for name in NAMES:
        a = np.ascontiguousarray(inputs[name])
        arrays[f"in_{name}"] = a
        args.append(nc.dram_tensor(f"in_{name}", a.shape, mybir.dt.from_np(a.dtype), kind="ExternalInput").ap())
    arrays["table"] = constant_table()
    args.append(nc.dram_tensor("table", (P, CONST_COLS), F32, kind="ExternalInput").ap())
    args.append(nc.dram_tensor("out", (1, SEQ, D), F32, kind="ExternalOutput").ap())
    hybrid_trunk(nc, *args)
    return run(nc, [arrays], core_ids=[0]).results[0]["out"]
```
